# Optimizing a Trainium2 kernel written in Bass

```python
import jax, jax.numpy as jnp
from jax import lax
import numpy as np

D_MODEL = 1024
BATCH = 1
SEQ = 1024
DEPTH = 1

MLA_HEADS = 8
QK_NOPE_DIM = 64
QK_ROPE_DIM = 32
QK_HEAD_DIM = QK_NOPE_DIM + QK_ROPE_DIM
V_HEAD_DIM = 64
Q_LORA_RANK = 384
KV_LORA_RANK = 256
ROPE_THETA = 10000.0
Q_BLOCK = 128
RWKV_HEADS = 8
RWKV_HEAD_DIM = 64
RWKV_DIM = RWKV_HEADS * RWKV_HEAD_DIM
DECAY_LORA = 64
AAA_LORA = 64
GATE_LORA = 128
GN_EPS = RWKV_HEAD_DIM * 1e-5
MLA_COLS = Q_LORA_RANK + KV_LORA_RANK + QK_ROPE_DIM
RWKV_COLS = 3 * RWKV_DIM + DECAY_LORA + AAA_LORA + GATE_LORA
GATE_COLS = 2 * D_MODEL
IN_COLS = MLA_COLS + RWKV_COLS + GATE_COLS
D_FF = 4 * D_MODEL
PLE_DIM = 256
RMS_EPS = 1e-6


def rmsnorm(x, g):
    xf = x.astype(jnp.float32)
    y = xf * lax.rsqrt(jnp.mean(xf * xf, axis=-1, keepdims=True) + RMS_EPS)
    return (y * g.astype(jnp.float32)).astype(x.dtype)

def rope_tables(positions):
    half = QK_ROPE_DIM // 2
    inv_freq = ROPE_THETA ** (-jnp.arange(half, dtype=jnp.float32) / half)
    ang = positions.astype(jnp.float32)[..., None] * inv_freq
    return jnp.cos(ang), jnp.sin(ang)

def apply_rope(x, cos, sin):
    xf = x.astype(jnp.float32)
    x1, x2 = jnp.split(xf, 2, axis=-1)
    out = jnp.concatenate([x1 * cos - x2 * sin, x2 * cos + x1 * sin], axis=-1)
    return out.astype(x.dtype)

def causal_block_attention(q, k, v, scale):
    S = q.shape[1]
    outs = []
    for blk in range(S // Q_BLOCK):
        q0 = blk * Q_BLOCK
        kend = q0 + Q_BLOCK
        qb = q[:, q0:kend]
        s = jnp.einsum('bqhd,bkhd->bhqk', qb, k[:, :kend]).astype(jnp.float32) * scale
        mask = jnp.arange(kend)[None, :] <= (q0 + jnp.arange(Q_BLOCK))[:, None]
        s = jnp.where(mask, s, jnp.float32(-1e30))
        prob = jax.nn.softmax(s, axis=-1).astype(v.dtype)
        outs.append(jnp.einsum('bhqk,bkhd->bqhd', prob, v[:, :kend]))
    return jnp.concatenate(outs, axis=1)

def mla_branch(z, cos, sin, g_q_a, w_uq, g_kv_a, w_ukv, w_o_mla):
    B, S, _ = z.shape
    c_q, c_kv, k_pe = jnp.split(z, [Q_LORA_RANK, Q_LORA_RANK + KV_LORA_RANK], axis=-1)
    q = (rmsnorm(c_q, g_q_a) @ w_uq).reshape(B, S, MLA_HEADS, QK_HEAD_DIM)
    q_nope, q_pe = jnp.split(q, [QK_NOPE_DIM], axis=-1)
    q_pe = apply_rope(q_pe, cos[:, :, None, :], sin[:, :, None, :])
    kv = (rmsnorm(c_kv, g_kv_a) @ w_ukv).reshape(B, S, MLA_HEADS, QK_NOPE_DIM + V_HEAD_DIM)
    k_nope, v = jnp.split(kv, [QK_NOPE_DIM], axis=-1)
    k_pe = apply_rope(k_pe, cos, sin)
    qh = jnp.concatenate([q_nope, q_pe], axis=-1)
    kh = jnp.concatenate([k_nope, jnp.broadcast_to(k_pe[:, :, None, :], (B, S, MLA_HEADS, QK_ROPE_DIM))], axis=-1)
    o = causal_block_attention(qh, kh, v, QK_HEAD_DIM ** -0.5)
    return o.reshape(B, S, MLA_HEADS * V_HEAD_DIM) @ w_o_mla

def token_shift(z, mu):
    prev = jnp.pad(z, ((0, 0), (1, 0), (0, 0)))[:, :-1]
    return z + (prev - z) * mu

def wkv7_scan(r, decay, k, v, a_vec, b_vec):
    B, S, H, N = r.shape

    def step(state, inp):
        r_t, d_t, k_t, v_t, a_t, b_t = inp
        sa = jnp.einsum('bhvk,bhk->bhv', state, a_t)
        state = (state * d_t[:, :, None, :] + sa[..., None] * b_t[:, :, None, :]
                 + v_t[..., None] * k_t[:, :, None, :])
        return state, jnp.einsum('bhvk,bhk->bhv', state, r_t)

    xs = tuple(jnp.moveaxis(t, 1, 0) for t in (r, decay, k, v, a_vec, b_vec))
    _, ys = lax.scan(step, jnp.zeros((B, H, N, N), jnp.float32), xs)
    return jnp.moveaxis(ys, 0, 1)

def rwkv7_branch(z, mu_rwkv, w0, w2, a0, a2, g2, k_k, k_a, r_k, ln_x_w, ln_x_b, w_o_rwkv):
    B, S, _ = z.shape
    f32 = jnp.float32
    z = token_shift(z, mu_rwkv)
    r, k, v, w_lo, a_lo, g_lo = jnp.split(
        z, [RWKV_DIM, 2 * RWKV_DIM, 3 * RWKV_DIM, 3 * RWKV_DIM + DECAY_LORA,
            3 * RWKV_DIM + DECAY_LORA + AAA_LORA], axis=-1)
    w_log = -jax.nn.softplus(-(w0.astype(f32) + (jnp.tanh(w_lo) @ w2).astype(f32))) - 0.5
    decay = jnp.exp(-jnp.exp(w_log))
    a = jax.nn.sigmoid(a0.astype(f32) + (a_lo @ a2).astype(f32))
    g = jax.nn.sigmoid(g_lo) @ g2
    hs = (B, S, RWKV_HEADS, RWKV_HEAD_DIM)
    r = r.astype(f32).reshape(hs)
    k = k.astype(f32)
    v = v.astype(f32).reshape(hs)
    kk = (k * k_k.astype(f32)).reshape(hs)
    kk = kk / jnp.maximum(jnp.linalg.norm(kk, axis=-1, keepdims=True), 1e-12)
    k = (k * (1.0 + (a - 1.0) * k_a.astype(f32))).reshape(hs)
    a = a.reshape(hs)
    decay = decay.reshape(hs)
    y = wkv7_scan(r, decay, k, v, -kk, kk * a)
    mean = jnp.mean(y, axis=-1, keepdims=True)
    var = jnp.mean(jnp.square(y - mean), axis=-1, keepdims=True)
    y = ((y - mean) * lax.rsqrt(var + GN_EPS)).reshape(B, S, RWKV_DIM)
    y = y * ln_x_w.astype(f32) + ln_x_b.astype(f32)
    bonus = jnp.sum(r * k * r_k.astype(f32), axis=-1, keepdims=True) * v
    y = (y + bonus.reshape(B, S, RWKV_DIM)).astype(z.dtype) * g
    return y @ w_o_rwkv

def first_inputs(seed: int = 0) -> dict:
    key = jax.random.key(seed)
    ks = jax.random.split(key, 40)
    f32 = jnp.float32
    L = DEPTH

    def nrm(k, shape, fan_in):
        return jax.random.normal(k, shape, f32) * (fan_in ** -0.5)

    def gain(k, shape):
        return 1.0 + 0.02 * jax.random.normal(k, shape, f32)

    H, N = RWKV_HEADS, RWKV_HEAD_DIM
    return {
        "x": jax.random.normal(ks[0], (BATCH, SEQ, D_MODEL), f32),
        "p": jax.random.normal(ks[1], (DEPTH, BATCH, SEQ, PLE_DIM), f32),
        "positions": (jax.random.randint(ks[2], (BATCH, 1), 0, 1024, jnp.int32)
                      + jnp.arange(SEQ, dtype=jnp.int32)[None, :]),
        "g_mix": gain(ks[3], (L, D_MODEL)),
        "w_in": nrm(ks[4], (L, D_MODEL, IN_COLS), D_MODEL),
        "g_q_a": gain(ks[5], (L, Q_LORA_RANK)),
        "w_uq": nrm(ks[6], (L, Q_LORA_RANK, MLA_HEADS * QK_HEAD_DIM), Q_LORA_RANK),
        "g_kv_a": gain(ks[7], (L, KV_LORA_RANK)),
        "w_ukv": nrm(ks[8], (L, KV_LORA_RANK, MLA_HEADS * (QK_NOPE_DIM + V_HEAD_DIM)), KV_LORA_RANK),
        "w_o_mla": nrm(ks[9], (L, MLA_HEADS * V_HEAD_DIM, D_MODEL), MLA_HEADS * V_HEAD_DIM),
        "mu_rwkv": jax.random.uniform(ks[10], (L, RWKV_COLS), f32),
        "w0": jax.random.uniform(ks[11], (L, RWKV_DIM), f32, -6.5, -1.5),
        "w2": nrm(ks[12], (L, DECAY_LORA, RWKV_DIM), DECAY_LORA),
        "a0": 0.1 * jax.random.normal(ks[13], (L, RWKV_DIM), f32),
        "a2": nrm(ks[14], (L, AAA_LORA, RWKV_DIM), AAA_LORA),
        "g2": nrm(ks[15], (L, GATE_LORA, RWKV_DIM), GATE_LORA),
        "k_k": 0.85 + 0.02 * jax.random.normal(ks[16], (L, RWKV_DIM), f32),
        "k_a": gain(ks[17], (L, RWKV_DIM)),
        "r_k": 0.1 * jax.random.normal(ks[18], (L, H, N), f32),
        "ln_x_w": gain(ks[19], (L, RWKV_DIM)),
        "ln_x_b": 0.02 * jax.random.normal(ks[20], (L, RWKV_DIM), f32),
        "w_o_rwkv": nrm(ks[21], (L, RWKV_DIM, D_MODEL), RWKV_DIM),
        "w_out": nrm(ks[22], (L, D_MODEL, D_MODEL), D_MODEL),
        "g_ffn": gain(ks[23], (L, D_MODEL)),
        "w_ffn_up": nrm(ks[24], (L, D_MODEL, D_FF), D_MODEL),
        "w_ffn_down": nrm(ks[25], (L, D_FF, D_MODEL), D_FF),
        "g_ple": gain(ks[26], (L, D_MODEL)),
        "w_ple_gate": nrm(ks[27], (L, D_MODEL, D_MODEL), D_MODEL),
        "w_ple_proj": nrm(ks[28], (L, PLE_DIM, D_MODEL), PLE_DIM),
        "g_final": gain(ks[29], (D_MODEL,)),
    }

def first_block(x, p, positions, g_mix, w_in, g_q_a, w_uq, g_kv_a, w_ukv, w_o_mla,
              mu_rwkv, w0, w2, a0, a2, g2, k_k, k_a, r_k, ln_x_w, ln_x_b, w_o_rwkv,
              w_out, g_ffn, w_ffn_up, w_ffn_down, g_ple, w_ple_gate, w_ple_proj, g_final):
    cos, sin = rope_tables(positions)
    for i in range(DEPTH):
        h = rmsnorm(x, g_mix[i])
        z = h @ w_in[i]
        z_mla, z_rwkv, z_gate = jnp.split(z, [MLA_COLS, MLA_COLS + RWKV_COLS], axis=-1)
        y_a = mla_branch(z_mla, cos, sin, g_q_a[i], w_uq[i], g_kv_a[i], w_ukv[i], w_o_mla[i])
        y_b = rwkv7_branch(z_rwkv, mu_rwkv[i], w0[i], w2[i], a0[i], a2[i], g2[i], k_k[i], k_a[i],
                           r_k[i], ln_x_w[i], ln_x_b[i], w_o_rwkv[i])
        gate = jax.nn.sigmoid(z_gate)
        gate_a, gate_b = jnp.split(gate, 2, axis=-1)
        x = x + (gate_a * y_a + gate_b * y_b) @ w_out[i]
        h = rmsnorm(x, g_ffn[i])
        x = x + jnp.square(jax.nn.relu(h @ w_ffn_up[i])) @ w_ffn_down[i]
        ple_gate = jax.nn.sigmoid(rmsnorm(x, g_ple[i]) @ w_ple_gate[i])
        x = x + ple_gate * (p[i] @ w_ple_proj[i])
    return rmsnorm(x, g_final)


_first_inputs = first_inputs


def first_inputs(seed=0):
    import zlib

    import numpy as np

    out = dict(_first_inputs(seed))
    spreads = {}
    factors = {'g_mix': 5.058,
     'g_q_a': 49.471,
     'g_kv_a': 56.252,
     'w2': 16.471,
     'a0': 5.452,
     'k_k': 64.0,
     'k_a': 8.0,
     'ln_x_w': 64.0,
     'ln_x_b': 64.0,
     'g_ffn': 27.832,
     'g_ple': 64.0,
     'g_final': 8.488,
     'p': 7.018,
     'w0': 3.919,
     'w_ple_gate': 8.0,
     'w_ple_proj': 7.024}
    for name, (base, spread) in spreads.items():
        noise = np.random.default_rng([zlib.crc32(name.encode()), seed]).standard_normal(out[name].shape)
        drawn = base * np.exp(spread * noise) if base else spread * noise
        out[name] = __import__('jax').numpy.asarray(drawn.astype(out[name].dtype))
    for name, factor in factors.items():
        out[name] = (out[name] * factor).astype(out[name].dtype)
    return out


_narrow_inputs = first_inputs


def first_inputs(seed=0):

    out = dict(_narrow_inputs(seed))
    wider = {'k_k': 12.0, 'ln_x_w': 10.22, 'ln_x_b': 10.24, 'g_ple': 12.0, 'g_final': 3.25}
    for name, times in wider.items():
        mean = out[name].mean()
        out[name] = (mean + times * (out[name] - mean)).astype(out[name].dtype)
    return out


LRU_WIDTH = D_MODEL * 5 // 4
LRU_HEADS = 10
LRU_HEAD_DIM = LRU_WIDTH // LRU_HEADS
LRU_C = 8.0
LRU_CONV = 4
POOL_WIDTH = D_MODEL
POOL_WINDOWS = (2, 4, 8, 16)
POOL_GROUPS = len(POOL_WINDOWS)
POOL_GROUP_DIM = POOL_WIDTH // POOL_GROUPS
N_BRANCHES = 2
IN_WIDTH = LRU_WIDTH + POOL_WIDTH + N_BRANCHES * D_MODEL
D_FF_2 = D_MODEL * 11 // 4
FFN_CONV = 3


def rms_norm(x, g):
    x32 = x.astype(jnp.float32)
    y = x32 * lax.rsqrt(jnp.mean(x32 * x32, axis=-1, keepdims=True) + RMS_EPS)
    return (y * g.astype(jnp.float32)).astype(x.dtype)

def depthwise_conv(x, w, b, left):
    k_width = w.shape[0]
    s = x.shape[1]
    xp = jnp.pad(x, ((0, 0), (left, k_width - 1 - left), (0, 0)))
    y = b
    for k in range(k_width):
        y = y + w[k] * xp[:, k:k + s]
    return y

def block_diag(x, w, b):
    bsz, s, _ = x.shape
    h, i, j = w.shape
    y = jnp.einsum('bshi,hij->bshj', x.reshape(bsz, s, h, i), w)
    return y.reshape(bsz, s, h * j) + b

def _lin_combine(left, right):
    a_l, b_l = left
    a_r, b_r = right
    return a_l * a_r, a_r * b_l + b_r

def rglru_direction(xc, wa, ba, wx, bx, lam, reverse):
    x32 = xc.astype(jnp.float32)
    r = jax.nn.sigmoid(block_diag(xc, wa, ba).astype(jnp.float32))
    i = jax.nn.sigmoid(block_diag(xc, wx, bx).astype(jnp.float32))
    log_a = -LRU_C * r * jax.nn.softplus(-lam.astype(jnp.float32))
    a = jnp.exp(log_a)
    b_in = jnp.sqrt(-jnp.expm1(2.0 * log_a)) * (i * x32)
    _, h = lax.associative_scan(_lin_combine, (a, b_in), axis=1, reverse=reverse)
    return h

def multiscale_pool(u):
    bsz, s, width = u.shape
    u32 = u.astype(jnp.float32)
    csum = jnp.concatenate([jnp.zeros((bsz, 1, width), jnp.float32),
                            jnp.cumsum(u32, axis=1)], axis=1)
    t = jnp.arange(s)
    outs = []
    for g, w in enumerate(POOL_WINDOWS):
        sl = slice(g * POOL_GROUP_DIM, (g + 1) * POOL_GROUP_DIM)
        cg = csum[..., sl]
        lo = jnp.clip(t - w // 2, 0, s - 1)
        hi = jnp.clip(t + w // 2 - 1, 0, s - 1)
        win_sum = jnp.take(cg, hi + 1, axis=1) - jnp.take(cg, lo, axis=1)
        count = (hi - lo + 1).astype(jnp.float32)[None, :, None]
        outs.append(win_sum / count - u32[..., sl])
    return jnp.concatenate(outs, axis=-1).astype(u.dtype)

def second_inputs(seed: int = 0) -> dict:
    key = jax.random.key(seed)
    ks = jax.random.split(key, 32)
    f32 = jnp.float32
    L = DEPTH

    def nrm(k, shape, scale):
        return jax.random.normal(k, shape, f32) * scale

    def gain(k, shape):
        return 1.0 + 0.05 * jax.random.normal(k, shape, f32)

    def lru_lambda(k):
        u = jax.random.uniform(k, (L, LRU_WIDTH), f32, 0.9, 0.999)
        s = u ** (1.0 / LRU_C)
        return jnp.log(s) - jnp.log1p(-s)

    return {
        "x": jax.random.normal(ks[0], (BATCH, SEQ, D_MODEL), f32),
        "g_mix": gain(ks[1], (L, D_MODEL)),
        "w_in": nrm(ks[2], (L, D_MODEL, IN_WIDTH), D_MODEL ** -0.5),
        "b_gate": nrm(ks[3], (L, N_BRANCHES * D_MODEL), 0.01),
        "conv_a_w": nrm(ks[4], (L, LRU_CONV, LRU_WIDTH), LRU_CONV ** -0.5),
        "conv_a_b": nrm(ks[5], (L, LRU_WIDTH), 0.01),
        "wa_f": nrm(ks[6], (L, LRU_HEADS, LRU_HEAD_DIM, LRU_HEAD_DIM), LRU_HEAD_DIM ** -0.5),
        "ba_f": nrm(ks[7], (L, LRU_WIDTH), 0.01),
        "wx_f": nrm(ks[8], (L, LRU_HEADS, LRU_HEAD_DIM, LRU_HEAD_DIM), LRU_HEAD_DIM ** -0.5),
        "bx_f": nrm(ks[9], (L, LRU_WIDTH), 0.01),
        "lam_f": lru_lambda(ks[10]),
        "wa_b": nrm(ks[11], (L, LRU_HEADS, LRU_HEAD_DIM, LRU_HEAD_DIM), LRU_HEAD_DIM ** -0.5),
        "ba_b": nrm(ks[12], (L, LRU_WIDTH), 0.01),
        "wx_b": nrm(ks[13], (L, LRU_HEADS, LRU_HEAD_DIM, LRU_HEAD_DIM), LRU_HEAD_DIM ** -0.5),
        "bx_b": nrm(ks[14], (L, LRU_WIDTH), 0.01),
        "lam_b": lru_lambda(ks[15]),
        "w_pool": nrm(ks[16], (L, POOL_GROUPS, POOL_GROUP_DIM, POOL_GROUP_DIM), POOL_GROUP_DIM ** -0.5),
        "b_pool": nrm(ks[17], (L, POOL_WIDTH), 0.01),
        "pool_scale": gain(ks[18], (L, POOL_WIDTH)),
        "p_a": nrm(ks[19], (L, LRU_WIDTH, D_MODEL), LRU_WIDTH ** -0.5),
        "p_b": nrm(ks[20], (L, POOL_WIDTH, D_MODEL), POOL_WIDTH ** -0.5),
        "w_out": nrm(ks[21], (L, D_MODEL, D_MODEL), D_MODEL ** -0.5),
        "g_ffn": gain(ks[22], (L, D_MODEL)),
        "w_up": nrm(ks[23], (L, D_MODEL, 2 * D_FF_2), D_MODEL ** -0.5),
        "conv_f_w": nrm(ks[24], (L, FFN_CONV, 2 * D_FF_2), FFN_CONV ** -0.5),
        "conv_f_b": nrm(ks[25], (L, 2 * D_FF_2), 0.01),
        "w_down": nrm(ks[26], (L, D_FF_2, D_MODEL), D_FF_2 ** -0.5),
        "g_final": gain(ks[27], (D_MODEL,)),
    }

def second_block(x, g_mix, w_in, b_gate, conv_a_w, conv_a_b, wa_f, ba_f, wx_f, bx_f, lam_f,
              wa_b, ba_b, wx_b, bx_b, lam_b, w_pool, b_pool, pool_scale, p_a, p_b, w_out,
              g_ffn, w_up, conv_f_w, conv_f_b, w_down, g_final):
    for l in range(DEPTH):
        h = rms_norm(x, g_mix[l])
        proj = h @ w_in[l]
        u_a = proj[..., :LRU_WIDTH]
        u_b = proj[..., LRU_WIDTH:LRU_WIDTH + POOL_WIDTH]
        gate_logits = proj[..., LRU_WIDTH + POOL_WIDTH:] + b_gate[l]

        xa = depthwise_conv(u_a, conv_a_w[l], conv_a_b[l], LRU_CONV // 2)
        h_fwd = rglru_direction(xa, wa_f[l], ba_f[l], wx_f[l], bx_f[l], lam_f[l], False)
        h_bwd = rglru_direction(xa, wa_b[l], ba_b[l], wx_b[l], bx_b[l], lam_b[l], True)
        y_a = (h_fwd + h_bwd).astype(x.dtype) @ p_a[l]

        pooled = multiscale_pool(u_b)
        y_b = (block_diag(pooled, w_pool[l], b_pool[l]) * pool_scale[l]) @ p_b[l]

        gates = jax.nn.sigmoid(gate_logits.astype(jnp.float32)).astype(x.dtype)
        merged = gates[..., :D_MODEL] * y_a + gates[..., D_MODEL:] * y_b
        x = x + merged @ w_out[l]

        h = rms_norm(x, g_ffn[l])
        up = depthwise_conv(h @ w_up[l], conv_f_w[l], conv_f_b[l], FFN_CONV // 2)
        act = jax.nn.gelu(up[..., :D_FF_2], approximate=True) * up[..., D_FF_2:]
        x = x + act @ w_down[l]
    return rms_norm(x, g_final)


def setup_inputs(seed=0):
    out = dict(first_inputs(seed))
    for name, value in second_inputs(seed + 1).items():
        if name != "x":
            out[name + "_2"] = value
    return out


def reference(
    x, p, positions, g_mix, w_in, g_q_a, w_uq, g_kv_a, w_ukv, w_o_mla, mu_rwkv, w0, w2, a0, a2,
    g2, k_k, k_a, r_k, ln_x_w, ln_x_b, w_o_rwkv, w_out, g_ffn, w_ffn_up, w_ffn_down, g_ple,
    w_ple_gate, w_ple_proj, g_final, g_mix_2, w_in_2, b_gate_2, conv_a_w_2, conv_a_b_2, wa_f_2,
    ba_f_2, wx_f_2, bx_f_2, lam_f_2, wa_b_2, ba_b_2, wx_b_2, bx_b_2, lam_b_2, w_pool_2,
    b_pool_2, pool_scale_2, p_a_2, p_b_2, w_out_2, g_ffn_2, w_up_2, conv_f_w_2, conv_f_b_2,
    w_down_2, g_final_2,
):
    x = first_block(
        x, p, positions, g_mix, w_in, g_q_a, w_uq, g_kv_a, w_ukv, w_o_mla, mu_rwkv, w0, w2, a0,
        a2, g2, k_k, k_a, r_k, ln_x_w, ln_x_b, w_o_rwkv, w_out, g_ffn, w_ffn_up, w_ffn_down,
        g_ple, w_ple_gate, w_ple_proj, g_final,
    )
    return second_block(
        x, g_mix_2, w_in_2, b_gate_2, conv_a_w_2, conv_a_b_2, wa_f_2, ba_f_2, wx_f_2, bx_f_2,
        lam_f_2, wa_b_2, ba_b_2, wx_b_2, bx_b_2, lam_b_2, w_pool_2, b_pool_2, pool_scale_2,
        p_a_2, p_b_2, w_out_2, g_ffn_2, w_up_2, conv_f_w_2, conv_f_b_2, w_down_2, g_final_2,
    )


_drawn_inputs = setup_inputs


def setup_inputs(seed=0):
    import zlib

    import numpy as np

    out = dict(_drawn_inputs(seed))
    spreads = {}
    factors = {'g_ple': 14.266,
     'g_mix_2': 3.899,
     'b_gate_2': 22.807,
     'conv_a_b_2': 8.0,
     'wa_f_2': 4.227,
     'ba_f_2': 64.0,
     'bx_f_2': 64.0,
     'wa_b_2': 4.345,
     'ba_b_2': 64.0,
     'bx_b_2': 64.0,
     'b_pool_2': 8.0,
     'pool_scale_2': 8.0,
     'g_ffn_2': 8.0,
     'conv_f_b_2': 34.768}
    for name, (base, spread) in spreads.items():
        noise = np.random.default_rng([zlib.crc32(name.encode()), seed]).standard_normal(out[name].shape)
        drawn = base * np.exp(spread * noise) if base else spread * noise
        out[name] = __import__('jax').numpy.asarray(drawn.astype(out[name].dtype))
    for name, factor in factors.items():
        out[name] = (out[name] * factor).astype(out[name].dtype)
    return out
```

```python
import math
from collections import namedtuple
from contextlib import ExitStack

import numpy as np
import concourse.bass as bass
from concourse import mybir

F32 = mybir.dt.float32
F32R = mybir.dt.float32r
I32 = mybir.dt.int32
ALU = mybir.AluOpType
ACT = mybir.ActivationFunctionType
AX = mybir.AxisListType

P = 128
S = 1024
D = 1024
NT = S // P
ND = D // P
HALF = 512
NHALF = S // HALF
HEADS, NOPE, ROPE, VDIM = 8, 64, 32, 64
QK = NOPE + ROPE
QRANK, KVRANK = 384, 256
NQ, NKV = QRANK // P, KVRANK // P
MLA_COLS = QRANK + KVRANK + ROPE
RDIM = 512
NR = RDIM // P
LORA, GLORA = 64, 128
RWKV_COLS = 3 * RDIM + 2 * LORA + GLORA
NZ = RWKV_COLS // P
DFF = 4 * D
PLE = 256
EPS = 1e-6
GN_EPS = 64 * 1e-5
THETA = 10000.0
CH = 128
NCH = S // CH
MID = CH // 2 - 1
LEVELS = 7
LW = 1280
NL = LW // P
PW = 1024
WINDOWS = (2, 4, 8, 16)
GDIM = PW // len(WINDOWS)
DFF2 = 2816
NF2 = DFF2 // P

TILE = 1024

Token = namedtuple("Token", "sem value")

CONST = {}
_at = 0
for _name, _n in (("ident", P), ("mask4", 4 * P), ("levels", LEVELS * P), ("causal", P), ("headsum", P),
                  ("headsel", 2), ("freq", ROPE // 2)):
    CONST[_name] = (_at, _at + _n)
    _at += _n
CONST_COLS = _at

ROW_TILES = [
    [("mu_rwkv", NZ), ("w0", NR), ("a0", NR), ("k_k", NR), ("k_a", NR), ("r_k", NR)],
    [("b_gate_2", 16), ("conv_a_w_2", 4 * NL), ("conv_a_b_2", NL), ("ba_f_2", NL), ("bx_f_2", NL),
     ("lam_f_2", NL), ("ba_b_2", NL), ("bx_b_2", NL), ("lam_b_2", NL)],
    [("b_pool_2", 8), ("pool_scale_2", 8), ("conv_f_b_2", 2 * NF2)],
    [("conv_f_w01", 4 * NF2)],
    [("conv_f_w2", 2 * NF2)],
]


def constants():
    c = np.zeros((P, CONST_COLS), np.float32)
    j, i = np.arange(P)[:, None], np.arange(P)[None, :]

    def put(name, a):
        c[:, CONST[name][0]:CONST[name][1]] = a
    put("ident", (j == i))
    strict, incl = (i > j), (i >= j)
    put("mask4", np.concatenate([strict, incl, strict, incl], 1))
    lv = []
    for l in range(LEVELS):
        b = 1 << l
        lv.append(((j // b) % 2 == 0) & (i // b == j // b + 1))
    put("levels", np.concatenate(lv, 1))
    put("causal", np.where(i <= j, 0.0, -1e30))
    put("headsum", (i // 64 == j // 64))
    put("headsel", (np.arange(2)[None, :] == j // 64))
    half = ROPE // 2
    put("freq", np.broadcast_to(
        np.float32(THETA) ** (-np.arange(half, dtype=np.float32) / np.float32(half)), (P, half)))
    return c


def pool_counts():
    t = np.arange(S)
    rows = []
    for w in WINDOWS:
        lo, hi = np.clip(t - w // 2, 0, S - 1), np.clip(t + w // 2 - 1, 0, S - 1)
        rows.append(np.float32(1.0) / (hi - lo + 1).astype(np.float32))
    return np.stack(rows).astype(np.float32)


class Engine:

    def __init__(self, queue, sem):
        self.queue, self.sem, self.count, self.seen = queue, sem, 0, {}

    def wait(self, *tokens):
        for t in tokens:
            if t is None:
                continue
            if isinstance(t, list):
                self.wait(*t)
                continue
            if self.seen.get(id(t.sem), 0) < t.value:
                self.queue.wait_ge(t.sem, t.value)
                self.seen[id(t.sem)] = t.value

    def mark(self, instruction):
        instruction.then_inc(self.sem, 1)
        self.count += 1
        return Token(self.sem, self.count)

    def last(self):
        return Token(self.sem, self.count) if self.count else None


class Slot:

    def __init__(self, ap, sem=None, lo=None):
        self.ap, self.lo, self.busy, self.sem, self.loads = ap, lo, [], sem, 0


class Ring:
    def __init__(self, slots):
        self.slots, self.at = slots, 0

    def next(self):
        s = self.slots[self.at % len(self.slots)]
        self.at += 1
        return s


class Kernel:
    def __init__(self, nc, io):
        self.nc, self.io = nc, io
        self.stack = ExitStack()
        self.names = 0
        self.PE = Engine(nc.tensor, self.semaphore("pe_done"))
        self.A = Engine(nc.scalar, self.semaphore("act_done"))
        self.V = Engine(nc.vector, self.semaphore("dve_done"))
        self.G = Engine(nc.gpsimd, self.semaphore("pool_done"))
        self.SP = Engine(nc.sync, self.semaphore("sp_done"))
        self.stored = {}

    def semaphore(self, name):
        return self.stack.enter_context(self.nc.semaphore(name))

    def sb(self, ctx, name, shape, dtype=F32, side=None):
        self.names += 1
        kw = {"side": side} if side else {}
        return ctx.enter_context(self.nc.sbuf_tensor(f"{name}_{self.names}", shape, dtype, **kw))

    def pair(self, ctx, name, shape, side=None):
        return (self.sb(ctx, name + "_hi", shape, F32R, side), self.sb(ctx, name + "_lo", shape, F32R, side))

    def load(self, slot, dst, src, queue=None, after=()):
        q = queue or self.SP
        q.wait(*slot.busy, *after)
        q.queue.dma_start(dst, src).then_inc(slot.sem, 16)
        slot.loads += 16
        return Token(slot.sem, slot.loads)

    def store(self, name, sem_slot, dst, src, queue, after=()):
        queue.wait(*after)
        queue.queue.dma_start(dst, src).then_inc(sem_slot.sem, 16)
        sem_slot.loads += 16
        t = Token(sem_slot.sem, sem_slot.loads)
        self.stored.setdefault(name, []).append(t)
        return t

    def handover(self):
        done = [e.last() for e in (self.PE, self.A, self.V, self.G)]
        for e in (self.PE, self.A, self.V, self.G, self.SP):
            e.wait(*[t for t in done if t])

    def queue_weights(self, tiles):
        self.pending.extend(tiles)
        self.pump()

    def open_ring(self, ctx, n):
        self.ring_slots = [Slot(*(lambda h, l: (h[:, :], None, l[:, :]))(*self.pair(ctx, f"w{i}", [P, TILE])))
                           for i in range(n)]
        self.ring_free = list(self.ring_slots)
        t = [e.last() for e in (self.PE, self.A, self.V, self.G) if e.last()]
        for s in self.ring_slots:
            s.busy = t
        self.pump()

    def close_ring(self):
        assert not self.ready, "tiles left"
        self.ring_slots, self.ring_free = [], []

    def fetch(self, src, shape):
        s = self.staging.next()
        n = int(np.prod(shape[1:]))
        view = s.ap[:, 0:n]
        if len(shape) == 3:
            view = view.rearrange("p (k c) -> p k c", k=shape[1])
        t = self.load(s, view, src)
        s.busy = []
        return s, n, t

    def split(self, src, hi, lo, after, before):
        self.A.wait(*after, *before)
        th = self.A.mark(self.nc.scalar.activation(hi, src, ACT.Copy))
        self.G.wait(*after, *before, th)
        tl = self.G.mark(self.nc.gpsimd.tensor_tensor(lo, src, hi.bitcast(F32), ALU.subtract))
        return [th, tl]

    def pump(self):
        while self.pending or self.fetched:
            while self.pending and len(self.fetched) < len(self.staging.slots):
                src, shape = self.pending.pop(0)
                self.fetched.append((*self.fetch(src, shape), shape))
            if not self.ring_free:
                return
            stage, n, arrived, shape = self.fetched.pop(0)
            slot = self.ring_free.pop(0)
            done = self.split(stage.ap[:, 0:n], slot.ap[:, 0:n], slot.lo[:, 0:n], [arrived], slot.busy)
            stage.busy = done
            self.ready.append((slot, shape, done))

    def take(self):
        self.pump()
        slot, shape, done = self.ready.pop(0)
        n = int(np.prod(shape[1:]))
        hi, lo = (x[:, 0:n].rearrange("p (k c) -> p k c", k=shape[1]) for x in (slot.ap, slot.lo))
        return slot, hi, lo, done

    def release(self, slots, token):
        for s in slots:
            s.busy = [token]
            self.ring_free.append(s)
        self.pump()

    def bank(self):
        return self.banks.next()

    def product(self, out, terms, bank=None):
        if bank is not None:
            self.PE.wait(*bank.busy)
        for n, (lhsT, rhs, after) in enumerate(terms):
            self.PE.wait(*after)
            mm = self.nc.tensor.matmul(out, lhsT, rhs, start=(n == 0), stop=(n == len(terms) - 1))
        return self.PE.mark(mm)

    @staticmethod
    def three(stat, mov, after):
        return [(stat[0], mov[0], after), (stat[0], mov[1], []), (stat[1], mov[0], [])]

    def rsqrt(self, out, total, scale, eps, tmp, after):
        nc, A, V = self.nc, self.A, self.V
        m, s, q = tmp
        V.wait(*after)
        t = V.mark(nc.vector.tensor_scalar(m, total, scale, eps, ALU.mult, ALU.add))
        A.wait(t)
        t = A.mark(nc.scalar.activation(s, m, ACT.Sqrt))
        V.wait(t)
        V.wait(V.mark(nc.vector.reciprocal(out, s)))
        V.wait(V.mark(nc.vector.tensor_tensor(q, out, out, ALU.mult)))
        V.wait(V.mark(nc.vector.tensor_tensor(q, q, m, ALU.mult)))
        V.wait(V.mark(nc.vector.tensor_scalar(q, q, -0.5, 1.5, ALU.mult, ALU.add)))
        t = V.mark(nc.vector.tensor_tensor(out, out, q, ALU.mult))
        return t

    def setup(self):
        nc, io = self.nc, self.io
        st = self.stack
        self.psum = st.enter_context(nc.psum_tensor("psum", [P, 8, HALF], F32))
        self.banks = Ring([Slot(self.psum[:, b, :]) for b in range(8)])
        self.const_load = Slot(None, self.semaphore("const_load"))
        self.ident = self.sb(st, "ident", [P, P])
        nparam = sum(n for tile in ROW_TILES for _, n in tile)
        self.param = self.sb(st, "param", [P, nparam])
        self.col = {}
        self.staging = Ring([Slot(self.sb(st, f"stage{i}", [P, TILE])[:, :], self.semaphore(f"stage{i}_load"))
                             for i in range(3)])
        self.pending, self.fetched, self.ready, self.ring_free, self.ring_slots = [], [], [], [], []
        self.load(self.const_load, self.ident[:, :], io["const"][:, CONST["ident"][0]:CONST["ident"][1]])
        with ExitStack() as ctx:
            at = 0
            row_load = Slot(None, self.semaphore("row_load"))
            rows = [self.sb(ctx, f"rows{n}", [P, P]) for n in range(len(ROW_TILES))]
            for n, tile in enumerate(ROW_TILES):
                r = 0
                for name, k in tile:
                    if name == "conv_f_w01":
                        src = io["conv_f_w_2"][0, 0:2, :].rearrange("a (b p) -> (a b) p", p=P)
                    elif name == "conv_f_w2":
                        src = io["conv_f_w_2"][0, 2:3, :].rearrange("a (b p) -> (a b) p", p=P)
                    elif name == "conv_a_w_2":
                        src = io[name][0, :, :].rearrange("a (b p) -> (a b) p", p=P)
                    elif name == "r_k":
                        src = io[name].rearrange("l h n -> (l h n)").rearrange("(b p) -> b p", p=P)
                    else:
                        src = io[name].rearrange("l n -> (l n)").rearrange("(b p) -> b p", p=P)
                    self.load(row_load, rows[n][r:r + k, :], src)
                    self.col[name] = at + r
                    r += k
                at += r
            self.col["conv_f_w_2"] = self.col["conv_f_w01"]
            at = 0
            for n, tile in enumerate(ROW_TILES):
                k = sum(c for _, c in tile)
                b = self.bank()
                self.PE.wait(Token(self.const_load.sem, self.const_load.loads),
                             Token(row_load.sem, row_load.loads), *b.busy)
                t = self.PE.mark(nc.tensor.transpose(b.ap[:, 0:k], rows[n][0:k, :], self.ident[0:k, 0:k]))
                self.V.wait(t)
                b.busy = [self.V.mark(nc.vector.tensor_copy(self.param[:, at:at + k], b.ap[:, 0:k]))]
                at += k
            self.param_ready = b.busy[0]
            for e in (self.A, self.V, self.G, self.PE):
                e.wait(self.param_ready)
            self.handover()

    def p_(self, name, i):
        c = self.col[name] + i
        return self.param[:, c:c + 1]

    def norm(self, hT, gain, source):
        nc, A, V, G, PE = self.nc, self.A, self.V, self.G, self.PE
        with ExitStack() as ctx:
            gb = self.sb(ctx, "gain", [P, D])
            xn = Ring([Slot(self.sb(ctx, f"xn{i}", [P, D])[:, :]) for i in range(2)])
            ss = self.sb(ctx, "ss", [P, NT])
            r = self.sb(ctx, "rstd", [P, NT])
            tmp = self.sb(ctx, "rtmp", [P, 3, NT])
            gl = self.load(self.const_load, gb[:, :], gain.partition_broadcast(P))
            ready = []
            for t in range(NT):
                x, after, release = source(t)
                n = xn.next()
                A.wait(*after, *n.busy)
                ts = A.mark(nc.scalar.activation(n.ap, x, ACT.Square, accum_out=ss[:, t:t + 1]))
                tr = self.rsqrt(r[:, t:t + 1], ss[:, t:t + 1], 1.0 / D, EPS,
                                [tmp[:, k, t:t + 1] for k in range(3)], [ts])
                V.wait(tr, gl, ts)
                tx = V.mark(nc.vector.scalar_tensor_tensor(n.ap, x, r[:, t:t + 1], gb[:, :], ALU.mult, ALU.mult))
                release(tx)
                done = []
                for k0 in range(0, ND, 4):
                    b = self.bank()
                    PE.wait(tx, *b.busy)
                    for k in range(k0, k0 + 4):
                        mm = nc.tensor.transpose(b.ap[:, (k - k0) * P:(k - k0 + 1) * P],
                                                 n.ap[:, k * P:(k + 1) * P], self.ident[:, :])
                    tt = PE.mark(mm)
                    src = b.ap.rearrange("p (k c) -> p k c", k=4)
                    hi = hT[0][:, k0:k0 + 4, t * P:(t + 1) * P]
                    lo = hT[1][:, k0:k0 + 4, t * P:(t + 1) * P]
                    A.wait(tt)
                    th = A.mark(nc.scalar.activation(hi, src, ACT.Copy))
                    V.wait(th)
                    tl = V.mark(nc.vector.tensor_tensor(lo, src, hi.bitcast(F32), ALU.subtract))
                    b.busy = [tl]
                    done += [th, tl]
                n.busy = [tt]
                ready.append(done)
            self.V.wait(*ready[-1])
        self.handover()
        return ready

    def dram_source(self, ctx, dram, name=None):
        slots = Ring([Slot(self.sb(ctx, f"xin{i}", [P, D])[:, :], self.semaphore(f"xin{self.names}")) for i in range(3)])
        rows = dram.rearrange("(t p) d -> t p d", p=P)

        def source(t):
            s = slots.next()
            tok = self.load(s, s.ap, rows[t], after=self.stored.get(name, []))

            def release(token):
                s.busy = [token]
            return s.ap, [tok], release
        return source

    def channel_major(self, hT, ready, evacuate, tile=None):
        slot, hi, lo, done = self.take()
        for h in range(NHALF):
            b = self.bank()
            terms = []
            for k in range(hi.shape[1]):
                cols = slice(h * HALF, (h + 1) * HALF)
                after = [*done, *ready] if k == 0 else []
                terms += self.three((hi[:, k, :], lo[:, k, :]), (hT[0][:, k, cols], hT[1][:, k, cols]), after)
            t = self.product(b.ap, terms, b)
            b.busy = evacuate(h, b.ap, t)
        self.release([slot], t)

    def token_major(self, xT, ready, k0, nk, cols, tiles, tokens, evacuate):
        taken = [self.take() for _ in range(tiles)]
        ks = [(hi[:, i, :], lo[:, i, :], done) for _, hi, lo, done in taken for i in range(hi.shape[1])]
        assert len(ks) == nk
        for t in tokens:
            b = self.bank()
            terms = []
            for k in range(nk):
                tc = slice(t * P, (t + 1) * P)
                terms += self.three((xT[0][:, k0 + k, tc], xT[1][:, k0 + k, tc]), ks[k][:2], [*ks[k][2], *ready])
            mm = self.product(b.ap[:, 0:cols], terms, b)
            b.busy = evacuate(t, b.ap[:, 0:cols], mm)
        self.release([x[0] for x in taken], mm)


def weight_block(w, c, width=P, k0=0, k1=None):
    v = w.rearrange("(k p) n -> p k n", p=P)
    k1 = v.shape[1] if k1 is None else k1
    return v[:, k0:k1, c:c + width], (P, k1 - k0, width)


def gate_stage(K, ctx, hT, ready, w, col0, bias, gates, name):
    nc, A = K.nc, K.A
    out = Ring([Slot(K.sb(ctx, f"gate{i}", [P, HALF])[:, :], K.semaphore(f"{name}_store{i}")) for i in range(4)])
    K.queue_weights([weight_block(w, col0 + c * P) for c in range(2 * ND)])
    for c in range(2 * ND):
        def evacuate(h, bank, mm, c=c):
            s = out.next()
            A.wait(mm, *s.busy)
            kw = {"bias": bias(c)} if bias else {}
            t = A.mark(nc.scalar.activation(s.ap, bank, ACT.Sigmoid, **kw))
            s.busy = [K.store(name, s, gates[c, :, h * HALF:(h + 1) * HALF], s.ap, A, [t])]
            return [t]
        K.channel_major(hT, ready, evacuate)
    return [s.busy for s in out.slots]


def rwkv_stage(K, hT, ready, yT_dram):
    nc, io, A, V, G, PE = K.nc, K.io, K.A, K.V, K.G, K.PE
    ctx = ExitStack()
    v_, g_, s_ = nc.vector, nc.gpsimd, nc.scalar
    w = io["w_in"][0]
    col0 = MLA_COLS
    K.open_ring(ctx, 3)
    order = [12, 13] + [x for b in range(NR) for x in (b, NR + b, 2 * NR + b)]
    K.queue_weights([weight_block(w, col0 + c * P) for c in order])
    ld = Slot(None, K.semaphore("rwkv_load"))
    lora_w = K.sb(ctx, "lora_w", [P, RDIM])
    g2 = K.sb(ctx, "g2", [P, RDIM])
    mask4 = K.sb(ctx, "mask4", [P, 4 * P])
    levels = K.sb(ctx, "levels", [P, LEVELS, P])
    headsum = K.sb(ctx, "headsum", [P, P])
    headsel = K.sb(ctx, "headsel", [P, 2])
    lnw = K.sb(ctx, "lnw", [P, P])
    lnb = K.sb(ctx, "lnb", [P, P])
    cst = io["const"]
    c_ = lambda n: cst[:, CONST[n][0]:CONST[n][1]]
    for dst, src in ((lora_w[0:LORA, :], io["w2"][0]), (lora_w[LORA:P, :], io["a2"][0]), (g2[:, :], io["g2"][0]),
                     (mask4[:, :], c_("mask4")), (levels[:, :, :], c_("levels").rearrange("p (l c) -> p l c", l=LEVELS)),
                     (headsum[:, :], c_("headsum")), (headsel[:, :], c_("headsel"))):
        small = K.load(ld, dst, src)
    lora = K.sb(ctx, "lora", [P, S])
    sig_g = K.sb(ctx, "sig_g", [P, S])

    class Shift:
        busy = []

    def shifted(zraw, z, c, out_busy):
        V.wait(*Shift.busy)
        tz = V.mark(v_.memset(zraw[:, 0:1], 0.0))
        copies = []

        def evacuate(h, bank, mm):
            A.wait(mm, *Shift.busy)
            t = A.mark(s_.activation(zraw[:, 1 + h * HALF:1 + (h + 1) * HALF], bank, ACT.Copy))
            copies.append(t)
            return [t]
        K.channel_major(hT, ready, evacuate)
        V.wait(tz, *copies, *out_busy)
        t = V.mark(v_.tensor_tensor(z, zraw[:, 0:S], zraw[:, 1:S + 1], ALU.subtract))
        V.wait(t)
        t = V.mark(v_.scalar_tensor_tensor(z, z, K.p_("mu_rwkv", c), zraw[:, 1:S + 1], ALU.mult, ALU.add))
        Shift.busy = [t]
        return t

    with ExitStack() as c2:
        zraw = K.sb(c2, "zraw", [P, S + 1])
        t = shifted(zraw, lora[:, :], 12, [])
        A.wait(t)
        lora_ready = A.mark(s_.activation(lora[0:LORA, :], lora[0:LORA, :], ACT.Tanh))
        t = shifted(zraw, sig_g[:, :], 13, [])
        A.wait(t)
        sig_ready = A.mark(s_.activation(sig_g[:, :], sig_g[:, :], ACT.Sigmoid))
        K.handover()
    PE.wait(small, lora_ready, sig_ready)

    hd = lambda h: slice(h * 64, (h + 1) * 64)
    AR = K.sb(ctx, "AR", [P, NCH, 2, CH])
    Bt = K.sb(ctx, "Bt", [P, NCH, CH])
    Kt = K.sb(ctx, "Kt", [P, NCH, CH])
    tok = K.sb(ctx, "tok", [P, 4, NCH, P])
    gain = K.sb(ctx, "gain", [P, NCH])
    bonus = K.sb(ctx, "bonus", [P, 2 * NCH])
    state = K.sb(ctx, "state", [P, NCH + 1, 64])
    y_sem = Slot(None, K.semaphore("y_store"))
    ln_load = Slot(None, K.semaphore("ln_load"))

    for blk in range(NR):
        with ExitStack() as c2:
            zraw = K.sb(c2, "zraw", [P, S + 1])
            k = K.sb(c2, "k", [P, S])
            v = K.sb(c2, "v", [P, S])
            a = K.sb(c2, "a", [P, S])
            kk = K.sb(c2, "kk", [P, S])
            Pd = K.sb(c2, "Pd", [P, NCH, CH + 1])
            tmp = K.sb(c2, "tmp", [P, S])
            zero = K.sb(c2, "zero", [P, CH])
            rmid = K.sb(c2, "rmid", [P, NCH])
            pmid = K.sb(c2, "pmid", [P, NCH])
            rT = AR[:, :, 1, :]
            ck = lambda x: x[:, :].rearrange("p (c t) -> p c t", c=NCH)
            ln_done = K.load(ln_load, lnw[:, :], io["ln_x_w"][0, blk * P:(blk + 1) * P].partition_broadcast(P))
            ln_done = K.load(ln_load, lnb[:, :], io["ln_x_b"][0, blk * P:(blk + 1) * P].partition_broadcast(P))
            t0 = V.mark(v_.memset(zero[:, :], 0.0))
            tr = shifted(zraw, tmp[:, :], blk, [])
            A.wait(tr)
            tr = A.mark(s_.activation(rT, ck(tmp), ACT.Copy))
            tk = shifted(zraw, k[:, :], NR + blk, [])
            tv = shifted(zraw, v[:, :], 2 * NR + blk, [])
            sg = []
            for h in range(NHALF):
                cs = slice(h * HALF, (h + 1) * HALF)
                b = K.bank()
                mm = K.product(b.ap, [(lora_w[0:LORA, blk * P:(blk + 1) * P], lora[0:LORA, cs], [])], b)
                A.wait(mm, tr)
                t = A.mark(s_.activation(tmp[:, cs], b.ap, ACT.Sigmoid, bias=K.p_("w0", blk)))
                b.busy = [t]
                sg.append(t)
                b = K.bank()
                mm = K.product(b.ap, [(lora_w[LORA:P, blk * P:(blk + 1) * P], lora[LORA:P, cs], [])], b)
                A.wait(mm)
                t = A.mark(s_.activation(a[:, cs], b.ap, ACT.Sigmoid, bias=K.p_("a0", blk)))
                b.busy = [t]
                sg.append(t)
            A.wait(*sg)
            td = A.mark(s_.activation(tmp[:, :], tmp[:, :], ACT.Exp, scale=-math.exp(-0.5)))
            V.wait(tk)
            t = V.mark(v_.tensor_scalar(kk[:, :], k[:, :], K.p_("k_k", blk), None, ALU.mult))
            V.wait(td, t0)
            for c in range(NCH):
                tp = V.mark(v_.tensor_tensor_scan(Pd[:, c, 1:CH + 1], tmp[:, c * CH:(c + 1) * CH], zero[:, :], 1.0,
                                                  ALU.mult, ALU.add))
            V.wait(tp)
            V.mark(v_.tensor_copy(pmid[:, :], Pd[:, :, 1 + MID]))
            t2 = V.mark(v_.reciprocal(rmid[:, :], Pd[:, :, 1 + MID]))
            V.wait(t2)
            V.mark(v_.tensor_copy(Pd[:, :, 0], rmid[:, :]))
            tp = V.mark(v_.tensor_tensor(Pd[:, :, 1:CH + 1], Pd[:, :, 1:CH + 1],
                                         rmid[:, :].unsqueeze(2).broadcast_to([P, NCH, CH]), ALU.mult))
            V.wait(tp)
            V.mark(v_.tensor_tensor(gain[:, 0:NCH - 1], Pd[:, 0:NCH - 1, CH], pmid[:, 1:NCH], ALU.mult))
            tkk = V.last()
            G.wait(t)
            t = G.mark(g_.tensor_tensor(zraw[:, 0:S], kk[:, :], kk[:, :], ALU.mult))
            nn = []
            for h in range(NHALF):
                cs = slice(h * HALF, (h + 1) * HALF)
                b = K.bank()
                mm = K.product(b.ap, [(headsum[:, :], zraw[:, cs], [t])], b)
                V.wait(mm)
                t3 = V.mark(v_.tensor_scalar(b.ap, b.ap, 1e-24, None, ALU.max))
                A.wait(t3)
                t3 = A.mark(s_.activation(b.ap, b.ap, ACT.Sqrt))
                V.wait(t3, mm)
                t3 = V.mark(v_.reciprocal(b.ap, b.ap))
                V.wait(t3)
                t3 = V.mark(v_.tensor_tensor(kk[:, cs], kk[:, cs], b.ap, ALU.mult))
                b.busy = [t3]
                nn.append(t3)
            V.wait(*nn, *sg)
            V.wait(V.mark(v_.tensor_scalar(tmp[:, :], a[:, :], 1.0, K.p_("k_a", blk), ALU.subtract, ALU.mult)))
            tk = V.mark(v_.scalar_tensor_tensor(k[:, :], tmp[:, :], 1.0, k[:, :], ALU.add, ALU.mult))
            V.wait(tk)
            V.wait(tr, t)
            t = V.mark(v_.scalar_tensor_tensor(ck(tmp), rT, K.p_("r_k", blk), ck(k), ALU.mult, ALU.mult))
            b = K.bank()
            PE.wait(t, *b.busy)
            for c in range(NCH):
                mm = nc.tensor.matmul(b.ap[:, 2 * c:2 * c + 2], tmp[:, c * CH:(c + 1) * CH], headsel[:, :],
                                      start=True, stop=True)
            mm = PE.mark(mm)
            V.wait(mm)
            b.busy = [V.mark(v_.tensor_copy(bonus[:, :], b.ap[:, 0:2 * NCH]))]
            V.mark(v_.tensor_tensor(rT, rT, Pd[:, :, 1:CH + 1], ALU.mult))
            V.wait(V.mark(v_.scalar_tensor_tensor(AR[:, :, 0, :], ck(kk), -1.0, Pd[:, :, 0:CH], ALU.mult, ALU.mult)))
            t = V.mark(v_.reciprocal(ck(tmp), Pd[:, :, 1:CH + 1]))
            G.wait(V.last())
            G.wait(G.mark(g_.tensor_tensor(a[:, :], a[:, :], kk[:, :], ALU.mult)))
            G.mark(g_.tensor_tensor(Bt[:, :, :], ck(a), ck(tmp), ALU.mult))
            V.wait(t)
            V.mark(v_.tensor_tensor(Kt[:, :, :], ck(k), ck(tmp), ALU.mult))
            elem = [V.last(), G.last()]
            PE.wait(*elem, tv)
            for n, src in enumerate((AR[:, :, 0, :], Bt[:, :, :], Kt[:, :, :], ck(v))):
                for c0 in range(0, NCH, 4):
                    b = K.bank()
                    PE.wait(*b.busy)
                    for c in range(4):
                        mm = nc.tensor.transpose(b.ap[:, c * P:(c + 1) * P], src[:, c0 + c, :], K.ident[:, :])
                    mm = PE.mark(mm)
                    A.wait(mm)
                    tt = A.mark(s_.activation(tok[:, n, c0:c0 + 4, :], b.ap.rearrange("p (c t) -> p c t", c=4), ACT.Copy))
                    b.busy = [tt]
            K.handover()
        with ExitStack() as c2:
            bufs = [[K.sb(c2, f"m4_{i}", [P, 4, 4 * P])] + [K.sb(c2, f"{n}{i}", [P, 4, P]) for n in ("T", "TT", "Wm", "Al")]
                    for i in range(2)]
            Y = K.sb(c2, "Y", [P, NCH, 2, 64])
            V.mark(v_.memset(state[:, 0, :], 0.0))
            chain = {"state": [V.last()], "y": []}
            busy = [[], []]

            def batch(n, side):
                m4, T, TT, Wm, Al = bufs[side]
                tiles = [(q, 2 * n + q // 2, q % 2) for q in range(4)]
                flat = lambda x: x[:, :, :].rearrange("p q c -> p (q c)")
                ev = []
                for q, c, h in tiles:
                    b = K.bank()
                    PE.wait(*b.busy)
                    rhs = AR[hd(h), c, :, :]
                    nc.tensor.matmul(b.ap[:, 0:2 * P], Bt[hd(h), c, :], rhs, start=True, stop=True)
                    mm = PE.mark(nc.tensor.matmul(b.ap[:, 2 * P:4 * P], Kt[hd(h), c, :], rhs, start=True, stop=True))
                    V.wait(mm, *busy[side])
                    t = V.mark(v_.tensor_tensor(m4[:, q, :], b.ap, mask4[:, :], ALU.mult))
                    b.busy = [t]
                    ev.append(t)
                    yield
                G.wait(*ev, *busy[side])
                lv = lambda l: levels[:, l, :].unsqueeze(1).broadcast_to([P, 4, P])
                t = G.mark(g_.tensor_tensor(Al[:, :, :], m4[:, :, 0:P], lv(0), ALU.mult))
                V.wait(t)
                tTT = V.mark(v_.tensor_tensor(TT[:, :, :], Al[:, :, :], K.ident[:, :].unsqueeze(1).broadcast_to([P, 4, P]), ALU.add))
                b = K.bank()
                PE.wait(tTT, *b.busy)
                for q in range(4):
                    mm = nc.tensor.transpose(b.ap[:, q * P:(q + 1) * P], TT[:, q, :], K.ident[:, :])
                mm = PE.mark(mm)
                A.wait(mm, *busy[side])
                tT = A.mark(s_.activation(flat(T), b.ap, ACT.Copy))
                b.busy = [tT]
                read_Al = [tTT]
                yield
                for l in range(1, LEVELS):
                    G.wait(*read_Al)
                    tA = G.mark(g_.tensor_tensor(Al[:, :, :], m4[:, :, 0:P], lv(l), ALU.mult))
                    b = K.bank()
                    PE.wait(tA, tT, *b.busy)
                    for q in range(4):
                        mm = nc.tensor.matmul(b.ap[:, q * P:(q + 1) * P], Al[:, q, :], T[:, q, :], start=True, stop=True)
                    mm = PE.mark(mm)
                    read_Al = [mm]
                    A.wait(mm)
                    tW = A.mark(s_.activation(flat(Wm), b.ap, ACT.Copy))
                    b.busy = [tW]
                    yield
                    PE.wait(tW, tTT)
                    b2 = K.bank()
                    PE.wait(*b2.busy)
                    for q in range(4):
                        m2 = nc.tensor.matmul(b2.ap[:, q * P:(q + 1) * P], Wm[:, q, :], TT[:, q, :], start=True, stop=True)
                    m2 = PE.mark(m2)
                    if l < LEVELS - 1:
                        b1 = K.bank()
                        PE.wait(*b1.busy)
                        for q in range(4):
                            m1 = nc.tensor.matmul(b1.ap[:, q * P:(q + 1) * P], TT[:, q, :], Wm[:, q, :], start=True, stop=True)
                        m1 = PE.mark(m1)
                        V.wait(m1)
                        tT = V.mark(v_.tensor_tensor(flat(T), flat(T), b1.ap, ALU.add))
                        b1.busy = [tT]
                    V.wait(m2, m1)
                    tTT = V.mark(v_.tensor_tensor(flat(TT), flat(TT), b2.ap, ALU.add))
                    b2.busy = [tTT]
                    yield
                b = K.bank()
                PE.wait(*b.busy)
                for q, c, h in tiles:
                    mm = nc.tensor.matmul(b.ap[:, q * 64:(q + 1) * 64], m4[:, q, 2 * P:3 * P], tok[:, 3, c, hd(h)],
                                          start=True, stop=True)
                mm = PE.mark(mm)
                A.wait(mm, tT)
                A.mark(s_.activation(T[:, :, 64:128], b.ap[:, 0:256].rearrange("p (q c) -> p q c", q=4), ACT.Copy))
                A.mark(s_.activation(T[:, :, 0:64].rearrange("p (c h) k -> p c h k", c=2),
                                     tok[:, 0, 2 * n:2 * n + 2, :].rearrange("p c (h k) -> p c h k", h=2), ACT.Copy))
                tX = A.last()
                b.busy = [tX]
                yield
                b = K.bank()
                PE.wait(tX, tTT, *b.busy)
                for q in range(4):
                    mm = nc.tensor.matmul(b.ap[:, q * P:(q + 1) * P], TT[:, q, :], T[:, q, :], start=True, stop=True)
                mm = PE.mark(mm)
                A.wait(mm)
                tW = A.mark(s_.activation(flat(Wm), b.ap, ACT.Copy))
                b.busy = [tW]
                yield
                bR, bM = K.bank(), K.bank()
                PE.wait(tW, *bR.busy, *bM.busy)
                for q, c, h in tiles:
                    nc.tensor.matmul(bR.ap[hd(h), (q // 2) * P:(q // 2 + 1) * P], Wm[:, q, 0:64], m4[:, q, P:2 * P],
                                     start=True, stop=True)
                for q, c, h in tiles:
                    o = (q // 2) * P
                    nc.tensor.matmul(bM.ap[hd(h), o:o + 64], Wm[:, q, 0:64], tok[:, 1, c, hd(h)], start=True, stop=True)
                for q, c, h in tiles:
                    o = (q // 2) * P + 64
                    nc.tensor.matmul(bM.ap[hd(h), o:o + 64], tok[:, 1, c, hd(h)], Wm[:, q, 64:128], start=True, stop=False)
                    mm = nc.tensor.matmul(bM.ap[hd(h), o:o + 64], tok[:, 2, c, hd(h)], tok[:, 3, c, hd(h)],
                                          start=False, stop=True)
                mm = PE.mark(mm)
                V.wait(mm)
                rh = TT[:, 0:2, :]
                V.mark(v_.tensor_tensor(rh, bR.ap[:, 0:2 * P].rearrange("p (c t) -> p c t", c=2),
                                        AR[:, 2 * n:2 * n + 2, 1, :], ALU.add))
                bR.busy = [V.last()]
                MT = TT[:, 2, :].rearrange("p (c k) -> p c k", c=2)
                for h in range(2):
                    V.mark(v_.tensor_tensor(MT[hd(h), :, :], bM.ap[hd(h), 0:2 * P].rearrange("p (c k) -> p c k", c=2)[:, :, 0:64],
                                            K.ident[hd(h), hd(h)].unsqueeze(1).broadcast_to([64, 2, 64]), ALU.add))
                gN = TT[:, 3, :].rearrange("p (c k) -> p c k", c=2)
                for i in range(2):
                    c = 2 * n + i
                    if c < NCH - 1:
                        V.mark(v_.tensor_scalar(gN[:, i, :], bM.ap[:, i * P + 64:(i + 1) * P], gain[:, c:c + 1], None, ALU.mult))
                bM.busy = [V.last()]
                ready_M = V.last()
                yield
                for i in range(2):
                    c = 2 * n + i
                    PE.wait(ready_M, *chain["state"])
                    if c < NCH - 1:
                        b = K.bank()
                        PE.wait(*b.busy)
                        for h in range(2):
                            mm = nc.tensor.matmul(b.ap[hd(h), 0:64], MT[hd(h), i, :], state[hd(h), c, :], start=True, stop=True)
                        mm = PE.mark(mm)
                        V.wait(mm)
                        t = V.mark(v_.scalar_tensor_tensor(state[:, c + 1, :], b.ap[:, 0:64], gain[:, c:c + 1], gN[:, i, :],
                                                           ALU.mult, ALU.add))
                        b.busy = [t]
                        chain["state"] = [t]
                    done = []
                    for h in range(2):
                        q = 2 * i + h
                        b = K.bank()
                        PE.wait(*b.busy)
                        o = b.ap[:, 0:64]
                        nc.tensor.matmul(o, TT[hd(h), i, :], state[hd(h), c, :], start=True, stop=False)
                        nc.tensor.matmul(o, m4[:, q, 3 * P:4 * P], tok[:, 3, c, hd(h)], start=False, stop=False)
                        mm = PE.mark(nc.tensor.matmul(o, m4[:, q, P:2 * P], Wm[:, q, 64:128], start=False, stop=True))
                        A.wait(mm)
                        t = A.mark(s_.activation(Y[:, c, h, :], o, ACT.Copy))
                        b.busy = [t]
                    chain["y"].append(t)
                    busy[side] = [mm, t, *chain["state"]]

            for n0 in (0, 2):
                running = [batch(n0, 0), batch(n0 + 1, 1)]
                while running:
                    running = [g for g in running if next(g, "end") != "end"]
            with ExitStack() as c3:
                sq = K.sb(c3, "sq", [P, 2 * NCH, 64])
                stat = K.sb(c3, "stat", [P, 6, 2 * NCH])
                yb = K.sb(c3, "yb", [P, S])
                Yh = Y[:, :, :, :].rearrange("p c h k -> p (c h) k")
                bc = lambda x: x.unsqueeze(2).broadcast_to([P, 2 * NCH, 64])
                V.wait(*chain["y"])
                V.wait(V.mark(v_.tensor_reduce(stat[:, 0, :], Yh, AX.X, ALU.add)))
                V.wait(V.mark(v_.tensor_scalar(stat[:, 0, :], stat[:, 0, :], 1.0 / 64, None, ALU.mult)))
                V.wait(V.mark(v_.tensor_tensor(Yh, Yh, bc(stat[:, 0, :]), ALU.subtract)))
                V.wait(V.mark(v_.tensor_tensor(sq[:, :, :], Yh, Yh, ALU.mult)))
                t = V.mark(v_.tensor_reduce(stat[:, 1, :], sq[:, :, :], AX.X, ALU.add))
                t = K.rsqrt(stat[:, 2, :], stat[:, 1, :], 1.0 / 64, GN_EPS, [stat[:, 3 + i, :] for i in range(3)], [t])
                V.wait(t)
                V.wait(V.mark(v_.tensor_tensor(Yh, Yh, bc(stat[:, 2, :]), ALU.mult)))
                V.wait(ln_done)
                Yc = Y[:, :, :, :].rearrange("p c h k -> p c (h k)")
                lb = lambda x: x[:, :].unsqueeze(1).broadcast_to([P, NCH, P])
                V.wait(V.mark(v_.tensor_tensor(Yc, Yc, lb(lnw), ALU.mult)))
                V.mark(v_.tensor_tensor(Yc, Yc, lb(lnb), ALU.add))
                V.wait(V.mark(v_.tensor_tensor(sq[:, :, :], tok[:, 3, :, :].rearrange("p c (h k) -> p (c h) k", h=2),
                                               bc(bonus[:, :]), ALU.mult)))
                ty = V.mark(v_.tensor_tensor(Yh, Yh, sq[:, :, :], ALU.add))
                V.wait(ty)
                for c0 in range(0, NCH, 4):
                    b = K.bank()
                    PE.wait(*b.busy)
                    for c in range(4):
                        mm = nc.tensor.matmul(b.ap[:, c * P:(c + 1) * P], sig_g[:, (c0 + c) * CH:(c0 + c + 1) * CH],
                                              g2[:, blk * P:(blk + 1) * P], start=True, stop=True)
                    mm = PE.mark(mm)
                    V.wait(mm)
                    ty = V.mark(v_.tensor_tensor(Yc[:, c0:c0 + 4, :], Yc[:, c0:c0 + 4, :],
                                                 b.ap.rearrange("p (c t) -> p c t", c=4), ALU.mult))
                    b.busy = [ty]
                    b = K.bank()
                    PE.wait(ty, *b.busy)
                    for c in range(4):
                        mm = nc.tensor.transpose(b.ap[:, c * P:(c + 1) * P], Yc[:, c0 + c, :], K.ident[:, :])
                    mm = PE.mark(mm)
                    A.wait(mm)
                    t = A.mark(s_.activation(yb[:, c0 * P:(c0 + 4) * P], b.ap, ACT.Copy))
                    b.busy = [t]
                t = K.store("yT", y_sem, yT_dram[blk], yb[:, :], A, [t])
                for e in (A, V, G, PE, K.SP):
                    e.wait(t)
            K.handover()
    K.close_ring()
    ctx.close()


def compressed_stage(K, hT, ready, cT, kpe):
    nc, io, A, V, G, PE = K.nc, K.io, K.A, K.V, K.G, K.PE
    with ExitStack() as ctx:
        K.open_ring(ctx, 5)
        w = io["w_in"][0]
        K.queue_weights([weight_block(w, 0, QRANK, k, k + 2) for k in range(0, ND, 2)] +
                        [weight_block(w, QRANK, KVRANK + ROPE, k, min(k + 3, ND)) for k in range(0, ND, 3)])
        gl = Slot(None, K.semaphore("gqkv"))
        z = K.sb(ctx, "z", [P, NT, QRANK])
        junk = K.sb(ctx, "junk", [P, QRANK])
        g = K.sb(ctx, "g", [P, QRANK + KVRANK])
        stat = K.sb(ctx, "stat", [P, 5, NT])
        K.load(gl, g[:, 0:QRANK], io["g_q_a"][0].partition_broadcast(P))
        gt = K.load(gl, g[:, QRANK:], io["g_kv_a"][0].partition_broadcast(P))
        freed = []
        for nk, tiles, width, rank, c0, g0 in ((ND, 4, QRANK, QRANK, 0, 0), (ND, 3, KVRANK + ROPE, KVRANK, NQ, QRANK)):
            marks = []

            def evacuate(t, bank, mm):
                A.wait(mm, *freed, *marks[-1:])
                if rank == KVRANK:
                    marks.append(A.mark(nc.scalar.activation(kpe[:, t, :], bank[:, rank:width], ACT.Copy)))
                A.mark(nc.scalar.activation(z[:, t, 0:rank], bank[:, 0:rank], ACT.Copy))
                last = A.mark(nc.scalar.activation(junk[:, 0:rank], bank[:, 0:rank], ACT.Square, accum_out=stat[:, 0, t:t + 1]))
                marks.append(last)
                return [last]
            K.token_major(hT, ready, 0, nk, width, tiles, range(NT), evacuate)
            tr = K.rsqrt(stat[:, 1, :], stat[:, 0, :], 1.0 / rank, EPS, [stat[:, 2 + i, :] for i in range(3)], marks)
            V.wait(tr, gt)
            for t in range(NT):
                tz = V.mark(nc.vector.scalar_tensor_tensor(z[:, t, 0:rank], z[:, t, 0:rank], stat[:, 1, t:t + 1],
                                                           g[:, g0:g0 + rank], ALU.mult, ALU.mult))
            freed = []
            for c in range(rank // P):
                for t0 in range(0, NT, 4):
                    b = K.bank()
                    PE.wait(tz, *b.busy)
                    for t in range(4):
                        mm = nc.tensor.transpose(b.ap[:, t * P:(t + 1) * P], z[:, t0 + t, c * P:(c + 1) * P], K.ident[:, :])
                    mm = PE.mark(mm)
                    freed.append(mm)
                    A.wait(mm)
                    tc = A.mark(nc.scalar.activation(cT[:, c0 + c, t0 * P:(t0 + 4) * P], b.ap, ACT.Copy))
                    b.busy = [tc]
        K.close_ring()
        K.handover()
    return tc


def angles(K, ctx):
    nc, io, A, V = K.nc, K.io, K.A, K.V
    half = ROPE // 2
    ld = Slot(None, K.semaphore("pos_load"))
    pos = K.sb(ctx, "pos", [NT, P], I32)
    posr = K.sb(ctx, "posr", [NT, P])
    posf = K.sb(ctx, "posf", [P, NT])
    freq = K.sb(ctx, "freq", [P, half])
    cs = K.sb(ctx, "cs", [P, 2, NT, half])
    ang = K.sb(ctx, "ang", [P, NT, half])
    n = K.sb(ctx, "n", [P, NT, half])
    ni = K.sb(ctx, "ni", [P, NT, half], I32)
    K.load(ld, pos[:, :], io["positions"].rearrange("b (t p) -> (b t) p", p=P))
    t = K.load(ld, freq[:, :], io["const"][:, CONST["freq"][0]:CONST["freq"][1]])
    V.wait(t)
    t = V.mark(nc.vector.tensor_copy(posr[:, :], pos[:, :]))
    b = K.bank()
    K.PE.wait(t, *b.busy)
    t = K.PE.mark(nc.tensor.transpose(b.ap[:, 0:NT], posr[:, :], K.ident[0:NT, 0:NT]))
    V.wait(t)
    b.busy = [V.mark(nc.vector.tensor_copy(posf[:, :], b.ap[:, 0:NT]))]
    V.wait(*b.busy)
    V.wait(V.mark(nc.vector.tensor_tensor(ang[:, :, :], posf[:, :].unsqueeze(2).broadcast_to([P, NT, half]),
                                          freq[:, :].unsqueeze(1).broadcast_to([P, NT, half]), ALU.mult)))
    p1 = 6.28125
    p2 = float(np.float32(2 * math.pi - p1).view(np.uint32) & np.uint32(0xFFFFF000)) and \
        float((np.array([2 * math.pi - p1], np.float32).view(np.uint32) & np.uint32(0xFFFFF000)).view(np.float32)[0])
    p3 = float(np.float32(2 * math.pi - p1 - p2))
    for i, (shift, add) in enumerate(((0.25, math.pi / 2), (0.0, 0.0))):
        r = cs[:, i, :, :]
        V.wait(V.mark(nc.vector.tensor_scalar(n[:, :, :], ang[:, :, :], 1 / (2 * math.pi), shift, ALU.mult, ALU.add)))
        V.wait(V.mark(nc.vector.tensor_copy(ni[:, :, :], n[:, :, :])))
        V.wait(V.mark(nc.vector.tensor_copy(n[:, :, :], ni[:, :, :])))
        V.wait(V.mark(nc.vector.scalar_tensor_tensor(r, n[:, :, :], -p1, ang[:, :, :], ALU.mult, ALU.add)))
        V.wait(V.mark(nc.vector.scalar_tensor_tensor(r, n[:, :, :], -p2, r, ALU.mult, ALU.add)))
        V.wait(V.mark(nc.vector.scalar_tensor_tensor(r, n[:, :, :], -p3, r, ALU.mult, ALU.add)))
        V.wait(V.mark(nc.vector.tensor_scalar(r, r, add, 3.1415925, ALU.add, ALU.min)))
        t = V.mark(nc.vector.tensor_scalar(r, r, -3.1415925, None, ALU.max))
        A.wait(t)
        t = A.mark(nc.scalar.activation(r, r, ACT.Sin))
    for e in (V, K.G):
        e.wait(t)
    return cs


def rope(K, x, cs, tmp, heads, after):
    nc, V = K.nc, K.V
    half = ROPE // 2
    x1, x2 = x[:, :, :, 0:half], x[:, :, :, half:ROPE]
    c, s = (cs[:, i, :, :].unsqueeze(2).broadcast_to([P, NT, heads, half]) for i in range(2))
    t4 = [tmp[:, i, 0:NT * heads * half].rearrange("p (t h k) -> p t h k", t=NT, h=heads) for i in range(4)]
    V.wait(*after)
    V.mark(nc.vector.tensor_tensor(t4[0], x1, c, ALU.mult))
    V.mark(nc.vector.tensor_tensor(t4[1], x2, s, ALU.mult))
    V.mark(nc.vector.tensor_tensor(t4[2], x2, c, ALU.mult))
    V.wait(V.mark(nc.vector.tensor_tensor(t4[3], x1, s, ALU.mult)))
    V.mark(nc.vector.tensor_tensor(x1, t4[0], t4[1], ALU.subtract))
    t = V.mark(nc.vector.tensor_tensor(x2, t4[2], t4[3], ALU.add))
    V.wait(t)
    return t


def attention_stage(K, cT, c_ready, kpe, oT):
    nc, io, A, V, G, PE = K.nc, K.io, K.A, K.V, K.G, K.PE
    ctx = ExitStack()
    cs = angles(K, ctx)
    tmp = K.sb(ctx, "ropetmp", [P, 4, NT * 2 * 16])
    causal = K.sb(ctx, "causal", [P, P])
    ld = Slot(None, K.semaphore("causal_load"))
    K.V.wait(K.load(ld, causal[:, :], io["const"][:, CONST["causal"][0]:CONST["causal"][1]]))
    kp4 = kpe[:, :, :].unsqueeze(2)
    kpe_ready = rope(K, kp4, cs, tmp, 1, [c_ready, A.last()])
    scale = QK ** -0.5

    class Pair:
        pass
    sets = []
    for i in range(2):
        s = Pair()
        s.w = Slot(K.sb(ctx, f"wqkv{i}", [P, NQ * 2 * QK + NKV * 256])[:, :], K.semaphore(f"wqkv{i}"))
        s.qT = K.sb(ctx, f"qT{i}", [P, 2, S])
        s.kT = K.sb(ctx, f"kT{i}", [P, 2, S])
        s.v = K.sb(ctx, f"v{i}", [P, NT, 2, VDIM])
        s.busy = []
        sets.append(s)
    qtok = K.sb(ctx, "qtok", [P, NT, 2, QK])
    ktok = K.sb(ctx, "ktok", [P, NT, 2, QK])
    otok = K.sb(ctx, "otok", [P, NT, P])
    Pm = Ring([Slot(K.sb(ctx, f"P{i}", [P, S])[:, :]) for i in range(3)])
    PT = Ring([Slot(K.sb(ctx, f"PT{i}", [P, NT, P])[:, :, :]) for i in range(2)])
    st = K.sb(ctx, "st", [P, 4, 2 * HEADS * NT])
    bank = [s for s in K.banks.slots]
    scores = Ring([Slot(K.psum[:, 0:2, :].rearrange("p b c -> p (b c)")), Slot(K.psum[:, 2:4, :].rearrange("p b c -> p (b c)"))])
    for s, (x, y) in zip(scores.slots, ((0, 1), (2, 3))):
        s.busy = [*bank[x].busy, *bank[y].busy]
    work = Ring([bank[4], bank[5]])
    outs = Ring([bank[6], bank[7]])
    tok_busy = {"q": [], "k": [], "o": []}

    def project(pair):
        s = sets[pair % 2]
        wq = s.w.ap[:, 0:NQ * 2 * QK].rearrange("p (k c) -> p k c", k=NQ)
        wkv = s.w.ap[:, NQ * 2 * QK:].rearrange("p (k c) -> p k c", k=NKV)
        K.load(s.w, wq, weight_block(io["w_uq"][0], pair * 2 * QK, 2 * QK)[0])
        t0 = K.load(s.w, wkv, weight_block(io["w_ukv"][0], pair * 256, 256)[0])
        tq, tk = [], []
        for t in range(NT):
            tc = slice(t * P, (t + 1) * P)
            b = work.next()
            mm = K.product(b.ap[:, 0:2 * QK], [(cT[:, k, tc], wq[:, k, :], [t0, c_ready]) for k in range(NQ)], b)
            A.wait(mm, *tok_busy["q"])
            x = A.mark(nc.scalar.activation(qtok[:, t, :, :], b.ap[:, 0:2 * QK].rearrange("p (h k) -> p h k", h=2), ACT.Copy))
            b.busy = [x]
            tq.append(x)
            yield
        for t in range(NT):
            tc = slice(t * P, (t + 1) * P)
            b = work.next()
            mm = K.product(b.ap[:, 0:256], [(cT[:, NQ + k, tc], wkv[:, k, :], []) for k in range(NKV)], b)
            A.wait(mm, *tok_busy["k"], *s.busy)
            src = b.ap[:, 0:256].rearrange("p (h c) -> p h c", h=2)
            A.mark(nc.scalar.activation(ktok[:, t, :, 0:NOPE], src[:, :, 0:NOPE], ACT.Copy))
            x = A.mark(nc.scalar.activation(s.v[:, t, :, :], src[:, :, NOPE:], ACT.Copy))
            b.busy = [x]
            tk.append(x)
            yield
        s.w.busy = [mm]
        tr = rope(K, qtok[:, :, :, NOPE:QK], cs, tmp, 2, tq)
        V.wait(kpe_ready, *tok_busy["k"])
        x = V.mark(nc.vector.tensor_copy(ktok[:, :, :, NOPE:QK], kpe[:, :, :].unsqueeze(2).broadcast_to([P, NT, 2, ROPE])))
        yield
        done = [tk[-1]]
        for name, src, dst, after in (("q", qtok, s.qT, [tr, *tq]), ("k", ktok, s.kT, [x, *tk])):
            for h in range(2):
                for t1 in range(0, NT, 4):
                    b = work.next()
                    PE.wait(*after, *b.busy)
                    for t in range(4):
                        mm = nc.tensor.transpose(b.ap[0:QK, t * P:(t + 1) * P], src[:, t1 + t, h, :], K.ident[:, :])
                    mm = PE.mark(mm)
                    V.wait(mm, *s.busy)
                    y = V.mark(nc.vector.tensor_copy(dst[0:QK, h, t1 * P:(t1 + 4) * P], b.ap[0:QK, :]))
                    b.busy = [y]
                    done.append(y)
                    yield
            tok_busy[name] = [mm]
        s.ready = done

    units = [(pair, h, qb) for pair in range(HEADS // 2) for h in range(2) for qb in range(NT)]
    live = {}

    def score(u):
        pair, h, qb = units[u]
        s = sets[pair % 2]
        n = (qb + 1) * P
        sc = scores.next()
        PE.wait(*s.ready, *sc.busy)
        for k0 in range(0, n, HALF):
            w = min(HALF, n - k0)
            mm = nc.tensor.matmul(sc.ap[:, k0:k0 + w], s.qT[0:QK, h, qb * P:(qb + 1) * P], s.kT[0:QK, h, k0:k0 + w],
                                  start=True, stop=True)
        mm = PE.mark(mm)
        V.wait(mm)
        V.wait(V.mark(nc.vector.tensor_tensor(sc.ap[:, qb * P:n], sc.ap[:, qb * P:n], causal[:, :], ALU.add)))
        V.wait(V.mark(nc.vector.reduce_max(st[:, 0, u:u + 1], sc.ap[:, 0:n], AX.X)))
        t = V.mark(nc.vector.tensor_scalar(st[:, 1, u:u + 1], st[:, 0, u:u + 1], -scale, None, ALU.mult))
        p = Pm.next()
        A.wait(t, *p.busy)
        t = A.mark(nc.scalar.activation(p.ap[:, 0:n], sc.ap[:, 0:n], ACT.Exp, bias=st[:, 1, u:u + 1], scale=scale,
                                        accum_out=st[:, 2, u:u + 1]))
        sc.busy = [t]
        V.wait(t)
        r = V.mark(nc.vector.reciprocal(st[:, 3, u:u + 1], st[:, 2, u:u + 1]))
        live[u] = [p, t, r, None, None]

    def turn(u):
        pair, h, qb = units[u]
        p, t = live[u][:2]
        x = PT.next()
        evs = []
        for j0 in range(0, qb + 1, 4):
            nj = min(4, qb + 1 - j0)
            b = work.next()
            PE.wait(t, *b.busy)
            for j in range(nj):
                mm = nc.tensor.transpose(b.ap[:, j * P:(j + 1) * P], p.ap[:, (j0 + j) * P:(j0 + j + 1) * P], K.ident[:, :])
            mm = PE.mark(mm)
            e, op = (V, nc.vector.tensor_copy) if j0 else (A, nc.scalar.copy)
            e.wait(mm, *x.busy)
            ev = e.mark(op(x.ap[:, j0:j0 + nj, :], b.ap[:, 0:nj * P].rearrange("p (j c) -> p j c", j=nj)))
            b.busy = [ev]
            evs.append(ev)
        p.busy = [mm]
        live[u][3:] = [x, evs]

    def output(u):
        pair, h, qb = units[u]
        s = sets[pair % 2]
        p, _, r, x, evs = live.pop(u)
        b = outs.next()
        mm = K.product(b.ap[:, 0:VDIM], [(x.ap[:, j, :], s.v[:, j, h, :], evs) for j in range(qb + 1)], b)
        x.busy = [mm]
        V.wait(mm, r, *tok_busy["o"])
        t = V.mark(nc.vector.tensor_scalar(otok[:, qb, h * VDIM:(h + 1) * VDIM], b.ap[:, 0:VDIM], st[:, 3, u:u + 1], None, ALU.mult))
        b.busy = [t]
        s.busy = [mm]
        if (h, qb) == (1, NT - 1):
            for t0 in range(0, NT, 4):
                b = outs.next()
                PE.wait(t, *b.busy)
                for i in range(4):
                    m2 = nc.tensor.transpose(b.ap[:, i * P:(i + 1) * P], otok[:, t0 + i, :], K.ident[:, :])
                m2 = PE.mark(m2)
                hi, lo = (o[:, pair, t0 * P:(t0 + 4) * P] for o in oT)
                A.wait(m2)
                th = A.mark(nc.scalar.activation(hi, b.ap, ACT.Copy))
                V.wait(th)
                tl = V.mark(nc.vector.tensor_tensor(lo, b.ap, hi.bitcast(F32), ALU.subtract))
                b.busy = [tl]
            tok_busy["o"] = [m2]

    for _ in project(0):
        pass
    feed = iter(())
    for i in range(len(units) + 2):
        if i < len(units):
            pair = units[i][0]
            if units[i][1:] == (0, 0):
                for _ in feed:
                    pass
                feed = project(pair + 1) if pair + 1 < HEADS // 2 else iter(())
                fed = -3
            score(i)
        fed += 1
        if fed > 0:
            for _ in range(3):
                next(feed, None)
        if 1 <= i < len(units) + 1:
            turn(i - 1)
        if i >= 2:
            output(i - 2)
    for s, (x, y) in zip(scores.slots, ((0, 1), (2, 3))):
        bank[x].busy = bank[y].busy = s.busy
    K.handover()
    ctx.close()


def load_split(K, name, dram, n, cols, pair):
    width = cols.stop - cols.start
    step = TILE // width
    out = []
    for k in range(0, n, step):
        m = min(step, n - k)
        s = K.staging.next()
        view = s.ap[:, 0:m * width].rearrange("p (k c) -> p k c", k=m)
        t = K.load(s, view, dram[k:k + m, :, cols].rearrange("k p c -> p k c"), after=K.stored[name])
        hi, lo = (x[:, k:k + m, :] for x in pair)
        done = K.split(view, hi, lo, [t], [])
        s.busy = done
        out += done
    return out


def residual_source(K, ctx, dram, name=None):
    slots = Ring([Slot(K.sb(ctx, f"res{i}", [P, HALF])[:, :], K.semaphore(f"res{K.names}")) for i in range(2)])
    rows = dram.rearrange("(t p) d -> t p d", p=P)

    def source(t, n):
        s = slots.next()
        return s, K.load(s, s.ap, rows[t][:, n * HALF:(n + 1) * HALF], after=K.stored.get(name, []))
    return source


def merge_stage(K, branches, gates, gate_name, w_out, res_dram, res_name, x, parts):
    nc, io, A, V, G, PE = K.nc, K.io, K.A, K.V, K.G, K.PE
    span = S // parts
    halves = span // HALF
    with ExitStack() as ctx:
        K.open_ring(ctx, 5)
        res = residual_source(K, ctx, res_dram, res_name)
        gs = Ring([Slot(K.sb(ctx, f"g{i}", [P, HALF])[:, :], K.semaphore(f"{gate_name}_load{i}")) for i in range(3)])
        ms = Ring([Slot(K.sb(ctx, f"m{i}", [P, HALF])[:, :]) for i in range(2)])
        ts = Ring([Slot(K.sb(ctx, "t", [P, HALF])[:, :])])
        merged = K.pair(ctx, "merged", [P, ND, span])
        merged_busy = []
        opened = []
        for part in range(parts):
            cols = slice(part * span, (part + 1) * span)
            inner = ExitStack()
            ops, waits = [], []
            if part == 0:
                for bi, (w, n, src) in enumerate(branches):
                    opened.append(src if not isinstance(src[0], str) else K.pair(ctx, f"br{bi}", [P, n, span]))
            else:
                for e in (K.A, K.G):
                    e.wait(PE.last())
            for op, (w, n, src) in zip(opened, branches):
                ops.append(op)
                waits.append(load_split(K, src[0], src[1], n, cols, op) if isinstance(src[0], str) else [A.last(), V.last(), G.last()])
            tiles = []
            for j in range(0, ND):
                for w, n, _ in branches:
                    if n > 8:
                        tiles += [weight_block(w, j * P, P, 0, n // 2), weight_block(w, j * P, P, n // 2, n)]
                    else:
                        tiles += [weight_block(w, j * P)]
            K.queue_weights(tiles)
            merged_ready = []
            for j in range(ND):
                taken = [[K.take() for _ in range(2 if n > 8 else 1)] for _, n, _ in branches]
                for h in range(halves):
                    hs = slice(h * HALF, (h + 1) * HALF)
                    gh = slice(part * span + h * HALF, part * span + (h + 1) * HALF)
                    prods = []
                    for bi, (op, tl) in enumerate(zip(ops, taken)):
                        g = gs.next()
                        gt = K.load(g, g.ap, gates[bi * ND + j, :, gh], after=K.stored[gate_name])
                        ks = [(hi[:, i, :], lo[:, i, :], d) for _, hi, lo, d in tl for i in range(hi.shape[1])]
                        terms = []
                        for k, (hi, lo, d) in enumerate(ks):
                            oc = hs if isinstance(branches[bi][2][0], str) else gh
                            terms += K.three((hi, lo), (op[0][:, k, oc], op[1][:, k, oc]), [*d, *waits[bi]])
                        b = K.bank()
                        mm = K.product(b.ap, terms, b)
                        prods.append((b, mm, g, gt))
                    (b0, mm0, g0, gt0), (b1, mm1, g1, gt1) = prods
                    m, t_ = ms.next(), ts.next()
                    V.wait(mm0, gt0, *t_.busy)
                    ta = V.mark(nc.vector.tensor_tensor(t_.ap, b0.ap, g0.ap, ALU.mult))
                    b0.busy, g0.busy = [ta], [ta]
                    V.wait(mm1, gt1, *m.busy)
                    tb = V.mark(nc.vector.tensor_tensor(m.ap, b1.ap, g1.ap, ALU.mult))
                    b1.busy, g1.busy = [tb], [tb]
                    V.wait(ta, tb)
                    tm = V.mark(nc.vector.tensor_tensor(m.ap, m.ap, t_.ap, ALU.add))
                    t_.busy = [tm]
                    done = K.split(m.ap, merged[0][:, j, hs], merged[1][:, j, hs], [tm], merged_busy)
                    m.busy = done
                    merged_ready += done
                K.release([s[0] for tl in taken for s in tl], mm)
            K.queue_weights([weight_block(w_out, n * HALF, HALF, k, k + 2) for n in range(2) for k in range(0, ND, 2)])
            for n in range(2):
                pre = {}

                def evacuate(t, bank, mm, n=n):
                    tt = part * (span // P) + t
                    s, rt = pre.pop(t)
                    V.wait(mm, rt)
                    v = V.mark(nc.vector.tensor_tensor(x[:, tt, n * HALF:(n + 1) * HALF], bank, s.ap, ALU.add))
                    s.busy = [v]
                    if t + 2 < span // P:
                        pre[t + 2] = res(tt + 2, n)
                    return [v]
                for t in range(2):
                    pre[t] = res(part * (span // P) + t, n)
                K.token_major(merged, merged_ready, 0, ND, HALF, 4, range(span // P), evacuate)
            merged_busy = [PE.last()]
        K.close_ring()
        K.handover()


def ffn_stage(K, x, hT, ready, blocks, up_tiles, make, w_down):
    nc, A, V, G, PE = K.nc, K.A, K.V, K.G, K.PE
    GRP = 2
    with ExitStack() as ctx:
        act = K.pair(ctx, "act", [P, 4, S])
        busy = [[] for _ in range(4)]
        done = {}
        groups = blocks // GRP
        plan = []
        nxt = 0
        for g in range(groups):
            want = min(blocks, GRP * (g + 1) + 1)
            while nxt < want:
                plan.append(("up", nxt))
                nxt += 1
            plan.append(("down", g))
        tiles = []
        for kind, i in plan:
            if kind == "up":
                tiles += up_tiles(i)
            else:
                tiles += [weight_block(w_down, n * HALF, HALF, GRP * i, GRP * (i + 1)) for n in range(2)]
        K.queue_weights(tiles)
        for kind, i in plan:
            if kind == "up":
                s = i % 4
                done[i] = make(i, (act[0][:, s, :], act[1][:, s, :]), busy[s])
            else:
                k0 = (GRP * i) % 4
                after = done[GRP * i] + done[GRP * i + 1]
                for n in range(2):
                    def evacuate(t, bank, mm, n=n):
                        dst = x[:, t, n * HALF:(n + 1) * HALF]
                        V.wait(mm, K.x_done.get((t, n)))
                        v = V.mark(nc.vector.tensor_tensor(dst, dst, bank, ALU.add))
                        K.x_done[(t, n)] = v
                        return [v]
                    K.token_major(act, after, k0, GRP, HALF, 1, range(NT), evacuate)
                for s in (k0, k0 + 1):
                    busy[s] = [PE.last()]
        K.handover()


def lru_stage(K, hT, ready, ya_dram, yb_dram):
    nc, io, A, V, G, PE = K.nc, K.io, K.A, K.V, K.G, K.PE
    w = io["w_in_2"][0]
    with ExitStack() as ctx:
        K.open_ring(ctx, 3)
        K.queue_weights([weight_block(w, c * P) for c in range(NL + PW // P)])
        nl2 = 2 * NL
        sp = K.sb(ctx, "sp", [P, 6, nl2])
        y, e, z, z2, acc, c_rate = (sp[:, i, :] for i in range(6))
        for i, n in enumerate(("lam_f_2", "lam_b_2")):
            V.mark(nc.vector.tensor_scalar(y[:, i * NL:(i + 1) * NL], K.param[:, K.col[n]:K.col[n] + NL], -1.0, None, ALU.mult))
        V.wait(V.last())
        V.wait(V.mark(nc.vector.tensor_scalar(e, y, -1.0, None, ALU.mult)))
        t = V.mark(nc.vector.tensor_tensor(e, e, y, ALU.min))
        A.wait(t)
        t = A.mark(nc.scalar.activation(e, e, ACT.Exp))
        V.wait(t)
        V.wait(V.mark(nc.vector.tensor_scalar(z, e, 2.0, None, ALU.add)))
        V.wait(V.mark(nc.vector.reciprocal(z, z)))
        V.wait(V.mark(nc.vector.tensor_tensor(z, z, e, ALU.mult)))
        V.wait(V.mark(nc.vector.tensor_tensor(z2, z, z, ALU.mult)))
        terms = 9
        V.wait(V.mark(nc.vector.memset(acc, 1.0 / (2 * terms - 1))))
        for n in range(terms - 2, -1, -1):
            V.wait(V.mark(nc.vector.tensor_tensor(acc, acc, z2, ALU.mult)))
            V.wait(V.mark(nc.vector.tensor_scalar(acc, acc, 1.0 / (2 * n + 1), None, ALU.add)))
        V.wait(V.mark(nc.vector.tensor_tensor(acc, acc, z, ALU.mult)))
        V.wait(V.mark(nc.vector.tensor_scalar(acc, acc, 2.0, None, ALU.mult)))
        V.wait(V.mark(nc.vector.scalar_tensor_tensor(acc, y, 0.0, acc, ALU.max, ALU.add)))
        neg = K.sb(ctx, "neg", [P, nl2])
        V.mark(nc.vector.tensor_scalar(c_rate, acc, -8.0, None, ALU.mult))
        t = V.mark(nc.vector.tensor_scalar(neg[:, :], acc, 8.0, None, ALU.mult))
        A.wait(t)

        raw = K.sb(ctx, "raw", [P, 16 + S + 16])
        wt = Slot(K.sb(ctx, "wbd", [P, 4, P])[:, :, :], K.semaphore("wbd_load"))
        xc = K.sb(ctx, "xc", [P, S])
        gt = [K.sb(ctx, f"gt{i}", [P, S]) for i in range(4)]
        dc = [K.sb(ctx, f"dc{i}", [P, S]) for i in range(2)]
        th = [K.sb(ctx, f"th{i}", [P, S]) for i in range(2)]
        hs = [K.sb(ctx, f"hs{i}", [P, S]) for i in range(2)]
        y_sem = Slot(None, K.semaphore("ya_store"))
        raw_busy, xc_busy, gt_busy, dc_busy, th_busy, hs_busy = [], [], [], [], [], []
        V.mark(nc.vector.memset(raw[:, 0:16], 0.0))
        tz = V.mark(nc.vector.memset(raw[:, 16 + S:], 0.0))
        V.wait(tz)
        A.wait(tz)
        for j in range(NL):
            wl = None
            for i, n in enumerate(("wa_f_2", "wx_f_2", "wa_b_2", "wx_b_2")):
                wl = K.load(wt, wt.ap[:, i, :], io[n][0, j])
            copies = []

            def evacuate(h, bank, mm):
                A.wait(mm, *raw_busy)
                t = A.mark(nc.scalar.activation(raw[:, 16 + h * HALF:16 + (h + 1) * HALF], bank, ACT.Copy))
                copies.append(t)
                return [t]
            K.channel_major(hT, ready, evacuate)
            tap = lambda k: raw[:, 16 + k - 2:16 + k - 2 + S]
            cw = lambda k: K.p_("conv_a_w_2", k * NL + j)
            A.wait(*copies, *xc_busy)
            t = A.mark(nc.scalar.activation(xc[:, :], tap(0), ACT.Identity, scale=cw(0), bias=K.p_("conv_a_b_2", j)))
            V.wait(t, *copies)
            for k in range(1, 4):
                t = V.mark(nc.vector.scalar_tensor_tensor(xc[:, :], tap(k), cw(k), xc[:, :], ALU.mult, ALU.add))
                V.wait(t)
            raw_busy = [t]
            tx = t
            marks = []
            for i, bn in enumerate(("ba_f_2", "bx_f_2", "ba_b_2", "bx_b_2")):
                for h in range(NHALF):
                    cs = slice(h * HALF, (h + 1) * HALF)
                    b = K.bank()
                    mm = K.product(b.ap, [(wt.ap[:, i, :], xc[:, cs], [wl, tx])], b)
                    A.wait(mm, *gt_busy)
                    t = A.mark(nc.scalar.activation(gt[i][:, cs], b.ap, ACT.Sigmoid, bias=K.p_(bn, j)))
                    b.busy = [t]
                    marks.append(t)
            wt.busy = [mm]
            A.wait(*marks, *dc_busy, *th_busy)
            te = []
            for d in range(2):
                ci = d * NL + j
                A.mark(nc.scalar.activation(dc[d][:, :], gt[2 * d][:, :], ACT.Exp, scale=c_rate[:, ci:ci + 1]))
                te.append(A.mark(nc.scalar.activation(th[d][:, :], gt[2 * d][:, :], ACT.Tanh, scale=neg[:, ci:ci + 1])))
            tv = []
            for d in range(2):
                r, i_ = gt[2 * d], gt[2 * d + 1]
                G.wait(te[d])
                G.mark(nc.gpsimd.tensor_tensor(r[:, :], dc[d][:, :], dc[d][:, :], ALU.mult))
                G.mark(nc.gpsimd.tensor_tensor(i_[:, :], i_[:, :], xc[:, :], ALU.mult))
                V.wait(te[d], G.last())
                V.wait(V.mark(nc.vector.scalar_tensor_tensor(th[d][:, :], r[:, :], 1.0, th[d][:, :], ALU.add, ALU.mult)))
                tv.append(V.mark(nc.vector.tensor_scalar(th[d][:, :], th[d][:, :], 1e-34, None, ALU.max)))
            for d in range(2):
                A.wait(tv[d])
                t = A.mark(nc.scalar.activation(th[d][:, :], th[d][:, :], ACT.Sqrt))
                V.wait(t)
                V.wait(V.mark(nc.vector.tensor_tensor(th[d][:, :], th[d][:, :], gt[2 * d + 1][:, :], ALU.mult)))
                V.wait(*hs_busy)
                if d == 0:
                    t = V.mark(nc.vector.tensor_tensor_scan(hs[0][:, :], dc[0][:, :], th[0][:, :], 0.0, ALU.mult, ALU.add))
                else:
                    t = V.mark(nc.vector.tensor_tensor_scan(hs[1][:, ::-1], dc[1][:, ::-1], th[1][:, ::-1], 0.0, ALU.mult, ALU.add))
            G.wait(t)
            tg = G.mark(nc.gpsimd.tensor_tensor(hs[0][:, :], hs[0][:, :], hs[1][:, :], ALU.add))
            ts = K.store("ya", y_sem, ya_dram[j], hs[0][:, :], G, [tg])
            hs_busy = [ts, tg]
            gt_busy = dc_busy = th_busy = [t]
            xc_busy = [mm, tg]
        K.handover()
        K.V.wait(*hs_busy)
        K.G.wait(*hs_busy)
        K.A.wait(*hs_busy)
        wp = Slot(K.sb(ctx, "wpool", [P, 2, GDIM])[:, :, :], K.semaphore("wpool_load"))
        rc = Slot(gt[0][:, :], K.semaphore("count_load"))
        sums = [K.sb(ctx, f"sums{i}", [P, 16 + S + 16]) for i in range(2)]
        raw2 = K.sb(ctx, "raw2", [P, 16 + S + 16])
        pooled = [dc[0], dc[1]]
        yb = Ring([Slot(th[0][:, :], K.semaphore("yb_store0")), Slot(th[1][:, :], K.semaphore("yb_store1"))])
        pooled_busy = []
        V.mark(nc.vector.memset(raw2[:, 0:16], 0.0))
        V.wait(V.mark(nc.vector.memset(raw2[:, 16 + S:], 0.0)))
        L = 16 + S + 16
        raws = Ring([Slot(raw), Slot(raw2)])
        for g, win in enumerate(WINDOWS):
            rl = K.load(rc, rc.ap, io["counts"][g].partition_broadcast(P))
            pl = K.load(wp, wp.ap, io["w_pool_2"][0, g].rearrange("(k p) n -> p k n", p=P))
            made = []
            for i in range(2):
                rs = raws.next()
                u = rs.ap
                copies = []

                def evacuate(h, bank, mm):
                    A.wait(mm, *rs.busy)
                    t = A.mark(nc.scalar.activation(u[:, 16 + h * HALF:16 + (h + 1) * HALF], bank, ACT.Copy))
                    copies.append(t)
                    return [t]
                K.channel_major(hT, ready, evacuate)
                V.wait(*copies)
                src, m, at = u, 1, 0
                while m < win:
                    dst = sums[at]
                    V.wait(V.mark(nc.vector.tensor_tensor(dst[:, 2 * m - 1:L], src[:, 2 * m - 1:L], src[:, m - 1:L - m], ALU.add)))
                    src, m, at = dst, 2 * m, 1 - at
                o = 16 + win // 2 - 1
                V.wait(rl, *pooled_busy)
                V.wait(V.mark(nc.vector.tensor_tensor(pooled[i][:, :], src[:, o:o + S], rc.ap, ALU.mult)))
                t = V.mark(nc.vector.tensor_tensor(pooled[i][:, :], pooled[i][:, :], u[:, 16:16 + S], ALU.subtract))
                rs.busy = [t]
                made.append(t)
            rc.busy = [t]
            for jo in range(2):
                blk = 2 * g + jo
                out = yb.next()
                for h in range(NHALF):
                    cs = slice(h * HALF, (h + 1) * HALF)
                    b = K.bank()
                    mm = K.product(b.ap, [(wp.ap[:, k, jo * P:(jo + 1) * P], pooled[k][:, cs], [pl, *made]) for k in range(2)], b)
                    V.wait(mm, *out.busy)
                    t = V.mark(nc.vector.tensor_scalar(out.ap[:, cs], b.ap, K.p_("b_pool_2", blk), K.p_("pool_scale_2", blk), ALU.add, ALU.mult))
                    b.busy = [t]
                out.busy = [K.store("yb", out, yb_dram[blk], out.ap, A, [t])]
            wp.busy = [mm]
            pooled_busy = [mm]
        for e in (K.A, K.V, K.G, K.PE, K.SP):
            for s in yb.slots:
                e.wait(*s.busy)
        K.close_ring()
        K.handover()


def norm_rows(K, x, gain, dram, name):
    nc, A, V, SP = K.nc, K.A, K.V, K.SP
    with ExitStack() as ctx:
        gb = K.sb(ctx, "grow", [P, D])
        gl = K.load(K.const_load, gb[:, :], gain.partition_broadcast(P))
        ys = Ring([Slot(K.sb(ctx, f"y{i}", [P, D])[:, :], K.semaphore(f"{name}_store{i}")) for i in range(3)])
        ss = K.sb(ctx, "ss", [P, 5, NT])
        rows = dram.rearrange("(t p) d -> t p d", p=P)
        for t in range(NT):
            s = ys.next()
            A.wait(*s.busy, *[K.x_done.get((t, n)) for n in range(2)])
            ts = A.mark(nc.scalar.activation(s.ap, x[:, t, :], ACT.Square, accum_out=ss[:, 0, t:t + 1]))
            tr = K.rsqrt(ss[:, 1, t:t + 1], ss[:, 0, t:t + 1], 1.0 / D, EPS, [ss[:, 2 + i, t:t + 1] for i in range(3)], [ts])
            V.wait(tr, gl)
            ty = V.mark(nc.vector.scalar_tensor_tensor(s.ap, x[:, t, :], ss[:, 1, t:t + 1], gb[:, :], ALU.mult, ALU.mult))
            s.busy = [K.store(name, s, rows[t], s.ap, SP, [ty])]
        for e in (K.A, K.V, K.G, K.PE, K.SP):
            for s in ys.slots:
                e.wait(*s.busy)


def program(nc, io, out):
    K = Kernel(nc, io)
    A, V, G, PE, SP = K.A, K.V, K.G, K.PE, K.SP
    K.setup()
    scratch = {}
    for name, shape in (("gates1", [2 * ND, P, S]), ("gates2", [2 * ND, P, S]), ("yT", [NR, P, S]),
                        ("ya", [NL, P, S]), ("yb", [PW // P, P, S]), ("x2", [S, D])):
        scratch[name] = nc.dram_tensor("scratch_" + name, shape, F32, kind="Internal").ap()

    right = ExitStack()
    hT = K.pair(right, "hT", [P, ND, S], side="right")
    with ExitStack() as ctx:
        ready = sum(K.norm(hT, io["g_mix"][0], K.dram_source(ctx, io["x"][0])), [])
    with ExitStack() as ctx:
        K.open_ring(ctx, 4)
        stores = gate_stage(K, ctx, hT, ready, io["w_in"][0], MLA_COLS + RWKV_COLS, None, scratch["gates1"], "gates1")
        K.close_ring()
        K.handover()
    for e in (A, V, G, PE, SP):
        e.wait(*stores)
    rwkv_stage(K, hT, ready, scratch["yT"])
    left = ExitStack()
    oT = K.pair(left, "oT", [P, NR, S])
    with ExitStack() as ctx:
        cT = K.sb(ctx, "cT", [P, NQ + NKV, S])
        kpe = K.sb(ctx, "kpe", [P, NT, ROPE])
        c_ready = compressed_stage(K, hT, ready, cT, kpe)
        right.close()
        attention_stage(K, cT, c_ready, kpe, oT)
    right = ExitStack()
    x = K.sb(right, "x", [P, NT, D], side="right")
    merge_stage(K, [(io["w_o_mla"][0], NR, oT), (io["w_o_rwkv"][0], NR, ("yT", scratch["yT"]))],
                scratch["gates1"], "gates1", io["w_out"][0], io["x"][0], None, x, 2)
    left.close()
    K.x_done = {}

    def sbuf_source(t):
        return x[:, t, :], [K.x_done.get((t, n)) for n in range(2)], (lambda token: None)

    hctx = ExitStack()
    hT = K.pair(hctx, "hT", [P, ND, S], side="right")
    ready = sum(K.norm(hT, io["g_ffn"][0], sbuf_source), [])
    with ExitStack() as ctx:
        K.open_ring(ctx, 4)
        rel = Ring([Slot(K.sb(ctx, f"rel{i}", [P, HALF])[:, :]) for i in range(3)])

        def squared_relu(j, dst, before):
            done = []

            def evacuate(h, bank, mm):
                cs = slice(h * HALF, (h + 1) * HALF)
                r = rel.next()
                A.wait(mm, *r.busy)
                t = A.mark(nc.scalar.activation(r.ap, bank, ACT.Relu))
                V.wait(t)
                tq = V.mark(nc.vector.tensor_tensor(r.ap, r.ap, bank, ALU.mult))
                d = K.split(r.ap, dst[0][:, cs], dst[1][:, cs], [tq], before)
                r.busy = d
                done.extend(d)
                return [tq]
            K.channel_major(hT, ready, evacuate)
            return done
        ffn_stage(K, x, hT, ready, DFF // P, lambda i: [weight_block(io["w_ffn_up"][0], i * P)], squared_relu,
                  io["w_ffn_down"][0])
        K.close_ring()
    K.handover()

    ready = sum(K.norm(hT, io["g_ple"][0], sbuf_source), [])
    with ExitStack() as ctx:
        pT = K.sb(ctx, "pT", [P, 2, S])
        prow = Slot(K.sb(ctx, "prow", [P, NT, PLE])[:, :, :], K.semaphore("prow_load"))
        wpp = Slot(K.sb(ctx, "wpp", [P, 2, D])[:, :, :], K.semaphore("wpp_load"))
        tp = K.load(prow, prow.ap, io["p"][0, 0].rearrange("(t p) c -> p t c", p=P))
        tw = K.load(wpp, wpp.ap, io["w_ple_proj"][0].rearrange("(k p) n -> p k n", p=P))
        K.open_ring(ctx, 5)
        K.queue_weights([weight_block(io["w_ple_gate"][0], n * HALF, HALF, k, k + 2) for n in range(2) for k in range(0, ND, 2)])
        for c in range(2):
            for t0 in range(0, NT, 4):
                b = K.bank()
                PE.wait(tp, *b.busy)
                for t in range(4):
                    mm = nc.tensor.transpose(b.ap[:, t * P:(t + 1) * P], prow.ap[:, t0 + t, c * P:(c + 1) * P], K.ident[:, :])
                mm = PE.mark(mm)
                V.wait(mm)
                tpt = V.mark(nc.vector.tensor_copy(pT[:, c, t0 * P:(t0 + 4) * P], b.ap))
                b.busy = [tpt]
        sg = Ring([Slot(K.sb(ctx, f"sg{i}", [P, HALF])[:, :]) for i in range(3)])
        for n in range(2):
            def evacuate(t, bank, mm, n=n):
                b = K.bank()
                m2 = K.product(b.ap, [(pT[:, k, t * P:(t + 1) * P], wpp.ap[:, k, n * HALF:(n + 1) * HALF], [tpt, tw])
                                      for k in range(2)], b)
                s = sg.next()
                A.wait(mm, *s.busy)
                ta = A.mark(nc.scalar.activation(s.ap, bank, ACT.Sigmoid))
                V.wait(ta, m2)
                tb = V.mark(nc.vector.tensor_tensor(s.ap, s.ap, b.ap, ALU.mult))
                b.busy = [tb]
                dst = x[:, t, n * HALF:(n + 1) * HALF]
                V.wait(tb)
                tx = V.mark(nc.vector.tensor_tensor(dst, dst, s.ap, ALU.add))
                s.busy = [tx]
                K.x_done[(t, n)] = tx
                return [ta]
            K.token_major(hT, ready, 0, ND, HALF, 4, range(NT), evacuate)
        K.close_ring()
        K.handover()
    norm_rows(K, x, io["g_final"], scratch["x2"], "x2")
    hctx.close()
    right.close()

    right = ExitStack()
    hT = K.pair(right, "hT", [P, ND, S], side="right")
    with ExitStack() as ctx:
        ready = sum(K.norm(hT, io["g_mix_2"][0], K.dram_source(ctx, scratch["x2"], "x2")), [])
    with ExitStack() as ctx:
        K.open_ring(ctx, 4)
        stores = gate_stage(K, ctx, hT, ready, io["w_in_2"][0], LW + PW, lambda c: K.p_("b_gate_2", c),
                            scratch["gates2"], "gates2")
        K.close_ring()
        K.handover()
    for e in (A, V, G, PE, SP):
        e.wait(*stores)
    lru_stage(K, hT, ready, scratch["ya"], scratch["yb"])
    right.close()
    right = ExitStack()
    x = K.sb(right, "x", [P, NT, D], side="right")
    merge_stage(K, [(io["p_a_2"][0], NL, ("ya", scratch["ya"])), (io["p_b_2"][0], PW // P, ("yb", scratch["yb"]))],
                scratch["gates2"], "gates2", io["w_out_2"][0], scratch["x2"], "x2", x, 2)
    K.x_done = {}

    hctx = ExitStack()
    hT = K.pair(hctx, "hT", [P, ND, S], side="right")
    ready = sum(K.norm(hT, io["g_ffn_2"][0], sbuf_source2(K, x)), [])
    with ExitStack() as ctx:
        K.open_ring(ctx, 4)
        raws = Ring([Slot(K.sb(ctx, f"up{i}", [P, S + 2])) for i in range(2)])
        conv = [Slot(K.sb(ctx, f"cv{i}", [P, S])[:, :]) for i in range(2)]
        for s in raws.slots:
            V.mark(nc.vector.memset(s.ap[:, 0:1], 0.0))
            V.wait(V.mark(nc.vector.memset(s.ap[:, S + 1:S + 2], 0.0)))
        A.wait(V.last())

        def gelu_product(j, dst, before):
            for part in range(2):
                c = part * NF2 + j
                raw, cv = raws.next(), conv[part]
                copies = []

                def evacuate(h, bank, mm):
                    A.wait(mm, *raw.busy)
                    t = A.mark(nc.scalar.activation(raw.ap[:, 1 + h * HALF:1 + (h + 1) * HALF], bank, ACT.Copy))
                    copies.append(t)
                    return [t]
                K.channel_major(hT, ready, evacuate)
                cw = lambda k: K.p_("conv_f_w_2", k * 2 * NF2 + c)
                A.wait(*copies, *cv.busy)
                t = A.mark(nc.scalar.activation(cv.ap, raw.ap[:, 0:S], ACT.Identity, scale=cw(0), bias=K.p_("conv_f_b_2", c)))
                V.wait(t)
                for k in (1, 2):
                    t = V.mark(nc.vector.scalar_tensor_tensor(cv.ap, raw.ap[:, k:k + S], cw(k), cv.ap, ALU.mult, ALU.add))
                    V.wait(t)
                raw.busy = [t]
                if part == 0:
                    A.wait(t)
                    tg = A.mark(nc.scalar.activation(cv.ap, cv.ap, ACT.Gelu_apprx_tanh))
            V.wait(t, tg)
            tm = V.mark(nc.vector.tensor_tensor(conv[0].ap, conv[0].ap, conv[1].ap, ALU.mult))
            conv[1].busy = [tm]
            d = K.split(conv[0].ap, dst[0], dst[1], [tm], before)
            conv[0].busy = d
            return d
        ffn_stage(K, x, hT, ready, NF2,
                  lambda i: [weight_block(io["w_up_2"][0], i * P), weight_block(io["w_up_2"][0], (NF2 + i) * P)],
                  gelu_product, io["w_down_2"][0])
        K.close_ring()
    K.handover()

    hctx.close()
    norm_rows(K, x, io["g_final_2"], out[0], "out")
    right.close()
    for toks in K.stored.values():
        SP.wait(*toks)
    K.stack.close()


def sbuf_source2(K, x):
    return lambda t: (x[:, t, :], [K.x_done.get((t, n)) for n in range(2)], (lambda token: None))


_INS = ["x", "p", "positions", "g_mix", "w_in", "g_q_a", "w_uq", "g_kv_a", "w_ukv", "w_o_mla", "mu_rwkv", "w0", "w2",
        "a0", "a2", "g2", "k_k", "k_a", "r_k", "ln_x_w", "ln_x_b", "w_o_rwkv", "w_out", "g_ffn", "w_ffn_up",
        "w_ffn_down", "g_ple", "w_ple_gate", "w_ple_proj", "g_final", "g_mix_2", "w_in_2", "b_gate_2", "conv_a_w_2",
        "conv_a_b_2", "wa_f_2", "ba_f_2", "wx_f_2", "bx_f_2", "lam_f_2", "wa_b_2", "ba_b_2", "wx_b_2", "bx_b_2",
        "lam_b_2", "w_pool_2", "b_pool_2", "pool_scale_2", "p_a_2", "p_b_2", "w_out_2", "g_ffn_2", "w_up_2",
        "conv_f_w_2", "conv_f_b_2", "w_down_2", "g_final_2"]


def kernel(**inputs):
    import concourse.bacc as bacc
    from concourse.bass_utils import run_bass_kernel_spmd

    nc = bacc.Bacc("TRN2", target_bir_lowering=False, num_devices=1)
    arrays = {name: np.ascontiguousarray(inputs[name]) for name in _INS}
    arrays["const"] = constants()
    arrays["counts"] = pool_counts()
    feed, io = {}, {}
    for name, a in arrays.items():
        feed[f"in_{name}"] = a
        io[name] = nc.dram_tensor(f"in_{name}", a.shape, mybir.dt.from_np(a.dtype), kind="ExternalInput").ap()
    out = nc.dram_tensor("out_x", (1, S, D), F32, kind="ExternalOutput").ap()
    program(nc, io, out)
    r = run_bass_kernel_spmd(nc, [feed], core_ids=[0])
    return r.results[0]["out_x"]
```

```python
import math
from collections import namedtuple
from contextlib import ExitStack

import numpy as np
import concourse.bass as bass
from concourse import mybir

F32 = mybir.dt.float32
F32R = mybir.dt.float32r
I32 = mybir.dt.int32
ALU = mybir.AluOpType
ACT = mybir.ActivationFunctionType
AX = mybir.AxisListType

P = 128
S = 1024
D = 1024
NT = S // P
ND = D // P
HALF = 512
NHALF = S // HALF
HEADS, NOPE, ROPE, VDIM = 8, 64, 32, 64
QK = NOPE + ROPE
QRANK, KVRANK = 384, 256
NQ, NKV = QRANK // P, KVRANK // P
MLA_COLS = QRANK + KVRANK + ROPE
RDIM = 512
NR = RDIM // P
LORA, GLORA = 64, 128
RWKV_COLS = 3 * RDIM + 2 * LORA + GLORA
NZ = RWKV_COLS // P
DFF = 4 * D
PLE = 256
EPS = 1e-6
GN_EPS = 64 * 1e-5
THETA = 10000.0
CH = 128
NCH = S // CH
MID = CH // 2 - 1
LEVELS = 7
LW = 1280
NL = LW // P
PW = 1024
WINDOWS = (2, 4, 8, 16)
GDIM = PW // len(WINDOWS)
DFF2 = 2816
NF2 = DFF2 // P

TILE = 1024

Token = namedtuple("Token", "sem value")
BARRIER = "tiles after this wait for pass_barrier()"

CONST = {}
_at = 0
for _name, _n in (("ident", P), ("mask4", 4 * P), ("levels", LEVELS * P), ("causal", P), ("headsum", P),
                  ("headsel", 2), ("freq", ROPE // 2)):
    CONST[_name] = (_at, _at + _n)
    _at += _n
CONST_COLS = _at

ROW_TILES = [
    [("mu_rwkv", NZ), ("w0", NR), ("a0", NR), ("k_k", NR), ("k_a", NR), ("r_k", NR)],
    [("b_gate_2", 16), ("conv_a_w_2", 4 * NL), ("conv_a_b_2", NL), ("ba_f_2", NL), ("bx_f_2", NL),
     ("lam_f_2", NL), ("ba_b_2", NL), ("bx_b_2", NL), ("lam_b_2", NL)],
    [("b_pool_2", 8), ("pool_scale_2", 8), ("conv_f_b_2", 2 * NF2)],
    [("conv_f_w01", 4 * NF2)],
    [("conv_f_w2", 2 * NF2)],
]


def constants():
    c = np.zeros((P, CONST_COLS), np.float32)
    j, i = np.arange(P)[:, None], np.arange(P)[None, :]

    def put(name, a):
        c[:, CONST[name][0]:CONST[name][1]] = a
    put("ident", (j == i))
    strict, incl = (i > j), (i >= j)
    put("mask4", np.concatenate([strict, incl, strict, incl], 1))
    lv = []
    for l in range(LEVELS):
        b = 1 << l
        lv.append(((j // b) % 2 == 0) & (i // b == j // b + 1))
    put("levels", np.concatenate(lv, 1))
    put("causal", np.where(i <= j, 0.0, -1e30))
    put("headsum", (i // 64 == j // 64))
    put("headsel", (np.arange(2)[None, :] == j // 64))
    half = ROPE // 2
    put("freq", np.broadcast_to(
        np.float32(THETA) ** (-np.arange(half, dtype=np.float32) / np.float32(half)), (P, half)))
    return c


def pool_counts():
    t = np.arange(S)
    rows = []
    for w in WINDOWS:
        lo, hi = np.clip(t - w // 2, 0, S - 1), np.clip(t + w // 2 - 1, 0, S - 1)
        rows.append(np.float32(1.0) / (hi - lo + 1).astype(np.float32))
    return np.stack(rows).astype(np.float32)


class Engine:

    def __init__(self, queue, sem):
        self.queue, self.sem, self.count, self.seen = queue, sem, 0, {}

    def wait(self, *tokens):
        for t in tokens:
            if t is None:
                continue
            if isinstance(t, list):
                self.wait(*t)
                continue
            if self.seen.get(id(t.sem), 0) < t.value:
                self.queue.wait_ge(t.sem, t.value)
                self.seen[id(t.sem)] = t.value

    def mark(self, instruction):
        instruction.then_inc(self.sem, 1)
        self.count += 1
        return Token(self.sem, self.count)

    def last(self):
        return Token(self.sem, self.count) if self.count else None


class Slot:

    def __init__(self, ap, sem=None, lo=None):
        self.ap, self.lo, self.busy, self.sem, self.loads = ap, lo, [], sem, 0


class Ring:
    def __init__(self, slots):
        self.slots, self.at = slots, 0

    def next(self):
        s = self.slots[self.at % len(self.slots)]
        self.at += 1
        return s


class Kernel:
    def __init__(self, nc, io):
        self.nc, self.io = nc, io
        self.stack = ExitStack()
        self.names = 0
        self.PE = Engine(nc.tensor, self.semaphore("pe_done"))
        self.A = Engine(nc.scalar, self.semaphore("act_done"))
        self.V = Engine(nc.vector, self.semaphore("dve_done"))
        self.G = Engine(nc.gpsimd, self.semaphore("pool_done"))
        self.SP = Engine(nc.sync, self.semaphore("sp_done"))
        self.stored = {}

    def semaphore(self, name):
        return self.stack.enter_context(self.nc.semaphore(name))

    def sb(self, ctx, name, shape, dtype=F32, side=None):
        self.names += 1
        kw = {"side": side} if side else {}
        return ctx.enter_context(self.nc.sbuf_tensor(f"{name}_{self.names}", shape, dtype, **kw))

    def pair(self, ctx, name, shape, side=None):
        return (self.sb(ctx, name + "_hi", shape, F32R, side), self.sb(ctx, name + "_lo", shape, F32R, side))

    def load(self, slot, dst, src, queue=None, after=()):
        q = queue or self.SP
        q.wait(*slot.busy, *after)
        q.queue.dma_start(dst, src).then_inc(slot.sem, 16)
        slot.loads += 16
        return Token(slot.sem, slot.loads)

    def store(self, name, sem_slot, dst, src, queue, after=()):
        queue.wait(*after)
        queue.queue.dma_start(dst, src).then_inc(sem_slot.sem, 16)
        sem_slot.loads += 16
        t = Token(sem_slot.sem, sem_slot.loads)
        self.stored[name] = [o for o in self.stored.get(name, []) if o.sem is not sem_slot.sem] + [t]
        return t

    def handover(self):
        done = [e.last() for e in (self.PE, self.A, self.V, self.G)]
        for e in (self.A, self.V, self.G, self.SP):
            e.wait(*[t for t in done if t])

    def queue_weights(self, tiles):
        self.pending.extend(tiles)
        self.pump()

    def fetch(self, src, shape):
        s = self.staging.next()
        n = int(np.prod(shape[1:]))
        view = s.ap[:, 0:n]
        if len(shape) == 3:
            view = view.rearrange("p (k c) -> p k c", k=shape[1])
        t = self.load(s, view, src)
        s.busy = []
        return s, n, t

    def split(self, src, hi, lo, after, before):
        self.A.wait(*after, *before)
        th = self.A.mark(self.nc.scalar.activation(hi, src, ACT.Copy))
        self.G.wait(*after, *before, th)
        tl = self.G.mark(self.nc.gpsimd.tensor_tensor(lo, src, hi.bitcast(F32), ALU.subtract))
        return [th, tl]

    def pump(self):
        while self.pending or self.fetched:
            while self.pending and self.pending[0] is not BARRIER and len(self.fetched) < len(self.staging.slots):
                src, shape = self.pending.pop(0)
                self.fetched.append((*self.fetch(src, shape), shape))
            if not self.ring_free or not self.fetched:
                return
            stage, n, arrived, shape = self.fetched.pop(0)
            slot = self.ring_free.pop(0)
            done = self.split(stage.ap[:, 0:n], slot.ap[:, 0:n], slot.lo[:, 0:n], [arrived], slot.busy)
            stage.busy = done
            self.ready.append((slot, shape, done))

    def pass_barrier(self):
        assert self.pending[0] is BARRIER and not self.fetched
        self.pending.pop(0)
        self.pump()

    def take(self):
        self.pump()
        slot, shape, done = self.ready.pop(0)
        n = int(np.prod(shape[1:]))
        hi, lo = (x[:, 0:n].rearrange("p (k c) -> p k c", k=shape[1]) for x in (slot.ap, slot.lo))
        return slot, hi, lo, done

    def release(self, slots, token):
        for s in slots:
            s.busy = [token]
            self.ring_free.append(s)
        self.pump()

    def bank(self):
        return self.banks.next()

    def product(self, out, terms, bank=None):
        if bank is not None:
            self.PE.wait(*bank.busy)
        for n, (lhsT, rhs, after) in enumerate(terms):
            self.PE.wait(*after)
            mm = self.nc.tensor.matmul(out, lhsT, rhs, start=(n == 0), stop=(n == len(terms) - 1))
        return self.PE.mark(mm)

    @staticmethod
    def three(stat, mov, after):
        return [(stat[0], mov[0], after), (stat[0], mov[1], []), (stat[1], mov[0], [])]

    def rsqrt(self, out, total, scale, eps, tmp, after):
        nc, A, V = self.nc, self.A, self.V
        m, s, q = tmp
        V.wait(*after)
        t = V.mark(nc.vector.tensor_scalar(m, total, scale, eps, ALU.mult, ALU.add))
        A.wait(t)
        t = A.mark(nc.scalar.activation(s, m, ACT.Sqrt))
        V.wait(t)
        V.wait(V.mark(nc.vector.reciprocal(out, s)))
        V.wait(V.mark(nc.vector.tensor_tensor(q, out, out, ALU.mult)))
        V.wait(V.mark(nc.vector.tensor_tensor(q, q, m, ALU.mult)))
        V.wait(V.mark(nc.vector.tensor_scalar(q, q, -0.5, 1.5, ALU.mult, ALU.add)))
        t = V.mark(nc.vector.tensor_tensor(out, out, q, ALU.mult))
        return t

    def setup(self):
        nc, io = self.nc, self.io
        st = self.stack
        self.psum = st.enter_context(nc.psum_tensor("psum", [P, 8, HALF], F32))
        self.banks = Ring([Slot(self.psum[:, b, :]) for b in range(8)])
        self.const_load = Slot(None, self.semaphore("const_load"))
        self.ident = self.sb(st, "ident", [P, P])
        nparam = sum(n for tile in ROW_TILES for _, n in tile)
        self.param = self.sb(st, "param", [P, nparam])
        self.col = {}
        self.squares = self.sb(st, "squares", [P, 7, NT])
        self.sq_done = {}
        self.staging = Ring([Slot(self.sb(st, f"stage{i}", [P, TILE])[:, :], self.semaphore(f"stage{i}_load"))
                             for i in range(3)])
        self.pending, self.fetched, self.ready = [], [], []
        self.ring_free = [Slot(hi[:, :], None, lo[:, :]) for hi, lo in
                          (self.pair(st, f"weight{i}", [P, TILE]) for i in range(5))]
        self.load(self.const_load, self.ident[:, :], io["const"][:, CONST["ident"][0]:CONST["ident"][1]])

    def load_parameters(self, ctx):
        io = self.io
        self.row_load = Slot(None, self.semaphore("row_load"))
        self.rows = [self.sb(ctx, f"rows{n}", [P, P]) for n in range(len(ROW_TILES))]
        at = 0
        for n, tile in enumerate(ROW_TILES):
            r = 0
            for name, k in tile:
                if name == "conv_f_w01":
                    src = io["conv_f_w_2"][0, 0:2, :].rearrange("a (b p) -> (a b) p", p=P)
                elif name == "conv_f_w2":
                    src = io["conv_f_w_2"][0, 2:3, :].rearrange("a (b p) -> (a b) p", p=P)
                elif name == "conv_a_w_2":
                    src = io[name][0, :, :].rearrange("a (b p) -> (a b) p", p=P)
                elif name == "r_k":
                    src = io[name].rearrange("l h n -> (l h n)").rearrange("(b p) -> b p", p=P)
                else:
                    src = io[name].rearrange("l n -> (l n)").rearrange("(b p) -> b p", p=P)
                arrived = self.load(self.row_load, self.rows[n][r:r + k, :], src, queue=self.G)
                self.col[name] = at + r
                r += k
            at += r
        self.col["conv_f_w_2"] = self.col["conv_f_w01"]
        return arrived

    def transpose_parameters(self, arrived):
        at = 0
        for n, tile in enumerate(ROW_TILES):
            k = sum(c for _, c in tile)
            b = self.bank()
            self.PE.wait(arrived, *b.busy)
            t = self.PE.mark(self.nc.tensor.transpose(b.ap[:, 0:k], self.rows[n][0:k, :], self.ident[0:k, 0:k]))
            self.V.wait(t)
            b.busy = [self.V.mark(self.nc.vector.tensor_copy(self.param[:, at:at + k], b.ap[:, 0:k]))]
            at += k
        for e in (self.A, self.V, self.G, self.PE, self.SP):
            e.wait(*b.busy)

    def p_(self, name, i):
        c = self.col[name] + i
        return self.param[:, c:c + 1]

    def square(self, x, t, n, x_ready, junk):
        self.A.wait(*x_ready)
        tok = self.A.mark(self.nc.scalar.activation(junk, x[:, t, n * HALF:(n + 1) * HALF], ACT.Square,
                                                    accum_out=self.squares[:, n, t:t + 1]))
        self.sq_done[(t, n)] = tok
        return tok

    def rstd_of(self, ts):
        V, sq, c = self.V, self.squares, slice(ts[0], ts[-1] + 1)
        V.wait(*[self.sq_done[(t, n)] for t in ts for n in range(2)])
        tot = V.mark(self.nc.vector.tensor_tensor(sq[:, 2, c], sq[:, 0, c], sq[:, 1, c], ALU.add))
        V.wait(tot)
        return self.rsqrt(sq[:, 3, c], sq[:, 2, c], 1.0 / D, EPS, [sq[:, 4 + i, c] for i in range(3)], [tot])

    def gain_row(self, ctx, gain):
        gb = self.sb(ctx, "gain", [P, D])
        s = Slot(None, self.semaphore(f"gain_load{self.names}"))
        return gb, self.load(s, gb[:, :], gain.partition_broadcast(P))

    def norm(self, x, hT, gain, rows=None):
        nc, A, V, PE = self.nc, self.A, self.V, self.PE
        ready, last = [], []
        with ExitStack() as ctx:
            gb, gl = self.gain_row(ctx, gain)
            xn = Ring([Slot(self.sb(ctx, f"xn{i}", [P, D])[:, :]) for i in range(2)])
            A.wait(PE.last())
            for half in range(NHALF):
                done = []
                ts = range(half * NT // 2, (half + 1) * NT // 2)
                tr = self.rstd_of(ts)
                V.wait(tr, gl)
                for t in ts:
                    n = xn.next()
                    V.wait(*n.busy)
                    tx = V.mark(nc.vector.scalar_tensor_tensor(n.ap, x[:, t, :], self.squares[:, 3, t:t + 1], gb[:, :],
                                                               ALU.mult, ALU.mult))
                    for k0 in range(0, ND, 4):
                        b = self.bank()
                        PE.wait(tx, *b.busy)
                        for k in range(4):
                            mm = nc.tensor.transpose(b.ap[:, k * P:(k + 1) * P],
                                                     n.ap[:, (k0 + k) * P:(k0 + k + 1) * P], self.ident[:, :])
                        tt = PE.mark(mm)
                        src = b.ap.rearrange("p (k c) -> p k c", k=4)
                        hi = hT[0][:, k0:k0 + 4, t * P:(t + 1) * P]
                        lo = hT[1][:, k0:k0 + 4, t * P:(t + 1) * P]
                        A.wait(tt)
                        th = A.mark(nc.scalar.activation(hi, src, ACT.Copy))
                        V.wait(th)
                        tl = V.mark(nc.vector.tensor_tensor(lo, src, hi.bitcast(F32), ALU.subtract))
                        b.busy = [tl]
                        done += [th, tl]
                    n.busy = [tt]
                ready.append(done)
        for e in (A, self.G, self.SP, V):
            e.wait(tt, tl, th)
        return ready

    def channel_major_steps(self, hT, ready, evacuate):
        slot, hi, lo, done = self.take()
        for h in range(NHALF):
            b = self.bank()
            terms = []
            for k in range(hi.shape[1]):
                cols = slice(h * HALF, (h + 1) * HALF)
                after = [*done, *of_half(ready, h)] if k == 0 else []
                terms += self.three((hi[:, k, :], lo[:, k, :]), (hT[0][:, k, cols], hT[1][:, k, cols]), after)
            t = self.product(b.ap, terms, b)
            b.busy = evacuate(h, b.ap, t)
            if h == NHALF - 1:
                self.release([slot], t)
            yield

    def channel_major(self, hT, ready, evacuate):
        for _ in self.channel_major_steps(hT, ready, evacuate):
            pass

    def token_major(self, xT, ready, k0, nk, cols, tiles, tokens, evacuate):
        taken = [self.take() for _ in range(tiles)]
        for t in tokens:
            tc = slice(t * P, (t + 1) * P)
            b = self.bank()
            out = b.ap[:, 0:cols]
            self.PE.wait(*b.busy, *of_half(ready, t * P // HALF))
            k, mm = 0, None
            for slot, hi, lo, done in taken:
                self.PE.wait(*done)
                for i in range(hi.shape[1]):
                    x = (xT[0][:, k0 + k, tc], xT[1][:, k0 + k, tc])
                    for n, (lhsT, rhs, _) in enumerate(self.three(x, (hi[:, i, :], lo[:, i, :]), [])):
                        mm = self.nc.tensor.matmul(out, lhsT, rhs, start=(k == 0 and n == 0), stop=(k == nk - 1 and n == 2))
                    k += 1
                if t == tokens[-1]:
                    done_with = self.PE.mark(mm)
                    self.release([slot], done_with)
            b.busy = evacuate(t, out, done_with if t == tokens[-1] else self.PE.mark(mm))


def of_half(ready, h):
    return ready[h] if ready and isinstance(ready[0], list) else ready


def weight_block(w, c, width=P, k0=0, k1=None):
    v = w.rearrange("(k p) n -> p k n", p=P)
    k1 = v.shape[1] if k1 is None else k1
    return v[:, k0:k1, c:c + width], (P, k1 - k0, width)


class Gates:

    def __init__(self, K, hT, ready, bias, dram, name):
        self.K, self.hT, self.ready, self.bias, self.dram, self.name = K, hT, ready, bias, dram, name
        self.stores = [K.semaphore(f"{name}_store{i}") for i in range(3)]
        self.loads = [0] * 3
        self.run = self.steps()

    def open(self, ctx):
        self.out = Ring([Slot(self.K.sb(ctx, f"gate{i}", [P, HALF])[:, :], s) for i, s in enumerate(self.stores)])
        for s, n in zip(self.out.slots, self.loads):
            s.loads = n

    def close(self):
        K = self.K
        for s in self.out.slots:
            for e in (K.A, K.V, K.G, K.SP):
                e.wait(*s.busy)
        self.loads = [s.loads for s in self.out.slots]

    def steps(self):
        K = self.K
        A = K.A
        for c in range(2 * ND):
            def evacuate(h, bank, mm):
                s = self.out.next()
                A.wait(mm, *s.busy)
                kw = {"bias": self.bias(c)} if self.bias else {}
                t = A.mark(K.nc.scalar.activation(s.ap, bank, ACT.Sigmoid, **kw))
                s.busy = [K.store(self.name, s, self.dram[c, :, h * HALF:(h + 1) * HALF], s.ap, A, [t])]
                return [t]
            yield from K.channel_major_steps(self.hT, self.ready, evacuate)

    def fill(self, n):
        for _ in range(n):
            next(self.run, None)


def rwkv_stage(K, hT, ready, yT_dram, gates):
    nc, io, A, V, G, PE = K.nc, K.io, K.A, K.V, K.G, K.PE
    ctx = ExitStack()
    v_, g_, s_ = nc.vector, nc.gpsimd, nc.scalar
    w = io["w_in"][0]
    col0 = MLA_COLS
    ld = Slot(None, K.semaphore("rwkv_load"))
    lora_w = K.sb(ctx, "lora_w", [P, RDIM])
    g2 = K.sb(ctx, "g2", [P, RDIM])
    mask4 = K.sb(ctx, "mask4", [P, 4 * P])
    levels = K.sb(ctx, "levels", [P, LEVELS, P])
    headsum = K.sb(ctx, "headsum", [P, P])
    headsel = K.sb(ctx, "headsel", [P, 2])
    cst = io["const"]
    c_ = lambda n: cst[:, CONST[n][0]:CONST[n][1]]
    for dst, src in ((lora_w[0:LORA, :], io["w2"][0]), (lora_w[LORA:P, :], io["a2"][0]), (g2[:, :], io["g2"][0]),
                     (mask4[:, :], c_("mask4")), (levels[:, :, :], c_("levels").rearrange("p (l c) -> p l c", l=LEVELS)),
                     (headsum[:, :], c_("headsum")), (headsel[:, :], c_("headsel"))):
        small = K.load(ld, dst, src)
    lora = K.sb(ctx, "lora", [P, S])
    sig_g = K.sb(ctx, "sig_g", [P, S])

    class Shift:
        busy = []

    def shifted(zraw, z, c, out_busy):
        V.wait(*Shift.busy)
        tz = V.mark(v_.memset(zraw[:, 0:1], 0.0))
        copies = []

        def evacuate(h, bank, mm):
            A.wait(mm, *Shift.busy)
            t = A.mark(s_.activation(zraw[:, 1 + h * HALF:1 + (h + 1) * HALF], bank, ACT.Copy))
            copies.append(t)
            return [t]
        K.channel_major(hT, ready, evacuate)
        V.wait(tz, *copies, *out_busy)
        t = V.mark(v_.tensor_tensor(z, zraw[:, 0:S], zraw[:, 1:S + 1], ALU.subtract))
        V.wait(t)
        t = V.mark(v_.scalar_tensor_tensor(z, z, K.p_("mu_rwkv", c), zraw[:, 1:S + 1], ALU.mult, ALU.add))
        Shift.busy = [t]
        return t

    with ExitStack() as c2:
        zraw = K.sb(c2, "zraw", [P, S + 1])
        t = shifted(zraw, lora[:, :], 12, [])
        A.wait(t)
        lora_ready = A.mark(s_.activation(lora[0:LORA, :], lora[0:LORA, :], ACT.Tanh))
        t = shifted(zraw, sig_g[:, :], 13, [])
        A.wait(t)
        sig_ready = A.mark(s_.activation(sig_g[:, :], sig_g[:, :], ACT.Sigmoid))
        K.handover()
    for e in (PE, V, G):
        e.wait(small, lora_ready, sig_ready)

    hd = lambda h: slice(h * 64, (h + 1) * 64)
    AR = K.sb(ctx, "AR", [P, NCH, 2, CH])
    Bt = K.sb(ctx, "Bt", [P, NCH, CH])
    Kt = K.sb(ctx, "Kt", [P, NCH, CH])
    tok = K.sb(ctx, "tok", [P, 4, NCH, P])
    gain = K.sb(ctx, "gain", [P, NCH])
    bonus = K.sb(ctx, "bonus", [P, 2 * NCH])
    state = K.sb(ctx, "state", [P, NCH + 1, 64])
    y_sem = Slot(None, K.semaphore("y_store"))
    ln_load = Slot(None, K.semaphore("ln_load"))

    for blk in range(NR):
        with ExitStack() as c2:
            zraw = K.sb(c2, "zraw", [P, S + 1])
            k = K.sb(c2, "k", [P, S])
            v = K.sb(c2, "v", [P, S])
            a = K.sb(c2, "a", [P, S])
            kk = K.sb(c2, "kk", [P, S])
            Pd = K.sb(c2, "Pd", [P, NCH, CH + 1])
            tmp = K.sb(c2, "tmp", [P, S])
            zero = K.sb(c2, "zero", [P, CH])
            gates.open(c2)
            rmid = K.sb(c2, "rmid", [P, NCH])
            pmid = K.sb(c2, "pmid", [P, NCH])
            rT = AR[:, :, 1, :]
            ck = lambda x: x[:, :].rearrange("p (c t) -> p c t", c=NCH)
            t0 = V.mark(v_.memset(zero[:, :], 0.0))
            tr = shifted(zraw, tmp[:, :], blk, [])
            A.wait(tr)
            tr = A.mark(s_.activation(rT, ck(tmp), ACT.Copy))
            tk = shifted(zraw, k[:, :], NR + blk, [])
            tv = shifted(zraw, v[:, :], 2 * NR + blk, [])
            sg = []
            for h in range(NHALF):
                cs = slice(h * HALF, (h + 1) * HALF)
                b = K.bank()
                mm = K.product(b.ap, [(lora_w[0:LORA, blk * P:(blk + 1) * P], lora[0:LORA, cs], [])], b)
                A.wait(mm, tr)
                t = A.mark(s_.activation(tmp[:, cs], b.ap, ACT.Sigmoid, bias=K.p_("w0", blk)))
                b.busy = [t]
                sg.append(t)
                b = K.bank()
                mm = K.product(b.ap, [(lora_w[LORA:P, blk * P:(blk + 1) * P], lora[LORA:P, cs], [])], b)
                A.wait(mm)
                t = A.mark(s_.activation(a[:, cs], b.ap, ACT.Sigmoid, bias=K.p_("a0", blk)))
                b.busy = [t]
                sg.append(t)
            A.wait(*sg)
            td = A.mark(s_.activation(tmp[:, :], tmp[:, :], ACT.Exp, scale=-math.exp(-0.5)))
            V.wait(tk)
            t = V.mark(v_.tensor_scalar(kk[:, :], k[:, :], K.p_("k_k", blk), None, ALU.mult))
            gates.fill(2)
            V.wait(td, t0)
            for c in range(NCH):
                tp = V.mark(v_.tensor_tensor_scan(Pd[:, c, 1:CH + 1], tmp[:, c * CH:(c + 1) * CH], zero[:, :], 1.0,
                                                  ALU.mult, ALU.add))
            V.wait(tp)
            V.mark(v_.tensor_copy(pmid[:, :], Pd[:, :, 1 + MID]))
            t2 = V.mark(v_.reciprocal(rmid[:, :], Pd[:, :, 1 + MID]))
            V.wait(t2)
            V.mark(v_.tensor_copy(Pd[:, :, 0], rmid[:, :]))
            tp = V.mark(v_.tensor_tensor(Pd[:, :, 1:CH + 1], Pd[:, :, 1:CH + 1],
                                         rmid[:, :].unsqueeze(2).broadcast_to([P, NCH, CH]), ALU.mult))
            V.wait(tp)
            V.mark(v_.tensor_tensor(gain[:, 0:NCH - 1], Pd[:, 0:NCH - 1, CH], pmid[:, 1:NCH], ALU.mult))
            tkk = V.last()
            G.wait(t)
            t = G.mark(g_.tensor_tensor(zraw[:, 0:S], kk[:, :], kk[:, :], ALU.mult))
            nn = []
            for h in range(NHALF):
                cs = slice(h * HALF, (h + 1) * HALF)
                b = K.bank()
                mm = K.product(b.ap, [(headsum[:, :], zraw[:, cs], [t])], b)
                V.wait(mm)
                t3 = V.mark(v_.tensor_scalar(b.ap, b.ap, 1e-24, None, ALU.max))
                A.wait(t3)
                t3 = A.mark(s_.activation(b.ap, b.ap, ACT.Sqrt))
                V.wait(t3, mm)
                t3 = V.mark(v_.reciprocal(b.ap, b.ap))
                V.wait(t3)
                t3 = V.mark(v_.tensor_tensor(kk[:, cs], kk[:, cs], b.ap, ALU.mult))
                b.busy = [t3]
                nn.append(t3)
                gates.fill(1)
            V.wait(*nn, *sg)
            V.wait(V.mark(v_.tensor_scalar(tmp[:, :], a[:, :], 1.0, K.p_("k_a", blk), ALU.subtract, ALU.mult)))
            tk = V.mark(v_.scalar_tensor_tensor(k[:, :], tmp[:, :], 1.0, k[:, :], ALU.add, ALU.mult))
            V.wait(tk)
            V.wait(tr, t)
            t = V.mark(v_.scalar_tensor_tensor(ck(tmp), rT, K.p_("r_k", blk), ck(k), ALU.mult, ALU.mult))
            b = K.bank()
            PE.wait(t, *b.busy)
            for c in range(NCH):
                mm = nc.tensor.matmul(b.ap[:, 2 * c:2 * c + 2], tmp[:, c * CH:(c + 1) * CH], headsel[:, :],
                                      start=True, stop=True)
            mm = PE.mark(mm)
            V.wait(mm)
            b.busy = [V.mark(v_.tensor_copy(bonus[:, :], b.ap[:, 0:2 * NCH]))]
            gates.fill(2)
            V.mark(v_.tensor_tensor(rT, rT, Pd[:, :, 1:CH + 1], ALU.mult))
            V.wait(V.mark(v_.scalar_tensor_tensor(AR[:, :, 0, :], ck(kk), -1.0, Pd[:, :, 0:CH], ALU.mult, ALU.mult)))
            t = V.mark(v_.reciprocal(ck(tmp), Pd[:, :, 1:CH + 1]))
            G.wait(V.last())
            G.wait(G.mark(g_.tensor_tensor(a[:, :], a[:, :], kk[:, :], ALU.mult)))
            G.mark(g_.tensor_tensor(Bt[:, :, :], ck(a), ck(tmp), ALU.mult))
            V.wait(t)
            V.mark(v_.tensor_tensor(Kt[:, :, :], ck(k), ck(tmp), ALU.mult))
            elem = [V.last(), G.last()]
            gates.fill(2)
            PE.wait(*elem, tv)
            for n, src in enumerate((AR[:, :, 0, :], Bt[:, :, :], Kt[:, :, :], ck(v))):
                for c0 in range(0, NCH, 4):
                    b = K.bank()
                    PE.wait(*b.busy)
                    for c in range(4):
                        mm = nc.tensor.transpose(b.ap[:, c * P:(c + 1) * P], src[:, c0 + c, :], K.ident[:, :])
                    mm = PE.mark(mm)
                    A.wait(mm)
                    tt = A.mark(s_.activation(tok[:, n, c0:c0 + 4, :], b.ap.rearrange("p (c t) -> p c t", c=4), ACT.Copy))
                    b.busy = [tt]
            gates.close()
            K.handover()
        with ExitStack() as c2:
            Y = K.sb(c2, "Y", [P, NCH, 2, 64])
            cb = ExitStack()
            bufs = [[K.sb(cb, f"m4_{i}", [P, 4, 4 * P])] + [K.sb(cb, f"{n}{i}", [P, 4, P]) for n in ("T", "TT", "Wm", "Al")]
                    for i in range(2)]
            V.mark(v_.memset(state[:, 0, :], 0.0))
            chain = {"state": [V.last()], "y": []}
            busy = [[], []]

            def batch(n, side):
                m4, T, TT, Wm, Al = bufs[side]
                tiles = [(q, 2 * n + q // 2, q % 2) for q in range(4)]
                flat = lambda x: x[:, :, :].rearrange("p q c -> p (q c)")
                ev = []
                for q, c, h in tiles:
                    b = K.bank()
                    PE.wait(*b.busy)
                    rhs = AR[hd(h), c, :, :]
                    nc.tensor.matmul(b.ap[:, 0:2 * P], Bt[hd(h), c, :], rhs, start=True, stop=True)
                    mm = PE.mark(nc.tensor.matmul(b.ap[:, 2 * P:4 * P], Kt[hd(h), c, :], rhs, start=True, stop=True))
                    V.wait(mm, *busy[side])
                    t = V.mark(v_.tensor_tensor(m4[:, q, :], b.ap, mask4[:, :], ALU.mult))
                    b.busy = [t]
                    ev.append(t)
                    yield
                G.wait(*ev, *busy[side])
                lv = lambda l: levels[:, l, :].unsqueeze(1).broadcast_to([P, 4, P])
                t = G.mark(g_.tensor_tensor(Al[:, :, :], m4[:, :, 0:P], lv(0), ALU.mult))
                V.wait(t)
                tTT = V.mark(v_.tensor_tensor(TT[:, :, :], Al[:, :, :], K.ident[:, :].unsqueeze(1).broadcast_to([P, 4, P]), ALU.add))
                b = K.bank()
                PE.wait(tTT, *b.busy)
                for q in range(4):
                    mm = nc.tensor.transpose(b.ap[:, q * P:(q + 1) * P], TT[:, q, :], K.ident[:, :])
                mm = PE.mark(mm)
                A.wait(mm, *busy[side])
                tT = A.mark(s_.activation(flat(T), b.ap, ACT.Copy))
                b.busy = [tT]
                read_Al = [tTT]
                yield
                for l in range(1, LEVELS):
                    G.wait(*read_Al)
                    tA = G.mark(g_.tensor_tensor(Al[:, :, :], m4[:, :, 0:P], lv(l), ALU.mult))
                    b = K.bank()
                    PE.wait(tA, tT, *b.busy)
                    for q in range(4):
                        mm = nc.tensor.matmul(b.ap[:, q * P:(q + 1) * P], Al[:, q, :], T[:, q, :], start=True, stop=True)
                    mm = PE.mark(mm)
                    read_Al = [mm]
                    A.wait(mm)
                    tW = A.mark(s_.activation(flat(Wm), b.ap, ACT.Copy))
                    b.busy = [tW]
                    yield
                    PE.wait(tW, tTT)
                    b2 = K.bank()
                    PE.wait(*b2.busy)
                    for q in range(4):
                        m2 = nc.tensor.matmul(b2.ap[:, q * P:(q + 1) * P], Wm[:, q, :], TT[:, q, :], start=True, stop=True)
                    m2 = PE.mark(m2)
                    if l < LEVELS - 1:
                        b1 = K.bank()
                        PE.wait(*b1.busy)
                        for q in range(4):
                            m1 = nc.tensor.matmul(b1.ap[:, q * P:(q + 1) * P], TT[:, q, :], Wm[:, q, :], start=True, stop=True)
                        m1 = PE.mark(m1)
                        V.wait(m1)
                        tT = V.mark(v_.tensor_tensor(flat(T), flat(T), b1.ap, ALU.add))
                        b1.busy = [tT]
                    V.wait(m2, m1)
                    tTT = V.mark(v_.tensor_tensor(flat(TT), flat(TT), b2.ap, ALU.add))
                    b2.busy = [tTT]
                    yield
                b = K.bank()
                PE.wait(*b.busy)
                for q, c, h in tiles:
                    mm = nc.tensor.matmul(b.ap[:, q * 64:(q + 1) * 64], m4[:, q, 2 * P:3 * P], tok[:, 3, c, hd(h)],
                                          start=True, stop=True)
                mm = PE.mark(mm)
                A.wait(mm, tT)
                A.mark(s_.activation(T[:, :, 64:128], b.ap[:, 0:256].rearrange("p (q c) -> p q c", q=4), ACT.Copy))
                A.mark(s_.activation(T[:, :, 0:64].rearrange("p (c h) k -> p c h k", c=2),
                                     tok[:, 0, 2 * n:2 * n + 2, :].rearrange("p c (h k) -> p c h k", h=2), ACT.Copy))
                tX = A.last()
                b.busy = [tX]
                yield
                b = K.bank()
                PE.wait(tX, tTT, *b.busy)
                for q in range(4):
                    mm = nc.tensor.matmul(b.ap[:, q * P:(q + 1) * P], TT[:, q, :], T[:, q, :], start=True, stop=True)
                mm = PE.mark(mm)
                A.wait(mm)
                tW = A.mark(s_.activation(flat(Wm), b.ap, ACT.Copy))
                b.busy = [tW]
                yield
                bR, bM = K.bank(), K.bank()
                PE.wait(tW, *bR.busy, *bM.busy)
                for q, c, h in tiles:
                    nc.tensor.matmul(bR.ap[hd(h), (q // 2) * P:(q // 2 + 1) * P], Wm[:, q, 0:64], m4[:, q, P:2 * P],
                                     start=True, stop=True)
                for q, c, h in tiles:
                    o = (q // 2) * P
                    nc.tensor.matmul(bM.ap[hd(h), o:o + 64], Wm[:, q, 0:64], tok[:, 1, c, hd(h)], start=True, stop=True)
                for q, c, h in tiles:
                    o = (q // 2) * P + 64
                    nc.tensor.matmul(bM.ap[hd(h), o:o + 64], tok[:, 1, c, hd(h)], Wm[:, q, 64:128], start=True, stop=False)
                    mm = nc.tensor.matmul(bM.ap[hd(h), o:o + 64], tok[:, 2, c, hd(h)], tok[:, 3, c, hd(h)],
                                          start=False, stop=True)
                mm = PE.mark(mm)
                V.wait(mm)
                rh = TT[:, 0:2, :]
                V.mark(v_.tensor_tensor(rh, bR.ap[:, 0:2 * P].rearrange("p (c t) -> p c t", c=2),
                                        AR[:, 2 * n:2 * n + 2, 1, :], ALU.add))
                bR.busy = [V.last()]
                MT = TT[:, 2, :].rearrange("p (c k) -> p c k", c=2)
                for h in range(2):
                    V.mark(v_.tensor_tensor(MT[hd(h), :, :], bM.ap[hd(h), 0:2 * P].rearrange("p (c k) -> p c k", c=2)[:, :, 0:64],
                                            K.ident[hd(h), hd(h)].unsqueeze(1).broadcast_to([64, 2, 64]), ALU.add))
                gN = TT[:, 3, :].rearrange("p (c k) -> p c k", c=2)
                for i in range(2):
                    c = 2 * n + i
                    if c < NCH - 1:
                        V.mark(v_.tensor_scalar(gN[:, i, :], bM.ap[:, i * P + 64:(i + 1) * P], gain[:, c:c + 1], None, ALU.mult))
                bM.busy = [V.last()]
                ready_M = V.last()
                yield
                for i in range(2):
                    c = 2 * n + i
                    PE.wait(ready_M, *chain["state"])
                    if c < NCH - 1:
                        b = K.bank()
                        PE.wait(*b.busy)
                        for h in range(2):
                            mm = nc.tensor.matmul(b.ap[hd(h), 0:64], MT[hd(h), i, :], state[hd(h), c, :], start=True, stop=True)
                        mm = PE.mark(mm)
                        V.wait(mm)
                        t = V.mark(v_.scalar_tensor_tensor(state[:, c + 1, :], b.ap[:, 0:64], gain[:, c:c + 1], gN[:, i, :],
                                                           ALU.mult, ALU.add))
                        b.busy = [t]
                        chain["state"] = [t]
                    done = []
                    for h in range(2):
                        q = 2 * i + h
                        b = K.bank()
                        PE.wait(*b.busy)
                        o = b.ap[:, 0:64]
                        nc.tensor.matmul(o, TT[hd(h), i, :], state[hd(h), c, :], start=True, stop=False)
                        nc.tensor.matmul(o, m4[:, q, 3 * P:4 * P], tok[:, 3, c, hd(h)], start=False, stop=False)
                        mm = PE.mark(nc.tensor.matmul(o, m4[:, q, P:2 * P], Wm[:, q, 64:128], start=False, stop=True))
                        A.wait(mm)
                        t = A.mark(s_.activation(Y[:, c, h, :], o, ACT.Copy))
                        b.busy = [t]
                    chain["y"].append(t)
                    busy[side] = [mm, t, *chain["state"]]

            for n0 in (0, 2):
                running = [batch(n0, 0), batch(n0 + 1, 1)]
                while running:
                    running = [g for g in running if next(g, "end") != "end"]
            K.handover()
            cb.close()
            with ExitStack() as c3:
                sq = K.sb(c3, "sq", [P, 2 * NCH, 64])
                stat = K.sb(c3, "stat", [P, 6, 2 * NCH])
                yb = K.sb(c3, "yb", [P, S])
                lnw = K.sb(c3, "lnw", [P, P])
                lnb = K.sb(c3, "lnb", [P, P])
                K.load(ln_load, lnw[:, :], io["ln_x_w"][0, blk * P:(blk + 1) * P].partition_broadcast(P))
                ln_done = K.load(ln_load, lnb[:, :], io["ln_x_b"][0, blk * P:(blk + 1) * P].partition_broadcast(P))
                Yh = Y[:, :, :, :].rearrange("p c h k -> p (c h) k")
                bc = lambda x: x.unsqueeze(2).broadcast_to([P, 2 * NCH, 64])
                V.wait(*chain["y"])
                V.wait(V.mark(v_.tensor_reduce(stat[:, 0, :], Yh, AX.X, ALU.add)))
                V.wait(V.mark(v_.tensor_scalar(stat[:, 0, :], stat[:, 0, :], 1.0 / 64, None, ALU.mult)))
                V.wait(V.mark(v_.tensor_tensor(Yh, Yh, bc(stat[:, 0, :]), ALU.subtract)))
                V.wait(V.mark(v_.tensor_tensor(sq[:, :, :], Yh, Yh, ALU.mult)))
                t = V.mark(v_.tensor_reduce(stat[:, 1, :], sq[:, :, :], AX.X, ALU.add))
                t = K.rsqrt(stat[:, 2, :], stat[:, 1, :], 1.0 / 64, GN_EPS, [stat[:, 3 + i, :] for i in range(3)], [t])
                V.wait(t)
                V.wait(V.mark(v_.tensor_tensor(Yh, Yh, bc(stat[:, 2, :]), ALU.mult)))
                V.wait(ln_done)
                Yc = Y[:, :, :, :].rearrange("p c h k -> p c (h k)")
                lb = lambda x: x[:, :].unsqueeze(1).broadcast_to([P, NCH, P])
                V.wait(V.mark(v_.tensor_tensor(Yc, Yc, lb(lnw), ALU.mult)))
                V.mark(v_.tensor_tensor(Yc, Yc, lb(lnb), ALU.add))
                V.wait(V.mark(v_.tensor_tensor(sq[:, :, :], tok[:, 3, :, :].rearrange("p c (h k) -> p (c h) k", h=2),
                                               bc(bonus[:, :]), ALU.mult)))
                ty = V.mark(v_.tensor_tensor(Yh, Yh, sq[:, :, :], ALU.add))
                V.wait(ty)
                for c0 in range(0, NCH, 4):
                    b = K.bank()
                    PE.wait(*b.busy)
                    for c in range(4):
                        mm = nc.tensor.matmul(b.ap[:, c * P:(c + 1) * P], sig_g[:, (c0 + c) * CH:(c0 + c + 1) * CH],
                                              g2[:, blk * P:(blk + 1) * P], start=True, stop=True)
                    mm = PE.mark(mm)
                    V.wait(mm)
                    ty = V.mark(v_.tensor_tensor(Yc[:, c0:c0 + 4, :], Yc[:, c0:c0 + 4, :],
                                                 b.ap.rearrange("p (c t) -> p c t", c=4), ALU.mult))
                    b.busy = [ty]
                    b = K.bank()
                    PE.wait(ty, *b.busy)
                    for c in range(4):
                        mm = nc.tensor.transpose(b.ap[:, c * P:(c + 1) * P], Yc[:, c0 + c, :], K.ident[:, :])
                    mm = PE.mark(mm)
                    A.wait(mm)
                    t = A.mark(s_.activation(yb[:, c0 * P:(c0 + 4) * P], b.ap, ACT.Copy))
                    b.busy = [t]
                t = K.store("yT", y_sem, yT_dram[blk], yb[:, :], A, [t])
                for e in (A, V, G, PE, K.SP):
                    e.wait(t)
            K.handover()
    ctx.close()


def compressed_stage(K, hT, ready, cT, kpe):
    nc, io, A, V, G, PE = K.nc, K.io, K.A, K.V, K.G, K.PE
    with ExitStack() as ctx:
        w = io["w_in"][0]
        gl = Slot(None, K.semaphore("gqkv"))
        z = K.sb(ctx, "z", [P, NT, QRANK])
        junk = K.sb(ctx, "junk", [P, QRANK])
        g = K.sb(ctx, "g", [P, QRANK + KVRANK])
        stat = K.sb(ctx, "stat", [P, 5, NT])
        K.load(gl, g[:, 0:QRANK], io["g_q_a"][0].partition_broadcast(P))
        gt = K.load(gl, g[:, QRANK:], io["g_kv_a"][0].partition_broadcast(P))
        freed = []
        for nk, tiles, width, rank, c0, g0 in ((ND, 4, QRANK, QRANK, 0, 0), (ND, 3, KVRANK + ROPE, KVRANK, NQ, QRANK)):
            marks = []

            def evacuate(t, bank, mm):
                A.wait(mm, *freed, *marks[-1:])
                if rank == KVRANK:
                    marks.append(A.mark(nc.scalar.activation(kpe[:, t, :], bank[:, rank:width], ACT.Copy)))
                A.mark(nc.scalar.activation(z[:, t, 0:rank], bank[:, 0:rank], ACT.Copy))
                last = A.mark(nc.scalar.activation(junk[:, 0:rank], bank[:, 0:rank], ACT.Square, accum_out=stat[:, 0, t:t + 1]))
                marks.append(last)
                return [last]
            K.token_major(hT, ready, 0, nk, width, tiles, range(NT), evacuate)
            tr = K.rsqrt(stat[:, 1, :], stat[:, 0, :], 1.0 / rank, EPS, [stat[:, 2 + i, :] for i in range(3)], marks)
            V.wait(tr, gt)
            for t in range(NT):
                tz = V.mark(nc.vector.scalar_tensor_tensor(z[:, t, 0:rank], z[:, t, 0:rank], stat[:, 1, t:t + 1],
                                                           g[:, g0:g0 + rank], ALU.mult, ALU.mult))
            freed = []
            for c in range(rank // P):
                for t0 in range(0, NT, 4):
                    b = K.bank()
                    PE.wait(tz, *b.busy)
                    for t in range(4):
                        mm = nc.tensor.transpose(b.ap[:, t * P:(t + 1) * P], z[:, t0 + t, c * P:(c + 1) * P], K.ident[:, :])
                    mm = PE.mark(mm)
                    freed.append(mm)
                    A.wait(mm)
                    tc = A.mark(nc.scalar.activation(cT[:, c0 + c, t0 * P:(t0 + 4) * P], b.ap, ACT.Copy))
                    b.busy = [tc]
        K.handover()
    return tc


def angles(K, ctx):
    nc, io, A, V = K.nc, K.io, K.A, K.V
    half = ROPE // 2
    ld = Slot(None, K.semaphore("pos_load"))
    pos = K.sb(ctx, "pos", [NT, P], I32)
    posr = K.sb(ctx, "posr", [NT, P])
    posf = K.sb(ctx, "posf", [P, NT])
    freq = K.sb(ctx, "freq", [P, half])
    cs = K.sb(ctx, "cs", [P, 2, NT, half])
    ang = K.sb(ctx, "ang", [P, NT, half])
    n = K.sb(ctx, "n", [P, NT, half])
    ni = K.sb(ctx, "ni", [P, NT, half], I32)
    K.load(ld, pos[:, :], io["positions"].rearrange("b (t p) -> (b t) p", p=P))
    t = K.load(ld, freq[:, :], io["const"][:, CONST["freq"][0]:CONST["freq"][1]])
    V.wait(t)
    t = V.mark(nc.vector.tensor_copy(posr[:, :], pos[:, :]))
    b = K.bank()
    K.PE.wait(t, *b.busy)
    t = K.PE.mark(nc.tensor.transpose(b.ap[:, 0:NT], posr[:, :], K.ident[0:NT, 0:NT]))
    V.wait(t)
    b.busy = [V.mark(nc.vector.tensor_copy(posf[:, :], b.ap[:, 0:NT]))]
    V.wait(*b.busy)
    V.wait(V.mark(nc.vector.tensor_tensor(ang[:, :, :], posf[:, :].unsqueeze(2).broadcast_to([P, NT, half]),
                                          freq[:, :].unsqueeze(1).broadcast_to([P, NT, half]), ALU.mult)))
    p1 = 6.28125
    p2 = float(np.float32(2 * math.pi - p1).view(np.uint32) & np.uint32(0xFFFFF000)) and \
        float((np.array([2 * math.pi - p1], np.float32).view(np.uint32) & np.uint32(0xFFFFF000)).view(np.float32)[0])
    p3 = float(np.float32(2 * math.pi - p1 - p2))
    for i, (shift, add) in enumerate(((0.25, math.pi / 2), (0.0, 0.0))):
        r = cs[:, i, :, :]
        V.wait(V.mark(nc.vector.tensor_scalar(n[:, :, :], ang[:, :, :], 1 / (2 * math.pi), shift, ALU.mult, ALU.add)))
        V.wait(V.mark(nc.vector.tensor_copy(ni[:, :, :], n[:, :, :])))
        V.wait(V.mark(nc.vector.tensor_copy(n[:, :, :], ni[:, :, :])))
        V.wait(V.mark(nc.vector.scalar_tensor_tensor(r, n[:, :, :], -p1, ang[:, :, :], ALU.mult, ALU.add)))
        V.wait(V.mark(nc.vector.scalar_tensor_tensor(r, n[:, :, :], -p2, r, ALU.mult, ALU.add)))
        V.wait(V.mark(nc.vector.scalar_tensor_tensor(r, n[:, :, :], -p3, r, ALU.mult, ALU.add)))
        V.wait(V.mark(nc.vector.tensor_scalar(r, r, add, 3.1415925, ALU.add, ALU.min)))
        t = V.mark(nc.vector.tensor_scalar(r, r, -3.1415925, None, ALU.max))
        A.wait(t)
        t = A.mark(nc.scalar.activation(r, r, ACT.Sin))
    for e in (V, K.G):
        e.wait(t)
    return cs


def rope(K, x, cs, tmp, heads, after):
    nc, V = K.nc, K.V
    half = ROPE // 2
    x1, x2 = x[:, :, :, 0:half], x[:, :, :, half:ROPE]
    c, s = (cs[:, i, :, :].unsqueeze(2).broadcast_to([P, NT, heads, half]) for i in range(2))
    t4 = [tmp[:, i, 0:NT * heads * half].rearrange("p (t h k) -> p t h k", t=NT, h=heads) for i in range(4)]
    V.wait(*after)
    V.mark(nc.vector.tensor_tensor(t4[0], x1, c, ALU.mult))
    V.mark(nc.vector.tensor_tensor(t4[1], x2, s, ALU.mult))
    V.mark(nc.vector.tensor_tensor(t4[2], x2, c, ALU.mult))
    V.wait(V.mark(nc.vector.tensor_tensor(t4[3], x1, s, ALU.mult)))
    V.mark(nc.vector.tensor_tensor(x1, t4[0], t4[1], ALU.subtract))
    t = V.mark(nc.vector.tensor_tensor(x2, t4[2], t4[3], ALU.add))
    V.wait(t)
    return t


def attention_stage(K, cT, c_ready, kpe, oT):
    nc, io, A, V, G, PE = K.nc, K.io, K.A, K.V, K.G, K.PE
    ctx = ExitStack()
    cs = angles(K, ctx)
    tmp = K.sb(ctx, "ropetmp", [P, 4, NT * 2 * 16])
    causal = K.sb(ctx, "causal", [P, P])
    ld = Slot(None, K.semaphore("causal_load"))
    K.V.wait(K.load(ld, causal[:, :], io["const"][:, CONST["causal"][0]:CONST["causal"][1]]))
    kp4 = kpe[:, :, :].unsqueeze(2)
    kpe_ready = rope(K, kp4, cs, tmp, 1, [c_ready, A.last()])
    scale = QK ** -0.5

    class Pair:
        pass
    sets = []
    for i in range(2):
        s = Pair()
        s.w = Slot(K.sb(ctx, f"wqkv{i}", [P, NQ * 2 * QK + NKV * 256])[:, :], K.semaphore(f"wqkv{i}"))
        s.qT = K.sb(ctx, f"qT{i}", [P, 2, S])
        s.kT = K.sb(ctx, f"kT{i}", [P, 2, S])
        s.v = K.sb(ctx, f"v{i}", [P, NT, 2, VDIM])
        s.busy = []
        sets.append(s)
    qtok = K.sb(ctx, "qtok", [P, NT, 2, QK])
    ktok = K.sb(ctx, "ktok", [P, NT, 2, QK])
    otok = K.sb(ctx, "otok", [P, NT, P])
    Pm = Ring([Slot(K.sb(ctx, f"P{i}", [P, S])[:, :]) for i in range(3)])
    PT = Ring([Slot(K.sb(ctx, f"PT{i}", [P, NT, P])[:, :, :]) for i in range(2)])
    st = K.sb(ctx, "st", [P, 4, 2 * HEADS * NT])
    bank = [s for s in K.banks.slots]
    scores = Ring([Slot(K.psum[:, 0:2, :].rearrange("p b c -> p (b c)")), Slot(K.psum[:, 2:4, :].rearrange("p b c -> p (b c)"))])
    for s, (x, y) in zip(scores.slots, ((0, 1), (2, 3))):
        s.busy = [*bank[x].busy, *bank[y].busy]
    work = Ring([bank[4], bank[5]])
    outs = Ring([bank[6], bank[7]])
    tok_busy = {"q": [], "k": [], "o": []}

    def project(pair):
        s = sets[pair % 2]
        wq = s.w.ap[:, 0:NQ * 2 * QK].rearrange("p (k c) -> p k c", k=NQ)
        wkv = s.w.ap[:, NQ * 2 * QK:].rearrange("p (k c) -> p k c", k=NKV)
        K.load(s.w, wq, weight_block(io["w_uq"][0], pair * 2 * QK, 2 * QK)[0])
        t0 = K.load(s.w, wkv, weight_block(io["w_ukv"][0], pair * 256, 256)[0])
        tq, tk = [], []
        for t in range(NT):
            tc = slice(t * P, (t + 1) * P)
            b = work.next()
            mm = K.product(b.ap[:, 0:2 * QK], [(cT[:, k, tc], wq[:, k, :], [t0, c_ready]) for k in range(NQ)], b)
            A.wait(mm, *tok_busy["q"])
            x = A.mark(nc.scalar.activation(qtok[:, t, :, :], b.ap[:, 0:2 * QK].rearrange("p (h k) -> p h k", h=2), ACT.Copy))
            b.busy = [x]
            tq.append(x)
            yield
        for t in range(NT):
            tc = slice(t * P, (t + 1) * P)
            b = work.next()
            mm = K.product(b.ap[:, 0:256], [(cT[:, NQ + k, tc], wkv[:, k, :], []) for k in range(NKV)], b)
            A.wait(mm, *tok_busy["k"], *s.busy)
            src = b.ap[:, 0:256].rearrange("p (h c) -> p h c", h=2)
            A.mark(nc.scalar.activation(ktok[:, t, :, 0:NOPE], src[:, :, 0:NOPE], ACT.Copy))
            x = A.mark(nc.scalar.activation(s.v[:, t, :, :], src[:, :, NOPE:], ACT.Copy))
            b.busy = [x]
            tk.append(x)
            yield
        s.w.busy = [mm]
        tr = rope(K, qtok[:, :, :, NOPE:QK], cs, tmp, 2, tq)
        V.wait(kpe_ready, *tok_busy["k"])
        x = V.mark(nc.vector.tensor_copy(ktok[:, :, :, NOPE:QK], kpe[:, :, :].unsqueeze(2).broadcast_to([P, NT, 2, ROPE])))
        yield
        done = [tk[-1]]
        for name, src, dst, after in (("q", qtok, s.qT, [tr, *tq]), ("k", ktok, s.kT, [x, *tk])):
            for h in range(2):
                for t1 in range(0, NT, 4):
                    b = work.next()
                    PE.wait(*after, *b.busy)
                    for t in range(4):
                        mm = nc.tensor.transpose(b.ap[0:QK, t * P:(t + 1) * P], src[:, t1 + t, h, :], K.ident[:, :])
                    mm = PE.mark(mm)
                    V.wait(mm, *s.busy)
                    y = V.mark(nc.vector.tensor_copy(dst[0:QK, h, t1 * P:(t1 + 4) * P], b.ap[0:QK, :]))
                    b.busy = [y]
                    done.append(y)
                    yield
            tok_busy[name] = [mm]
        s.ready = done

    units = [(pair, h, qb) for pair in range(HEADS // 2) for h in range(2) for qb in range(NT)]
    live = {}

    def score(u):
        pair, h, qb = units[u]
        s = sets[pair % 2]
        n = (qb + 1) * P
        sc = scores.next()
        PE.wait(*s.ready, *sc.busy)
        for k0 in range(0, n, HALF):
            w = min(HALF, n - k0)
            mm = nc.tensor.matmul(sc.ap[:, k0:k0 + w], s.qT[0:QK, h, qb * P:(qb + 1) * P], s.kT[0:QK, h, k0:k0 + w],
                                  start=True, stop=True)
        mm = PE.mark(mm)
        V.wait(mm)
        V.wait(V.mark(nc.vector.tensor_tensor(sc.ap[:, qb * P:n], sc.ap[:, qb * P:n], causal[:, :], ALU.add)))
        V.wait(V.mark(nc.vector.reduce_max(st[:, 0, u:u + 1], sc.ap[:, 0:n], AX.X)))
        t = V.mark(nc.vector.tensor_scalar(st[:, 1, u:u + 1], st[:, 0, u:u + 1], -scale, None, ALU.mult))
        p = Pm.next()
        A.wait(t, *p.busy)
        t = A.mark(nc.scalar.activation(p.ap[:, 0:n], sc.ap[:, 0:n], ACT.Exp, bias=st[:, 1, u:u + 1], scale=scale,
                                        accum_out=st[:, 2, u:u + 1]))
        sc.busy = [t]
        V.wait(t)
        r = V.mark(nc.vector.reciprocal(st[:, 3, u:u + 1], st[:, 2, u:u + 1]))
        live[u] = [p, t, r, None, None]

    def turn(u):
        pair, h, qb = units[u]
        p, t = live[u][:2]
        x = PT.next()
        evs = []
        for j0 in range(0, qb + 1, 4):
            nj = min(4, qb + 1 - j0)
            b = work.next()
            PE.wait(t, *b.busy)
            for j in range(nj):
                mm = nc.tensor.transpose(b.ap[:, j * P:(j + 1) * P], p.ap[:, (j0 + j) * P:(j0 + j + 1) * P], K.ident[:, :])
            mm = PE.mark(mm)
            e, op = (V, nc.vector.tensor_copy) if j0 else (A, nc.scalar.copy)
            e.wait(mm, *x.busy)
            ev = e.mark(op(x.ap[:, j0:j0 + nj, :], b.ap[:, 0:nj * P].rearrange("p (j c) -> p j c", j=nj)))
            b.busy = [ev]
            evs.append(ev)
        p.busy = [mm]
        live[u][3:] = [x, evs]

    def output(u):
        pair, h, qb = units[u]
        s = sets[pair % 2]
        p, _, r, x, evs = live.pop(u)
        b = outs.next()
        mm = K.product(b.ap[:, 0:VDIM], [(x.ap[:, j, :], s.v[:, j, h, :], evs) for j in range(qb + 1)], b)
        x.busy = [mm]
        V.wait(mm, r, *tok_busy["o"])
        t = V.mark(nc.vector.tensor_scalar(otok[:, qb, h * VDIM:(h + 1) * VDIM], b.ap[:, 0:VDIM], st[:, 3, u:u + 1], None, ALU.mult))
        b.busy = [t]
        s.busy = [mm]
        if (h, qb) == (1, NT - 1):
            for t0 in range(0, NT, 4):
                b = outs.next()
                PE.wait(t, *b.busy)
                for i in range(4):
                    m2 = nc.tensor.transpose(b.ap[:, i * P:(i + 1) * P], otok[:, t0 + i, :], K.ident[:, :])
                m2 = PE.mark(m2)
                hi, lo = (o[:, pair, t0 * P:(t0 + 4) * P] for o in oT)
                A.wait(m2)
                th = A.mark(nc.scalar.activation(hi, b.ap, ACT.Copy))
                V.wait(th)
                tl = V.mark(nc.vector.tensor_tensor(lo, b.ap, hi.bitcast(F32), ALU.subtract))
                b.busy = [tl]
            tok_busy["o"] = [m2]

    for _ in project(0):
        pass
    feed = iter(())
    for i in range(len(units) + 2):
        if i < len(units):
            pair = units[i][0]
            if units[i][1:] == (0, 0):
                for _ in feed:
                    pass
                feed = project(pair + 1) if pair + 1 < HEADS // 2 else iter(())
                fed = -3
            score(i)
        fed += 1
        if fed > 0:
            for _ in range(3):
                next(feed, None)
        if 1 <= i < len(units) + 1:
            turn(i - 1)
        if i >= 2:
            output(i - 2)
    for s, (x, y) in zip(scores.slots, ((0, 1), (2, 3))):
        bank[x].busy = bank[y].busy = s.busy
    K.handover()
    ctx.close()


def load_split(K, name, dram, n, cols, pair, before):
    width = cols.stop - cols.start
    step = TILE // width
    out = []
    for k in range(0, n, step):
        m = min(step, n - k)
        s = K.staging.next()
        view = s.ap[:, 0:m * width].rearrange("p (k c) -> p k c", k=m)
        t = K.load(s, view, dram[k:k + m, :, cols].rearrange("k p c -> p k c"), after=K.stored[name])
        hi, lo = (x[:, k:k + m, :] for x in pair)
        done = K.split(view, hi, lo, [t], before)
        s.busy = done
        out += done
    return out


def residual_source(K, ctx, dram, name=None):
    slots = Ring([Slot(K.sb(ctx, f"res{i}", [P, HALF])[:, :], K.semaphore(f"res{K.names}")) for i in range(2)])
    rows = dram.rearrange("(t p) d -> t p d", p=P)

    def source(t, n):
        s = slots.next()
        return s, K.load(s, s.ap, rows[t][:, n * HALF:(n + 1) * HALF], after=K.stored.get(name, []))
    return source


def merge_stage(K, branches, gates, gate_name, w_out, res_dram, res_name, x, parts):
    nc, io, A, V, G, PE = K.nc, K.io, K.A, K.V, K.G, K.PE
    span = S // parts
    halves = span // HALF
    with ExitStack() as ctx:
        res = residual_source(K, ctx, res_dram, res_name)
        gs = Ring([Slot(K.sb(ctx, f"g{i}", [P, HALF])[:, :], K.semaphore(f"{gate_name}_load{i}")) for i in range(6)])
        merged = K.pair(ctx, "merged", [P, ND, span])
        merged_busy = []
        opened = []
        for part in range(parts):
            cols = slice(part * span, (part + 1) * span)
            ops, waits = [], []
            inputs_free = [PE.last()]
            if part == 0:
                for bi, (w, n, src) in enumerate(branches):
                    opened.append(src if not isinstance(src[0], str) else K.pair(ctx, f"br{bi}", [P, n, span]))
            for op, (w, n, src) in zip(opened, branches):
                ops.append(op)
                waits.append(load_split(K, src[0], src[1], n, cols, op, inputs_free) if isinstance(src[0], str) else [A.last(), V.last(), G.last()])
            K.pass_barrier()
            merged_ready = []
            gate_order = [(j, h, bi) for j in range(ND) for h in range(halves) for bi in range(2)]
            gate_tiles = {}

            def fetch_gates(n):
                while gate_order and len(gate_tiles) < n:
                    j, h, bi = key = gate_order.pop(0)
                    g = gs.next()
                    gh = slice(part * span + h * HALF, part * span + (h + 1) * HALF)
                    gate_tiles[key] = (g, K.load(g, g.ap, gates[bi * ND + j, :, gh], after=K.stored[gate_name]))
            fetch_gates(6)
            for j in range(ND):
                taken = [[K.take() for _ in range(2 if n > 8 else 1)] for _, n, _ in branches]
                for h in range(halves):
                    hs = slice(h * HALF, (h + 1) * HALF)
                    gh = slice(part * span + h * HALF, part * span + (h + 1) * HALF)
                    prods = []
                    for bi, (op, tl) in enumerate(zip(ops, taken)):
                        g, gt = gate_tiles.pop((j, h, bi))
                        ks = [(hi[:, i, :], lo[:, i, :], d) for _, hi, lo, d in tl for i in range(hi.shape[1])]
                        terms = []
                        for k, (hi, lo, d) in enumerate(ks):
                            oc = hs if isinstance(branches[bi][2][0], str) else gh
                            terms += K.three((hi, lo), (op[0][:, k, oc], op[1][:, k, oc]), [*d, *waits[bi]])
                        b = K.bank()
                        mm = K.product(b.ap, terms, b)
                        prods.append((b, mm, g, gt))
                    (b0, mm0, g0, gt0), (b1, mm1, g1, gt1) = prods
                    V.wait(mm0, gt0)
                    ta = V.mark(nc.vector.tensor_tensor(g0.ap, b0.ap, g0.ap, ALU.mult))
                    V.wait(mm1, gt1)
                    tb = V.mark(nc.vector.tensor_tensor(g1.ap, b1.ap, g1.ap, ALU.mult))
                    b0.busy, b1.busy = [ta], [tb]
                    V.wait(ta, tb)
                    tm = V.mark(nc.vector.tensor_tensor(g1.ap, g1.ap, g0.ap, ALU.add))
                    done = K.split(g1.ap, merged[0][:, j, hs], merged[1][:, j, hs], [tm], merged_busy)
                    g0.busy, g1.busy = [tm], done
                    fetch_gates(6)
                    merged_ready += done
                K.release([s[0] for tl in taken for s in tl], mm)
            for n in range(2):
                pre = {}

                def evacuate(t, bank, mm, n=n):
                    tt = part * (span // P) + t
                    s, rt = pre.pop(t)
                    V.wait(mm, rt)
                    v = V.mark(nc.vector.tensor_tensor(x[:, tt, n * HALF:(n + 1) * HALF], bank, s.ap, ALU.add))
                    sq = K.square(x, tt, n, [v], bank)
                    s.busy = [v]
                    if t + 2 < span // P:
                        pre[t + 2] = res(tt + 2, n)
                    return [sq]
                for t in range(2):
                    pre[t] = res(part * (span // P) + t, n)
                K.token_major(merged, merged_ready, 0, ND, HALF, 4, range(span // P), evacuate)
            merged_busy = [PE.last()]
        K.handover()


POOL_GATES = (2, 2, 1, 1)
GRP = 2


def ffn_plan(blocks):
    plan, nxt = [], 0
    for g in range(blocks // GRP):
        while nxt < min(blocks, GRP * (g + 1) + 1):
            plan.append(("up", nxt))
            nxt += 1
        plan.append(("down", g))
    return plan


def weight_order(io):
    w1, w2 = io["w_in"][0], io["w_in_2"][0]
    rcol = MLA_COLS
    out = [weight_block(w1, rcol + c * P) for c in (NZ - 2, NZ - 1)]
    for b in range(NR):
        out += [weight_block(w1, rcol + c * P) for c in (b, NR + b, 2 * NR + b)]
        out += [weight_block(w1, rcol + RWKV_COLS + c * P) for c in range(4 * b, 4 * b + 4)]
    out += [weight_block(w1, 0, QRANK, k, k + 2) for k in range(0, ND, 2)]
    out += [weight_block(w1, QRANK, KVRANK + ROPE, k, min(k + 3, ND)) for k in range(0, ND, 3)]

    def rows512(w, k0=0, k1=ND):
        return [weight_block(w, n * HALF, HALF, k, k + 2) for n in range(2) for k in range(k0, k1, 2)]

    def merge(branches, w_out):
        t = []
        for _ in range(2):
            t.append(BARRIER)
            for j in range(ND):
                for w, n in branches:
                    cuts = (0, n) if n <= ND else (0, n // 2, n)
                    t += [weight_block(w, j * P, P, a, b) for a, b in zip(cuts, cuts[1:])]
            t += rows512(w_out)
        return t

    def ffn(blocks, up, down):
        t = []
        for kind, i in ffn_plan(blocks):
            t += up(i) if kind == "up" else rows512(down, GRP * i, GRP * (i + 1))
        return t
    out += merge([(io["w_o_mla"][0], NR), (io["w_o_rwkv"][0], NR)], io["w_out"][0])
    out += ffn(DFF // P, lambda i: [weight_block(io["w_ffn_up"][0], i * P)], io["w_ffn_down"][0])
    out += rows512(io["w_ple_gate"][0])
    gate2 = [weight_block(w2, LW + PW + c * P) for c in range(2 * ND)]
    for c in range(NL):
        out += [weight_block(w2, c * P), gate2.pop(0)]
    for g in range(len(WINDOWS)):
        out += [weight_block(w2, LW + c * P) for c in (2 * g, 2 * g + 1)] + [gate2.pop(0) for _ in range(POOL_GATES[g])]
    out += merge([(io["p_a_2"][0], NL), (io["p_b_2"][0], PW // P)], io["w_out_2"][0])
    out += ffn(NF2, lambda i: [weight_block(io["w_up_2"][0], i * P), weight_block(io["w_up_2"][0], (NF2 + i) * P)],
               io["w_down_2"][0])
    return out


def ffn_stage(K, x, hT, ready, blocks, make):
    nc, A, V, G, PE = K.nc, K.A, K.V, K.G, K.PE
    with ExitStack() as ctx:
        act = K.pair(ctx, "act", [P, 4, S])
        busy = [[] for _ in range(4)]
        done = {}
        plan = ffn_plan(blocks)
        for kind, i in plan:
            if kind == "up":
                s = i % 4
                done[i] = make(i, (act[0][:, s, :], act[1][:, s, :]), busy[s])
            else:
                k0 = (GRP * i) % 4
                after = done[GRP * i] + done[GRP * i + 1]
                k_last = i == blocks // GRP - 1
                for n in range(2):
                    def evacuate(t, bank, mm, n=n):
                        dst = x[:, t, n * HALF:(n + 1) * HALF]
                        V.wait(mm, K.x_done.get((t, n)))
                        v = V.mark(nc.vector.tensor_tensor(dst, dst, bank, ALU.add))
                        K.x_done[(t, n)] = v
                        return [K.square(x, t, n, [v], bank)] if k_last else [v]
                    K.token_major(act, after, k0, GRP, HALF, 1, range(NT), evacuate)
                for s in (k0, k0 + 1):
                    busy[s] = [PE.last()]
        K.handover()


def lru_stage(K, hT, ready, ya_dram, yb_dram, gates):
    nc, io, A, V, G, PE = K.nc, K.io, K.A, K.V, K.G, K.PE
    w = io["w_in_2"][0]
    with ExitStack() as ctx:
        nl2 = 2 * NL
        sp = K.sb(ctx, "sp", [P, 6, nl2])
        y, e, z, z2, acc, c_rate = (sp[:, i, :] for i in range(6))
        for i, n in enumerate(("lam_f_2", "lam_b_2")):
            V.mark(nc.vector.tensor_scalar(y[:, i * NL:(i + 1) * NL], K.param[:, K.col[n]:K.col[n] + NL], -1.0, None, ALU.mult))
        V.wait(V.last())
        V.wait(V.mark(nc.vector.tensor_scalar(e, y, -1.0, None, ALU.mult)))
        t = V.mark(nc.vector.tensor_tensor(e, e, y, ALU.min))
        A.wait(t)
        t = A.mark(nc.scalar.activation(e, e, ACT.Exp))
        V.wait(t)
        V.wait(V.mark(nc.vector.tensor_scalar(z, e, 2.0, None, ALU.add)))
        V.wait(V.mark(nc.vector.reciprocal(z, z)))
        V.wait(V.mark(nc.vector.tensor_tensor(z, z, e, ALU.mult)))
        V.wait(V.mark(nc.vector.tensor_tensor(z2, z, z, ALU.mult)))
        terms = 9
        V.wait(V.mark(nc.vector.memset(acc, 1.0 / (2 * terms - 1))))
        for n in range(terms - 2, -1, -1):
            V.wait(V.mark(nc.vector.tensor_tensor(acc, acc, z2, ALU.mult)))
            V.wait(V.mark(nc.vector.tensor_scalar(acc, acc, 1.0 / (2 * n + 1), None, ALU.add)))
        V.wait(V.mark(nc.vector.tensor_tensor(acc, acc, z, ALU.mult)))
        V.wait(V.mark(nc.vector.tensor_scalar(acc, acc, 2.0, None, ALU.mult)))
        V.wait(V.mark(nc.vector.scalar_tensor_tensor(acc, y, 0.0, acc, ALU.max, ALU.add)))
        neg = K.sb(ctx, "neg", [P, nl2])
        V.mark(nc.vector.tensor_scalar(c_rate, acc, -8.0, None, ALU.mult))
        t = V.mark(nc.vector.tensor_scalar(neg[:, :], acc, 8.0, None, ALU.mult))
        A.wait(t)

        gates.open(ctx)
        raw = K.sb(ctx, "raw", [P, 16 + S + 16])
        wts = Ring([Slot(K.sb(ctx, f"wbd{i}", [P, 4, P])[:, :, :], K.semaphore(f"wbd_load{i}")) for i in range(2)])
        xcs = Ring([Slot(K.sb(ctx, f"xc{i}", [P, S])) for i in range(2)])
        gt = [Slot(K.sb(ctx, f"gt{i}", [P, S])) for i in range(4)]
        dc = [Slot(K.sb(ctx, f"dc{i}", [P, S])) for i in range(2)]
        th = [Slot(K.sb(ctx, f"th{i}", [P, S])) for i in range(2)]
        hs = [Slot(K.sb(ctx, f"hs{i}", [P, S])) for i in range(2)]
        y_sem = Slot(None, K.semaphore("ya_store"))
        raw_busy = []
        V.mark(nc.vector.memset(raw[:, 0:16], 0.0))
        tz = V.mark(nc.vector.memset(raw[:, 16 + S:], 0.0))
        V.wait(tz)
        A.wait(tz)

        def front(j):
            nonlocal raw_busy
            w_slot, xs = wts.next(), xcs.next()
            for i, n in enumerate(("wa_f_2", "wx_f_2", "wa_b_2", "wx_b_2")):
                wl = K.load(w_slot, w_slot.ap[:, i, :], io[n][0, j])
            copies = []

            def evacuate(h, bank, mm):
                A.wait(mm, *raw_busy)
                t = A.mark(nc.scalar.activation(raw[:, 16 + h * HALF:16 + (h + 1) * HALF], bank, ACT.Copy))
                copies.append(t)
                return [t]
            K.channel_major(hT, ready, evacuate)
            xc = xs.ap
            tap = lambda k: raw[:, 16 + k - 2:16 + k - 2 + S]
            cw = lambda k: K.p_("conv_a_w_2", k * NL + j)
            A.wait(*copies, *xs.busy)
            t = A.mark(nc.scalar.activation(xc[:, :], tap(0), ACT.Identity, scale=cw(0), bias=K.p_("conv_a_b_2", j)))
            V.wait(t, *copies)
            for k in range(1, 4):
                t = V.mark(nc.vector.scalar_tensor_tensor(xc[:, :], tap(k), cw(k), xc[:, :], ALU.mult, ALU.add))
                V.wait(t)
            raw_busy = [t]
            return w_slot, wl, xs, t

        head = front(0)
        for j in range(NL):
            w_slot, wl, xs, tx = head
            xc = xs.ap
            marks = []
            for i, bn in enumerate(("ba_f_2", "bx_f_2", "ba_b_2", "bx_b_2")):
                for h in range(NHALF):
                    cs = slice(h * HALF, (h + 1) * HALF)
                    b = K.bank()
                    mm = K.product(b.ap, [(w_slot.ap[:, i, :], xc[:, cs], [wl, tx])], b)
                    A.wait(mm, *gt[i].busy)
                    t = A.mark(nc.scalar.activation(gt[i].ap[:, cs], b.ap, ACT.Sigmoid, bias=K.p_(bn, j)))
                    b.busy = [t]
                    marks.append(t)
            w_slot.busy = [mm]
            te, tv, ti = [], [], []
            for d in range(2):
                ci = d * NL + j
                A.wait(*marks[4 * d:4 * d + 2], *dc[d].busy, *th[d].busy)
                A.mark(nc.scalar.activation(dc[d].ap[:, :], gt[2 * d].ap[:, :], ACT.Exp, scale=c_rate[:, ci:ci + 1]))
                te.append(A.mark(nc.scalar.activation(th[d].ap[:, :], gt[2 * d].ap[:, :], ACT.Tanh, scale=neg[:, ci:ci + 1])))
            for d in range(2):
                r, i_, th_, dc_ = gt[2 * d].ap, gt[2 * d + 1].ap, th[d].ap, dc[d].ap
                G.wait(te[d])
                ta = G.mark(nc.gpsimd.tensor_tensor(r[:, :], dc_[:, :], dc_[:, :], ALU.mult))
                ti.append(G.mark(nc.gpsimd.tensor_tensor(i_[:, :], i_[:, :], xc[:, :], ALU.mult)))
                V.wait(te[d], ta)
                t = V.mark(nc.vector.scalar_tensor_tensor(th_[:, :], r[:, :], 1.0, th_[:, :], ALU.add, ALU.mult))
                gt[2 * d].busy = [t]
                V.wait(t)
                tv.append(V.mark(nc.vector.tensor_scalar(th_[:, :], th_[:, :], 1e-34, None, ALU.max)))
            xs.busy = [mm, ti[1]]
            gates.fill(1)
            for d in range(2):
                th_, dc_, h_ = th[d].ap, dc[d].ap, hs[d].ap
                A.wait(tv[d])
                t = A.mark(nc.scalar.activation(th_[:, :], th_[:, :], ACT.Sqrt))
                V.wait(t, ti[d])
                t = V.mark(nc.vector.tensor_tensor(th_[:, :], th_[:, :], gt[2 * d + 1].ap[:, :], ALU.mult))
                gt[2 * d + 1].busy = [t]
                V.wait(t, *hs[d].busy)
                if d == 0:
                    t = V.mark(nc.vector.tensor_tensor_scan(h_[:, :], dc_[:, :], th_[:, :], 0.0, ALU.mult, ALU.add))
                else:
                    t = V.mark(nc.vector.tensor_tensor_scan(h_[:, ::-1], dc_[:, ::-1], th_[:, ::-1], 0.0, ALU.mult, ALU.add))
                dc[d].busy = th[d].busy = [t]
            G.wait(t)
            tg = G.mark(nc.gpsimd.tensor_tensor(hs[0].ap[:, :], hs[0].ap[:, :], hs[1].ap[:, :], ALU.add))
            ts = K.store("ya", y_sem, ya_dram[j], hs[0].ap[:, :], G, [tg])
            hs[0].busy, hs[1].busy = [ts], [tg]
            if j + 1 < NL:
                head = front(j + 1)
            gates.fill(1)
        for e in (A, V, G, K.SP):
            e.wait(*hs[0].busy, *dc[1].busy, *gt[3].busy)
        gt, dc, th = ([s.ap for s in x] for x in (gt, dc, th))
        wp = Slot(K.sb(ctx, "wpool", [P, 2, GDIM])[:, :, :], K.semaphore("wpool_load"))
        rc = Slot(gt[0][:, :], K.semaphore("count_load"))
        sums = [K.sb(ctx, f"sums{i}", [P, 16 + S + 16]) for i in range(2)]
        raw2 = K.sb(ctx, "raw2", [P, 16 + S + 16])
        pooled = [dc[0], dc[1]]
        yb = Ring([Slot(th[0][:, :], K.semaphore("yb_store0")), Slot(th[1][:, :], K.semaphore("yb_store1"))])
        pooled_busy = []
        V.mark(nc.vector.memset(raw2[:, 0:16], 0.0))
        V.wait(V.mark(nc.vector.memset(raw2[:, 16 + S:], 0.0)))
        L = 16 + S + 16
        raws = Ring([Slot(raw), Slot(raw2)])
        for g, win in enumerate(WINDOWS):
            rl = K.load(rc, rc.ap, io["counts"][g].partition_broadcast(P))
            pl = K.load(wp, wp.ap, io["w_pool_2"][0, g].rearrange("(k p) n -> p k n", p=P))
            made = []
            for i in range(2):
                rs = raws.next()
                u = rs.ap
                copies = []

                def evacuate(h, bank, mm):
                    A.wait(mm, *rs.busy)
                    t = A.mark(nc.scalar.activation(u[:, 16 + h * HALF:16 + (h + 1) * HALF], bank, ACT.Copy))
                    copies.append(t)
                    return [t]
                K.channel_major(hT, ready, evacuate)
                V.wait(*copies)
                src, m, at = u, 1, 0
                while m < win:
                    dst = sums[at]
                    V.wait(V.mark(nc.vector.tensor_tensor(dst[:, 2 * m - 1:L], src[:, 2 * m - 1:L], src[:, m - 1:L - m], ALU.add)))
                    src, m, at = dst, 2 * m, 1 - at
                o = 16 + win // 2 - 1
                V.wait(rl, *pooled_busy)
                V.wait(V.mark(nc.vector.tensor_tensor(pooled[i][:, :], src[:, o:o + S], rc.ap, ALU.mult)))
                t = V.mark(nc.vector.tensor_tensor(pooled[i][:, :], pooled[i][:, :], u[:, 16:16 + S], ALU.subtract))
                rs.busy = [t]
                made.append(t)
            rc.busy = [t]
            gates.fill(2 * POOL_GATES[g])
            for jo in range(2):
                blk = 2 * g + jo
                out = yb.next()
                for h in range(NHALF):
                    cs = slice(h * HALF, (h + 1) * HALF)
                    b = K.bank()
                    mm = K.product(b.ap, [(wp.ap[:, k, jo * P:(jo + 1) * P], pooled[k][:, cs], [pl, *made]) for k in range(2)], b)
                    V.wait(mm, *out.busy)
                    t = V.mark(nc.vector.tensor_scalar(out.ap[:, cs], b.ap, K.p_("b_pool_2", blk), K.p_("pool_scale_2", blk), ALU.add, ALU.mult))
                    b.busy = [t]
                out.busy = [K.store("yb", out, yb_dram[blk], out.ap, A, [t])]
            wp.busy = [mm]
            pooled_busy = [mm]
        for e in (K.A, K.V, K.G, K.SP):
            for s in yb.slots:
                e.wait(*s.busy)
        gates.close()
        K.handover()


def norm_rows(K, x, gain, dram, name, again):
    nc, A, V, SP = K.nc, K.A, K.V, K.SP
    with ExitStack() as ctx:
        gb, gl = K.gain_row(ctx, gain)
        st = Slot(None, K.semaphore(f"{name}_store"))
        rows = dram.rearrange("(t p) d -> t p d", p=P)
        for half in range(NHALF):
            ts = range(half * NT // 2, (half + 1) * NT // 2)
            V.wait(K.rstd_of(ts), gl)
            for t in ts:
                ty = V.mark(nc.vector.scalar_tensor_tensor(x[:, t, :], x[:, t, :], K.squares[:, 3, t:t + 1], gb[:, :],
                                                           ALU.mult, ALU.mult))
                if again:
                    b = K.bank()
                    A.wait(*b.busy)
                    for n in range(2):
                        b.busy = [K.square(x, t, n, [ty, *b.busy], b.ap)]
                K.store(name, st, rows[t], x[:, t, :], SP, [ty])
                yield_to = ty
        for e in (A, K.G, SP):
            e.wait(yield_to)


def program(nc, io, out):
    K = Kernel(nc, io)
    A, V, G, PE, SP = K.A, K.V, K.G, K.PE, K.SP
    K.setup()
    scratch = {}
    for name, shape in (("gates1", [2 * ND, P, S]), ("gates2", [2 * ND, P, S]), ("yT", [NR, P, S]),
                        ("ya", [NL, P, S]), ("yb", [PW // P, P, S]), ("x2", [S, D])):
        scratch[name] = nc.dram_tensor("scratch_" + name, shape, F32, kind="Internal").ap()

    K.queue_weights(weight_order(io))

    right = ExitStack()
    hT = K.pair(right, "hT", [P, ND, S], side="right")
    with ExitStack() as ctx:
        x = K.sb(ctx, "x_in", [P, NT, D])
        rows_in = io["x"][0].rearrange("(t p) d -> t p d", p=P)
        for t in range(NT):
            xl = Slot(None, K.semaphore(f"x_in_load{t}"))
            arrived = K.load(xl, x[:, t, :], rows_in[t], queue=(A, SP)[t % 2])
            for n in range(2):
                b = K.bank()
                b.busy = [K.square(x, t, n, [arrived, *b.busy], b.ap)]
        params = K.load_parameters(ctx)
        ready = K.norm(x, hT, io["g_mix"][0])
        K.transpose_parameters(params)
    rwkv_stage(K, hT, ready, scratch["yT"], Gates(K, hT, ready, None, scratch["gates1"], "gates1"))
    with ExitStack() as ctx:
        cT = K.sb(ctx, "cT", [P, NQ + NKV, S])
        kpe = K.sb(ctx, "kpe", [P, NT, ROPE])
        c_ready = compressed_stage(K, hT, ready, cT, kpe)
        right.close()
        right = ExitStack()
        oT = K.pair(right, "oT", [P, NR, S], side="right")
        attention_stage(K, cT, c_ready, kpe, oT)
    left = ExitStack()
    x = K.sb(left, "x", [P, NT, D])
    merge_stage(K, [(io["w_o_mla"][0], NR, oT), (io["w_o_rwkv"][0], NR, ("yT", scratch["yT"]))],
                scratch["gates1"], "gates1", io["w_out"][0], io["x"][0], None, x, 2)
    right.close()
    K.x_done = {}

    right = ExitStack()
    hT = K.pair(right, "hT", [P, ND, S], side="right")
    ready = K.norm(x, hT, io["g_ffn"][0])
    with ExitStack() as ctx:
        rel = Ring([Slot(K.sb(ctx, f"rel{i}", [P, HALF])[:, :]) for i in range(3)])

        def squared_relu(j, dst, before):
            done = []

            def evacuate(h, bank, mm):
                cs = slice(h * HALF, (h + 1) * HALF)
                r = rel.next()
                A.wait(mm, *r.busy)
                t = A.mark(nc.scalar.activation(r.ap, bank, ACT.Relu))
                V.wait(t)
                tq = V.mark(nc.vector.tensor_tensor(r.ap, r.ap, bank, ALU.mult))
                d = K.split(r.ap, dst[0][:, cs], dst[1][:, cs], [tq], before)
                r.busy = d
                done.extend(d)
                return [tq]
            K.channel_major(hT, ready, evacuate)
            return done
        ffn_stage(K, x, hT, ready, DFF // P, squared_relu)
    K.handover()

    with ExitStack() as ctx:
        pT = K.sb(ctx, "pT", [P, 2, S])
        prow = Slot(K.sb(ctx, "prow", [P, NT, PLE])[:, :, :], K.semaphore("prow_load"))
        wpp = Slot(K.sb(ctx, "wpp", [P, 2, D])[:, :, :], K.semaphore("wpp_load"))
        tp = K.load(prow, prow.ap, io["p"][0, 0].rearrange("(t p) c -> p t c", p=P))
        tw = K.load(wpp, wpp.ap, io["w_ple_proj"][0].rearrange("(k p) n -> p k n", p=P))
        for c in range(2):
            for t0 in range(0, NT, 4):
                b = K.bank()
                PE.wait(tp, *b.busy)
                for t in range(4):
                    mm = nc.tensor.transpose(b.ap[:, t * P:(t + 1) * P], prow.ap[:, t0 + t, c * P:(c + 1) * P], K.ident[:, :])
                mm = PE.mark(mm)
                V.wait(mm)
                tpt = V.mark(nc.vector.tensor_copy(pT[:, c, t0 * P:(t0 + 4) * P], b.ap))
                b.busy = [tpt]
        sg = Ring([Slot(K.sb(ctx, f"sg{i}", [P, HALF])[:, :]) for i in range(3)])
        ready = K.norm(x, hT, io["g_ple"][0])
        for n in range(2):
            def evacuate(t, bank, mm, n=n):
                b = K.bank()
                m2 = K.product(b.ap, [(pT[:, k, t * P:(t + 1) * P], wpp.ap[:, k, n * HALF:(n + 1) * HALF], [tpt, tw])
                                      for k in range(2)], b)
                s = sg.next()
                A.wait(mm, *s.busy)
                ta = A.mark(nc.scalar.activation(s.ap, bank, ACT.Sigmoid))
                V.wait(ta, m2)
                tb = V.mark(nc.vector.tensor_tensor(s.ap, s.ap, b.ap, ALU.mult))
                b.busy = [tb]
                dst = x[:, t, n * HALF:(n + 1) * HALF]
                V.wait(tb)
                tx = V.mark(nc.vector.tensor_tensor(dst, dst, s.ap, ALU.add))
                s.busy = [tx]
                return [K.square(x, t, n, [tx], bank)]
            K.token_major(hT, ready, 0, ND, HALF, 4, range(NT), evacuate)
        K.handover()
    norm_rows(K, x, io["g_final"], scratch["x2"], "x2", True)

    ready = K.norm(x, hT, io["g_mix_2"][0])
    left.close()
    for e in (A, V, G, K.SP):
        e.wait(*K.stored["x2"][-1:])
    gates2 = Gates(K, hT, ready, lambda c: K.p_("b_gate_2", c), scratch["gates2"], "gates2")
    lru_stage(K, hT, ready, scratch["ya"], scratch["yb"], gates2)
    right.close()
    x = K.sb(left, "x", [P, NT, D])
    merge_stage(K, [(io["p_a_2"][0], NL, ("ya", scratch["ya"])), (io["p_b_2"][0], PW // P, ("yb", scratch["yb"]))],
                scratch["gates2"], "gates2", io["w_out_2"][0], scratch["x2"], "x2", x, 2)
    K.x_done = {}

    right = ExitStack()
    hT = K.pair(right, "hT", [P, ND, S], side="right")
    ready = K.norm(x, hT, io["g_ffn_2"][0])
    with ExitStack() as ctx:
        raws = Ring([Slot(K.sb(ctx, f"up{i}", [P, S + 2])) for i in range(2)])
        conv = [Slot(K.sb(ctx, f"cv{i}", [P, S])[:, :]) for i in range(2)]
        for s in raws.slots:
            V.mark(nc.vector.memset(s.ap[:, 0:1], 0.0))
            V.wait(V.mark(nc.vector.memset(s.ap[:, S + 1:S + 2], 0.0)))
        A.wait(V.last())

        def gelu_product(j, dst, before):
            for part in range(2):
                c = part * NF2 + j
                raw, cv = raws.next(), conv[part]
                copies = []

                def evacuate(h, bank, mm):
                    A.wait(mm, *raw.busy)
                    t = A.mark(nc.scalar.activation(raw.ap[:, 1 + h * HALF:1 + (h + 1) * HALF], bank, ACT.Copy))
                    copies.append(t)
                    return [t]
                K.channel_major(hT, ready, evacuate)
                cw = lambda k: K.p_("conv_f_w_2", k * 2 * NF2 + c)
                A.wait(*copies, *cv.busy)
                t = A.mark(nc.scalar.activation(cv.ap, raw.ap[:, 0:S], ACT.Identity, scale=cw(0), bias=K.p_("conv_f_b_2", c)))
                V.wait(t)
                for k in (1, 2):
                    t = V.mark(nc.vector.scalar_tensor_tensor(cv.ap, raw.ap[:, k:k + S], cw(k), cv.ap, ALU.mult, ALU.add))
                    V.wait(t)
                raw.busy = [t]
                if part == 0:
                    A.wait(t)
                    tg = A.mark(nc.scalar.activation(cv.ap, cv.ap, ACT.Gelu_apprx_tanh))
            V.wait(t, tg)
            tm = V.mark(nc.vector.tensor_tensor(conv[0].ap, conv[0].ap, conv[1].ap, ALU.mult))
            conv[1].busy = [tm]
            d = K.split(conv[0].ap, dst[0], dst[1], [tm], before)
            conv[0].busy = d
            return d
        ffn_stage(K, x, hT, ready, NF2, gelu_product)
    K.handover()

    norm_rows(K, x, io["g_final_2"], out[0], "out", False)
    right.close()
    left.close()
    for toks in K.stored.values():
        SP.wait(*toks)
    K.stack.close()


_INS = ["x", "p", "positions", "g_mix", "w_in", "g_q_a", "w_uq", "g_kv_a", "w_ukv", "w_o_mla", "mu_rwkv", "w0", "w2",
        "a0", "a2", "g2", "k_k", "k_a", "r_k", "ln_x_w", "ln_x_b", "w_o_rwkv", "w_out", "g_ffn", "w_ffn_up",
        "w_ffn_down", "g_ple", "w_ple_gate", "w_ple_proj", "g_final", "g_mix_2", "w_in_2", "b_gate_2", "conv_a_w_2",
        "conv_a_b_2", "wa_f_2", "ba_f_2", "wx_f_2", "bx_f_2", "lam_f_2", "wa_b_2", "ba_b_2", "wx_b_2", "bx_b_2",
        "lam_b_2", "w_pool_2", "b_pool_2", "pool_scale_2", "p_a_2", "p_b_2", "w_out_2", "g_ffn_2", "w_up_2",
        "conv_f_w_2", "conv_f_b_2", "w_down_2", "g_final_2"]


def kernel(**inputs):
    import concourse.bacc as bacc
    from concourse.bass_utils import run_bass_kernel_spmd

    nc = bacc.Bacc("TRN2", target_bir_lowering=False, num_devices=1)
    arrays = {name: np.ascontiguousarray(inputs[name]) for name in _INS}
    arrays["const"] = constants()
    arrays["counts"] = pool_counts()
    feed, io = {}, {}
    for name, a in arrays.items():
        feed[f"in_{name}"] = a
        io[name] = nc.dram_tensor(f"in_{name}", a.shape, mybir.dt.from_np(a.dtype), kind="ExternalInput").ap()
    out = nc.dram_tensor("out_x", (1, S, D), F32, kind="ExternalOutput").ap()
    program(nc, io, out)
    r = run_bass_kernel_spmd(nc, [feed], core_ids=[0])
    return r.results[0]["out_x"]
```

```python
import math
from collections import namedtuple
from contextlib import ExitStack

import numpy as np
import concourse.bass as bass
from concourse import mybir

F32 = mybir.dt.float32
F32R = mybir.dt.float32r
I32 = mybir.dt.int32
ALU = mybir.AluOpType
ACT = mybir.ActivationFunctionType
AX = mybir.AxisListType

P = 128
S = 1024
D = 1024
NT = S // P
ND = D // P
HALF = 512
NHALF = S // HALF
HEADS, NOPE, ROPE, VDIM = 8, 64, 32, 64
QK = NOPE + ROPE
QRANK, KVRANK = 384, 256
NQ, NKV = QRANK // P, KVRANK // P
MLA_COLS = QRANK + KVRANK + ROPE
RDIM = 512
NR = RDIM // P
LORA, GLORA = 64, 128
RWKV_COLS = 3 * RDIM + 2 * LORA + GLORA
NZ = RWKV_COLS // P
DFF = 4 * D
PLE = 256
EPS = 1e-6
GN_EPS = 64 * 1e-5
THETA = 10000.0
CH = 128
NCH = S // CH
MID = CH // 2 - 1
LEVELS = 7
LW = 1280
NL = LW // P
PW = 1024
WINDOWS = (2, 4, 8, 16)
GDIM = PW // len(WINDOWS)
DFF2 = 2816
NF2 = DFF2 // P

TILE = 1024

Token = namedtuple("Token", "sem value")
CONST = {}
_at = 0
for _name, _n in (("ident", P), ("mask4", 4 * P), ("levels", LEVELS * P), ("causal", P), ("headsum", P),
                  ("headsel", 2), ("freq", ROPE // 2)):
    CONST[_name] = (_at, _at + _n)
    _at += _n
CONST_COLS = _at

ROW_TILES = [
    [("mu_rwkv", NZ), ("w0", NR), ("a0", NR), ("k_k", NR), ("k_a", NR), ("r_k", NR)],
    [("b_gate_2", 16), ("conv_a_w_2", 4 * NL), ("conv_a_b_2", NL), ("ba_f_2", NL), ("bx_f_2", NL),
     ("lam_f_2", NL), ("ba_b_2", NL), ("bx_b_2", NL), ("lam_b_2", NL)],
    [("b_pool_2", 8), ("pool_scale_2", 8), ("conv_f_b_2", 2 * NF2)],
    [("conv_f_w01", 4 * NF2)],
    [("conv_f_w2", 2 * NF2)],
]


def constants():
    c = np.zeros((P, CONST_COLS), np.float32)
    j, i = np.arange(P)[:, None], np.arange(P)[None, :]

    def put(name, a):
        c[:, CONST[name][0]:CONST[name][1]] = a
    put("ident", (j == i))
    strict, incl = (i > j), (i >= j)
    put("mask4", np.concatenate([strict, incl, strict, incl], 1))
    lv = []
    for l in range(LEVELS):
        b = 1 << l
        lv.append(((j // b) % 2 == 0) & (i // b == j // b + 1))
    put("levels", np.concatenate(lv, 1))
    put("causal", np.where(i <= j, 0.0, -1e30))
    put("headsum", (i // 64 == j // 64))
    put("headsel", (np.arange(2)[None, :] == j // 64))
    half = ROPE // 2
    put("freq", np.broadcast_to(
        np.float32(THETA) ** (-np.arange(half, dtype=np.float32) / np.float32(half)), (P, half)))
    return c


def pool_counts():
    t = np.arange(S)
    rows = []
    for w in WINDOWS:
        lo, hi = np.clip(t - w // 2, 0, S - 1), np.clip(t + w // 2 - 1, 0, S - 1)
        rows.append(np.float32(1.0) / (hi - lo + 1).astype(np.float32))
    return np.stack(rows).astype(np.float32)


class Engine:

    def __init__(self, queue, sem):
        self.queue, self.sem, self.count, self.seen = queue, sem, 0, {}

    def wait(self, *tokens):
        for t in tokens:
            if t is None:
                continue
            if isinstance(t, list):
                self.wait(*t)
                continue
            if self.seen.get(id(t.sem), 0) < t.value:
                self.queue.wait_ge(t.sem, t.value)
                self.seen[id(t.sem)] = t.value

    def mark(self, instruction):
        instruction.then_inc(self.sem, 1)
        self.count += 1
        return Token(self.sem, self.count)

    def last(self):
        return Token(self.sem, self.count) if self.count else None


class Slot:

    def __init__(self, ap, sem=None, lo=None):
        self.ap, self.lo, self.busy, self.sem, self.loads = ap, lo, [], sem, 0


class Ring:
    def __init__(self, slots):
        self.slots, self.at = slots, 0

    def next(self):
        s = self.slots[self.at % len(self.slots)]
        self.at += 1
        return s


class Kernel:
    def __init__(self, nc, io):
        self.nc, self.io = nc, io
        self.stack = ExitStack()
        self.names = 0
        self.PE = Engine(nc.tensor, self.semaphore("pe_done"))
        self.A = Engine(nc.scalar, self.semaphore("act_done"))
        self.V = Engine(nc.vector, self.semaphore("dve_done"))
        self.G = Engine(nc.gpsimd, self.semaphore("pool_done"))
        self.SP = Engine(nc.sync, self.semaphore("sp_done"))
        self.stored = {}

    def semaphore(self, name):
        return self.stack.enter_context(self.nc.semaphore(name))

    def sb(self, ctx, name, shape, dtype=F32, side=None):
        self.names += 1
        kw = {"side": side} if side else {}
        return ctx.enter_context(self.nc.sbuf_tensor(f"{name}_{self.names}", shape, dtype, **kw))

    def pair(self, ctx, name, shape, side=None):
        return (self.sb(ctx, name + "_hi", shape, F32R, side), self.sb(ctx, name + "_lo", shape, F32R, side))

    def load(self, slot, dst, src, queue=None, after=()):
        q = queue or self.SP
        q.wait(*slot.busy, *after)
        q.queue.dma_start(dst, src).then_inc(slot.sem, 16)
        slot.loads += 16
        return Token(slot.sem, slot.loads)

    def store(self, name, sem_slot, dst, src, queue, after=()):
        queue.wait(*after)
        queue.queue.dma_start(dst, src).then_inc(sem_slot.sem, 16)
        sem_slot.loads += 16
        t = Token(sem_slot.sem, sem_slot.loads)
        self.stored[name] = [o for o in self.stored.get(name, []) if o.sem is not sem_slot.sem] + [t]
        return t

    def handover(self):
        done = [e.last() for e in (self.PE, self.A, self.V, self.G)]
        for e in (self.A, self.V, self.G, self.SP):
            e.wait(*[t for t in done if t])

    def queue_weights(self, tiles):
        self.pending.extend(tiles)
        self.pump()

    def fetch(self, src, shape):
        s = self.staging.next()
        n = int(np.prod(shape[1:]))
        view = s.ap[:, 0:n]
        if len(shape) == 3:
            view = view.rearrange("p (k c) -> p k c", k=shape[1])
        t = self.load(s, view, src)
        s.busy = []
        return s, n, t

    def split(self, src, hi, lo, after, before, low_engine=None):
        self.A.wait(*after, *before)
        th = self.A.mark(self.nc.scalar.activation(hi, src, ACT.Copy))
        e = low_engine or self.G
        e.wait(*after, *before, th)
        tl = e.mark(e.queue.tensor_tensor(lo, src, hi.bitcast(F32), ALU.subtract))
        return [th, tl]

    def pump(self):
        while self.pending or self.fetched:
            while self.pending and len(self.fetched) < len(self.staging.slots):
                src, shape = self.pending.pop(0)
                self.fetched.append((*self.fetch(src, shape), shape))
            if not self.ring_free or not self.fetched:
                return
            stage, n, arrived, shape = self.fetched.pop(0)
            slot = self.ring_free.pop(0)
            self.low_engines.append(low := self.low_engines.pop(0))
            done = self.split(stage.ap[:, 0:n], slot.ap[:, 0:n], slot.lo[:, 0:n], [arrived], slot.busy, low)
            stage.busy = done
            self.ready.append((slot, shape, done))

    def take(self):
        self.pump()
        slot, shape, done = self.ready.pop(0)
        n = int(np.prod(shape[1:]))
        hi, lo = (x[:, 0:n].rearrange("p (k c) -> p k c", k=shape[1]) for x in (slot.ap, slot.lo))
        return slot, hi, lo, done

    def release(self, slots, token):
        for s in slots:
            s.busy = [token]
            self.ring_free.append(s)
        self.pump()

    def bank(self):
        return self.banks.next()

    def product(self, out, terms, bank=None):
        if bank is not None:
            self.PE.wait(*bank.busy)
        for n, (lhsT, rhs, after) in enumerate(terms):
            self.PE.wait(*after)
            mm = self.nc.tensor.matmul(out, lhsT, rhs, start=(n == 0), stop=(n == len(terms) - 1))
        return self.PE.mark(mm)

    @staticmethod
    def three(stat, mov, after):
        return [(stat[0], mov[0], after), (stat[0], mov[1], []), (stat[1], mov[0], [])]

    def rsqrt(self, out, total, scale, eps, tmp, after):
        nc, A, V = self.nc, self.A, self.V
        m, s, q = tmp
        V.wait(*after)
        t = V.mark(nc.vector.tensor_scalar(m, total, scale, eps, ALU.mult, ALU.add))
        A.wait(t)
        t = A.mark(nc.scalar.activation(s, m, ACT.Sqrt))
        V.wait(t)
        V.wait(V.mark(nc.vector.reciprocal(out, s)))
        V.wait(V.mark(nc.vector.tensor_tensor(q, out, out, ALU.mult)))
        V.wait(V.mark(nc.vector.tensor_tensor(q, q, m, ALU.mult)))
        V.wait(V.mark(nc.vector.tensor_scalar(q, q, -0.5, 1.5, ALU.mult, ALU.add)))
        t = V.mark(nc.vector.tensor_tensor(out, out, q, ALU.mult))
        return t

    def setup(self):
        nc, io = self.nc, self.io
        st = self.stack
        self.psum = st.enter_context(nc.psum_tensor("psum", [P, 8, HALF], F32))
        self.banks = Ring([Slot(self.psum[:, b, :]) for b in range(8)])
        self.const_load = Slot(None, self.semaphore("const_load"))
        self.ident = self.sb(st, "ident", [P, P])
        nparam = sum(n for tile in ROW_TILES for _, n in tile)
        self.param = self.sb(st, "param", [P, nparam])
        self.col = {}
        self.squares = self.sb(st, "squares", [P, 7, NT])
        self.sq_done = {}
        self.staging = Ring([Slot(self.sb(st, f"stage{i}", [P, TILE])[:, :], self.semaphore(f"stage{i}_load"))
                             for i in range(3)])
        self.pending, self.fetched, self.ready = [], [], []
        self.low_engines = [self.G]
        self.ring_free = [Slot(hi[:, :], None, lo[:, :]) for hi, lo in
                          (self.pair(st, f"weight{i}", [P, TILE]) for i in range(5))]
        arrived = self.load(self.const_load, self.ident[:, :], io["const"][:, CONST["ident"][0]:CONST["ident"][1]])
        self.PE.wait(arrived)

    def load_parameters(self, ctx):
        io = self.io
        self.row_load = Slot(None, self.semaphore("row_load"))
        self.rows = [self.sb(ctx, f"rows{n}", [P, P]) for n in range(len(ROW_TILES))]
        at = 0
        for n, tile in enumerate(ROW_TILES):
            r = 0
            for name, k in tile:
                if name == "conv_f_w01":
                    src = io["conv_f_w_2"][0, 0:2, :].rearrange("a (b p) -> (a b) p", p=P)
                elif name == "conv_f_w2":
                    src = io["conv_f_w_2"][0, 2:3, :].rearrange("a (b p) -> (a b) p", p=P)
                elif name == "conv_a_w_2":
                    src = io[name][0, :, :].rearrange("a (b p) -> (a b) p", p=P)
                elif name == "r_k":
                    src = io[name].rearrange("l h n -> (l h n)").rearrange("(b p) -> b p", p=P)
                else:
                    src = io[name].rearrange("l n -> (l n)").rearrange("(b p) -> b p", p=P)
                arrived = self.load(self.row_load, self.rows[n][r:r + k, :], src, queue=self.G)
                self.col[name] = at + r
                r += k
            at += r
        self.col["conv_f_w_2"] = self.col["conv_f_w01"]
        return arrived

    def transpose_parameters(self, arrived):
        at = 0
        for n, tile in enumerate(ROW_TILES):
            k = sum(c for _, c in tile)
            b = self.bank()
            self.PE.wait(arrived, *b.busy)
            t = self.PE.mark(self.nc.tensor.transpose(b.ap[:, 0:k], self.rows[n][0:k, :], self.ident[0:k, 0:k]))
            self.V.wait(t)
            b.busy = [self.V.mark(self.nc.vector.tensor_copy(self.param[:, at:at + k], b.ap[:, 0:k]))]
            at += k
        for e in (self.A, self.V, self.G, self.PE, self.SP):
            e.wait(*b.busy)

    def p_(self, name, i):
        c = self.col[name] + i
        return self.param[:, c:c + 1]

    def square(self, x, t, n, x_ready, junk):
        self.A.wait(*x_ready)
        tok = self.A.mark(self.nc.scalar.activation(junk, x[:, t, n * HALF:(n + 1) * HALF], ACT.Square,
                                                    accum_out=self.squares[:, n, t:t + 1]))
        self.sq_done[(t, n)] = tok
        return tok

    def rstd_of(self, ts):
        V, sq, c = self.V, self.squares, slice(ts[0], ts[-1] + 1)
        V.wait(*[self.sq_done[(t, n)] for t in ts for n in range(2)])
        tot = V.mark(self.nc.vector.tensor_tensor(sq[:, 2, c], sq[:, 0, c], sq[:, 1, c], ALU.add))
        V.wait(tot)
        return self.rsqrt(sq[:, 3, c], sq[:, 2, c], 1.0 / D, EPS, [sq[:, 4 + i, c] for i in range(3)], [tot])

    def channel_major_steps(self, hT, ready, evacuate):
        slot, hi, lo, done = self.take()
        for h in range(NHALF):
            b = self.bank()
            terms = []
            for k in range(hi.shape[1]):
                cols = slice(h * HALF, (h + 1) * HALF)
                after = [*done, *of_half(ready, h)] if k == 0 else []
                terms += self.three((hi[:, k, :], lo[:, k, :]), (hT[0][:, k, cols], hT[1][:, k, cols]), after)
            t = self.product(b.ap, terms, b)
            b.busy = evacuate(h, b.ap, t)
            if h == NHALF - 1:
                self.release([slot], t)
            yield

    def channel_major(self, hT, ready, evacuate):
        for _ in self.channel_major_steps(hT, ready, evacuate):
            pass

    def staggered(self, blocks, norm, lead=1):
        norm.advance(1)
        for n, b in enumerate(blocks):
            next(b)
            if n >= lead - 1:
                norm.advance(1)
        norm.finish()
        for b in blocks:
            for _ in b:
                pass

    def token_major(self, xT, ready, k0, nk, cols, tiles, tokens, evacuate, by_block=None):
        taken = [self.take() for _ in range(tiles)]
        for t in tokens:
            tc = slice(t * P, (t + 1) * P)
            b = self.bank()
            out = b.ap[:, 0:cols]
            self.PE.wait(*b.busy, *of_half(ready, t * P // HALF))
            k, mm = 0, None
            for slot, hi, lo, done in taken:
                self.PE.wait(*done)
                for i in range(hi.shape[1]):
                    if by_block:
                        self.PE.wait(*by_block[k])
                    x = (xT[0][:, k0 + k, tc], xT[1][:, k0 + k, tc])
                    for n, (lhsT, rhs, _) in enumerate(self.three(x, (hi[:, i, :], lo[:, i, :]), [])):
                        mm = self.nc.tensor.matmul(out, lhsT, rhs, start=(k == 0 and n == 0), stop=(k == nk - 1 and n == 2))
                    k += 1
                if t == tokens[-1]:
                    done_with = self.PE.mark(mm)
                    self.release([slot], done_with)
            b.busy = evacuate(t, out, done_with if t == tokens[-1] else self.PE.mark(mm))


NORM_STEPS = 1 + NT // NHALF


class HeadWeights:

    def __init__(self, K, ctx):
        self.K, self.loaded = K, {}
        self.slots = [Slot(K.sb(ctx, f"wqkv{i}", [P, NQ * 2 * QK + NKV * 256])[:, :], K.semaphore(f"wqkv{i}"))
                      for i in range(2)]

    def load(self, pair):
        K, s = self.K, self.slots[pair % 2]
        wq = s.ap[:, 0:NQ * 2 * QK].rearrange("p (k c) -> p k c", k=NQ)
        wkv = s.ap[:, NQ * 2 * QK:].rearrange("p (k c) -> p k c", k=NKV)
        K.load(s, wq, weight_block(K.io["w_uq"][0], pair * 2 * QK, 2 * QK)[0])
        self.loaded[pair] = wq, wkv, K.load(s, wkv, weight_block(K.io["w_ukv"][0], pair * 256, 256)[0])

    def pop(self, pair):
        if pair not in self.loaded:
            self.load(pair)
        return self.loaded.pop(pair)


class Norm:

    class Memory:

        def __init__(self, K, ctx, blocks=2):
            K.names += 1
            self.gain = Slot(K.sb(ctx, "gain", [P, D])[:, :], K.semaphore(f"norm_gain_load{K.names}"))
            self.add_blocks(K, ctx, blocks)

        def add_blocks(self, K, ctx, blocks, side=None):
            self.xn = Ring([Slot(K.sb(ctx, f"xn{i}", [P, D], side=side)[:, :]) for i in range(blocks)])

    def __init__(self, K, memory, x, hT, gain, before):
        self.K, self.x, self.hT, self.before = K, x, hT, before
        self.gain, self.memory = memory.gain, memory
        self.gain_loaded = K.load(self.gain, self.gain.ap, gain.partition_broadcast(P), queue=K.G)
        self.ready = [[], []]
        self.run = self.steps()

    def steps(self):
        K, x = self.K, self.x
        nc, A, V, PE = K.nc, K.A, K.V, K.PE

        def scaled(t):
            n = self.memory.xn.next()
            V.wait(*n.busy)
            tx = V.mark(nc.vector.scalar_tensor_tensor(n.ap, x[:, t, :], K.squares[:, 3, t:t + 1], self.gain.ap,
                                                       ALU.mult, ALU.mult))
            self.gain.busy = [tx]
            return n, tx
        for half in range(NHALF):
            ts = list(range(half * NT // 2, (half + 1) * NT // 2))
            V.wait(K.rstd_of(ts), self.gain_loaded)
            ahead = [scaled(ts[0])]
            yield
            hT = self.hT
            A.wait(*self.before[half])
            for t in ts:
                n, tx = ahead.pop()
                if t < ts[-1]:
                    ahead.append(scaled(t + 1))
                for k0 in range(0, ND, 4):
                    b = K.bank()
                    PE.wait(tx, *b.busy)
                    for k in range(4):
                        mm = nc.tensor.transpose(b.ap[:, k * P:(k + 1) * P], n.ap[:, (k0 + k) * P:(k0 + k + 1) * P],
                                                 K.ident[:, :])
                    tt = PE.mark(mm)
                    src = b.ap.rearrange("p (k c) -> p k c", k=4)
                    hi = hT[0][:, k0:k0 + 4, t * P:(t + 1) * P]
                    lo = hT[1][:, k0:k0 + 4, t * P:(t + 1) * P]
                    A.wait(tt)
                    th = A.mark(nc.scalar.activation(hi, src, ACT.Copy))
                    V.wait(th)
                    tl = V.mark(nc.vector.tensor_tensor(lo, src, hi.bitcast(F32), ALU.subtract))
                    b.busy = [tl]
                    self.ready[half] += [th, tl]
                n.busy = [tt]
                yield

    def advance(self, n):
        for _ in range(n):
            next(self.run, None)

    def finish(self):
        for _ in self.run:
            pass


def of_half(ready, h):
    return ready[h] if ready and isinstance(ready[0], list) else ready


def weight_block(w, c, width=P, k0=0, k1=None):
    v = w.rearrange("(k p) n -> p k n", p=P)
    k1 = v.shape[1] if k1 is None else k1
    return v[:, k0:k1, c:c + width], (P, k1 - k0, width)


class Gates:

    def __init__(self, K, hT, ready, bias, dram, name):
        self.K, self.hT, self.ready, self.bias, self.dram, self.name = K, hT, ready, bias, dram, name
        self.stores = [K.semaphore(f"{name}_store{i}") for i in range(2)]
        self.loads = [0] * 2
        self.done, self.limit = 0, 4 * ND
        self.blocks = [self.block(c) for c in range(2 * ND)]

    def open(self, ctx):
        self.out = Ring([Slot(self.K.sb(ctx, f"gate{i}", [P, HALF])[:, :], s) for i, s in enumerate(self.stores)])
        for s, n in zip(self.out.slots, self.loads):
            s.loads = n

    def close(self):
        K = self.K
        for s in self.out.slots:
            for e in (K.A, K.V, K.G, K.SP):
                e.wait(*s.busy)
        self.loads = [s.loads for s in self.out.slots]

    def block(self, c):
        K, A = self.K, self.K.A

        def evacuate(h, bank, mm):
            s = self.out.next()
            A.wait(mm, *s.busy)
            kw = {"bias": self.bias(c)} if self.bias else {}
            t = A.mark(K.nc.scalar.activation(s.ap, bank, ACT.Sigmoid, **kw))
            s.busy = [K.store(self.name, s, self.dram[c, :, h * HALF:(h + 1) * HALF], s.ap, A, [t])]
            return [t]
        return K.channel_major_steps(self.hT, self.ready, evacuate)

    def fill(self, n):
        while n and self.blocks and self.done < self.limit:
            if next(self.blocks[0], "end") == "end":
                self.blocks.pop(0)
            else:
                n -= 1
                self.done += 1


def rwkv_stage(K, hT, ready, yT_dram, gates):
    nc, io, A, V, G, PE = K.nc, K.io, K.A, K.V, K.G, K.PE
    ctx = ExitStack()
    v_, g_, s_ = nc.vector, nc.gpsimd, nc.scalar
    w = io["w_in"][0]
    col0 = MLA_COLS
    ld = Slot(None, K.semaphore("rwkv_load"))
    lora_w = K.sb(ctx, "lora_w", [P, RDIM])
    g2 = K.sb(ctx, "g2", [P, RDIM])
    mask4 = K.sb(ctx, "mask4", [P, 4 * P])
    levels = K.sb(ctx, "levels", [P, LEVELS, P])
    headsum = K.sb(ctx, "headsum", [P, P])
    headsel = K.sb(ctx, "headsel", [P, 2])
    cst = io["const"]
    c_ = lambda n: cst[:, CONST[n][0]:CONST[n][1]]
    for dst, src in ((lora_w[0:LORA, :], io["w2"][0]), (lora_w[LORA:P, :], io["a2"][0]), (g2[:, :], io["g2"][0]),
                     (mask4[:, :], c_("mask4")), (levels[:, :, :], c_("levels").rearrange("p (l c) -> p l c", l=LEVELS)),
                     (headsum[:, :], c_("headsum")), (headsel[:, :], c_("headsel"))):
        small = K.load(ld, dst, src)
    lora = K.sb(ctx, "lora", [P, S])
    sig_g = K.sb(ctx, "sig_g", [P, S])

    class Shift:
        busy = []

    def shifted(zraw, z, c, out_busy, between=lambda: None):
        V.wait(*Shift.busy)
        tz = V.mark(v_.memset(zraw[:, 0:1], 0.0))
        copies = []

        def evacuate(h, bank, mm):
            A.wait(mm, *Shift.busy)
            t = A.mark(s_.activation(zraw[:, 1 + h * HALF:1 + (h + 1) * HALF], bank, ACT.Copy))
            copies.append(t)
            return [t]
        for _ in K.channel_major_steps(hT, ready, evacuate):
            between()
        V.wait(tz, *copies, *out_busy)
        t = V.mark(v_.tensor_tensor(z, zraw[:, 0:S], zraw[:, 1:S + 1], ALU.subtract))
        V.wait(t)
        t = V.mark(v_.scalar_tensor_tensor(z, z, K.p_("mu_rwkv", c), zraw[:, 1:S + 1], ALU.mult, ALU.add))
        Shift.busy = [t]
        return t

    with ExitStack() as c2:
        zraw = K.sb(c2, "zraw", [P, S + 1])
        t = shifted(zraw, lora[:, :], 12, [])
        A.wait(t)
        lora_ready = A.mark(s_.activation(lora[0:LORA, :], lora[0:LORA, :], ACT.Tanh))
        t = shifted(zraw, sig_g[:, :], 13, [])
        A.wait(t)
        sig_ready = A.mark(s_.activation(sig_g[:, :], sig_g[:, :], ACT.Sigmoid))
        K.handover()
    for e in (PE, V, G):
        e.wait(small, lora_ready, sig_ready)

    hd = lambda h: slice(h * 64, (h + 1) * 64)
    AR = K.sb(ctx, "AR", [P, NCH, 2, CH])
    Bt = K.sb(ctx, "Bt", [P, NCH, CH])
    Kt = K.sb(ctx, "Kt", [P, NCH, CH])
    tok = K.sb(ctx, "tok", [P, 4, NCH, P])
    gain = K.sb(ctx, "gain", [P, NCH])
    bonus = K.sb(ctx, "bonus", [P, 2 * NCH])
    state = K.sb(ctx, "state", [P, NCH + 1, 64])
    Y = K.sb(ctx, "Y", [P, NCH, 2, 64])
    y_sem = Slot(None, K.semaphore("y_store"))
    ln_load = Slot(None, K.semaphore("ln_load"))

    def finish(blk, c3, y_done):
        sq = K.sb(c3, "sq", [P, 2 * NCH, 64])
        stat = K.sb(c3, "stat", [P, 6, 2 * NCH])
        yb = K.sb(c3, "yb", [P, S])
        lnw = K.sb(c3, "lnw", [P, P])
        lnb = K.sb(c3, "lnb", [P, P])
        K.load(ln_load, lnw[:, :], io["ln_x_w"][0, blk * P:(blk + 1) * P].partition_broadcast(P))
        ln_done = K.load(ln_load, lnb[:, :], io["ln_x_b"][0, blk * P:(blk + 1) * P].partition_broadcast(P))
        Yh = Y[:, :, :, :].rearrange("p c h k -> p (c h) k")
        bc = lambda x: x.unsqueeze(2).broadcast_to([P, 2 * NCH, 64])
        V.wait(*y_done)
        V.wait(V.mark(v_.tensor_reduce(stat[:, 0, :], Yh, AX.X, ALU.add)))
        V.wait(V.mark(v_.tensor_scalar(stat[:, 0, :], stat[:, 0, :], 1.0 / 64, None, ALU.mult)))
        V.wait(V.mark(v_.tensor_tensor(Yh, Yh, bc(stat[:, 0, :]), ALU.subtract)))
        yield
        V.wait(V.mark(v_.tensor_tensor(sq[:, :, :], Yh, Yh, ALU.mult)))
        t = V.mark(v_.tensor_reduce(stat[:, 1, :], sq[:, :, :], AX.X, ALU.add))
        t = K.rsqrt(stat[:, 2, :], stat[:, 1, :], 1.0 / 64, GN_EPS, [stat[:, 3 + i, :] for i in range(3)], [t])
        V.wait(t)
        V.wait(V.mark(v_.tensor_tensor(Yh, Yh, bc(stat[:, 2, :]), ALU.mult)))
        V.wait(ln_done)
        Yc = Y[:, :, :, :].rearrange("p c h k -> p c (h k)")
        lb = lambda x: x[:, :].unsqueeze(1).broadcast_to([P, NCH, P])
        V.wait(V.mark(v_.tensor_tensor(Yc, Yc, lb(lnw), ALU.mult)))
        V.mark(v_.tensor_tensor(Yc, Yc, lb(lnb), ALU.add))
        V.wait(V.mark(v_.tensor_tensor(sq[:, :, :], tok[:, 3, :, :].rearrange("p c (h k) -> p (c h) k", h=2),
                                       bc(bonus[:, :]), ALU.mult)))
        V.wait(V.mark(v_.tensor_tensor(Yh, Yh, sq[:, :, :], ALU.add)))
        yield
        gated = []
        for c0 in range(0, NCH, 4):
            b = K.bank()
            PE.wait(*b.busy)
            for c in range(4):
                mm = nc.tensor.matmul(b.ap[:, c * P:(c + 1) * P], sig_g[:, (c0 + c) * CH:(c0 + c + 1) * CH],
                                      g2[:, blk * P:(blk + 1) * P], start=True, stop=True)
            mm = PE.mark(mm)
            V.wait(mm)
            ty = V.mark(v_.tensor_tensor(Yc[:, c0:c0 + 4, :], Yc[:, c0:c0 + 4, :],
                                         b.ap.rearrange("p (c t) -> p c t", c=4), ALU.mult))
            b.busy = [ty]
            gated.append(ty)
        yield
        for c0, ty in zip(range(0, NCH, 4), gated):
            b = K.bank()
            PE.wait(ty, *b.busy)
            for c in range(4):
                mm = nc.tensor.transpose(b.ap[:, c * P:(c + 1) * P], Yc[:, c0 + c, :], K.ident[:, :])
            mm = PE.mark(mm)
            A.wait(mm)
            t = A.mark(s_.activation(yb[:, c0 * P:(c0 + 4) * P], b.ap, ACT.Copy))
            b.busy = [t]
        t = K.store("yT", y_sem, yT_dram[blk], yb[:, :], A, [t])
        for e in (A, V, G, K.SP):
            e.wait(t)

    last_y = None
    for blk in range(NR):
        with ExitStack() as c2:
            zraw = K.sb(c2, "zraw", [P, S + 1])
            k = K.sb(c2, "k", [P, S])
            v = K.sb(c2, "v", [P, S])
            tmp = K.sb(c2, "tmp", [P, S])
            rT = AR[:, :, 1, :]
            ck = lambda x: x[:, :].rearrange("p (c t) -> p c t", c=NCH)
            with ExitStack() as c3:
                rest = finish(blk - 1, c3, last_y) if blk else iter(())
                between = lambda: next(rest, None)
                between()
                tr = shifted(zraw, tmp[:, :], blk, [], between)
                A.wait(tr)
                tr = A.mark(s_.activation(rT, ck(tmp), ACT.Copy))
                tk = shifted(zraw, k[:, :], NR + blk, [], between)
                tv = shifted(zraw, v[:, :], 2 * NR + blk, [], between)
                for _ in rest:
                    pass
                K.handover()
            a = K.sb(c2, "a", [P, S])
            kk = K.sb(c2, "kk", [P, S])
            Pd = K.sb(c2, "Pd", [P, NCH, CH + 1])
            zero = K.sb(c2, "zero", [P, CH])
            gates.open(c2)
            gates.limit = 2 * sum(RWKV_GATES[:blk + 1]) - (GATES_LAST if blk == NR - 1 else 0)
            rmid = K.sb(c2, "rmid", [P, NCH])
            pmid = K.sb(c2, "pmid", [P, NCH])
            t0 = V.mark(v_.memset(zero[:, :], 0.0))
            sg = []
            for h in range(NHALF):
                cs = slice(h * HALF, (h + 1) * HALF)
                b = K.bank()
                mm = K.product(b.ap, [(lora_w[0:LORA, blk * P:(blk + 1) * P], lora[0:LORA, cs], [])], b)
                A.wait(mm, tr)
                t = A.mark(s_.activation(tmp[:, cs], b.ap, ACT.Sigmoid, bias=K.p_("w0", blk)))
                b.busy = [t]
                sg.append(t)
                b = K.bank()
                mm = K.product(b.ap, [(lora_w[LORA:P, blk * P:(blk + 1) * P], lora[LORA:P, cs], [])], b)
                A.wait(mm)
                t = A.mark(s_.activation(a[:, cs], b.ap, ACT.Sigmoid, bias=K.p_("a0", blk)))
                b.busy = [t]
                sg.append(t)
            A.wait(*sg)
            td = A.mark(s_.activation(tmp[:, :], tmp[:, :], ACT.Exp, scale=-math.exp(-0.5)))
            A.wait(tk)
            t = tkk = A.mark(s_.activation(kk[:, :], k[:, :], ACT.Identity, scale=K.p_("k_k", blk)))
            gates.fill(3)
            V.wait(td, t0)
            for c in range(NCH):
                tp = V.mark(v_.tensor_tensor_scan(Pd[:, c, 1:CH + 1], tmp[:, c * CH:(c + 1) * CH], zero[:, :], 1.0,
                                                  ALU.mult, ALU.add))
            V.wait(tp)
            V.mark(v_.tensor_copy(pmid[:, :], Pd[:, :, 1 + MID]))
            t2 = V.mark(v_.reciprocal(rmid[:, :], Pd[:, :, 1 + MID]))
            V.wait(t2)
            t2 = V.mark(v_.tensor_copy(Pd[:, :, 0], rmid[:, :]))
            A.wait(t2)
            for c in range(NCH):
                tp = A.mark(s_.activation(Pd[:, c, 1:CH + 1], Pd[:, c, 1:CH + 1], ACT.Identity, scale=rmid[:, c:c + 1]))
            G.wait(t)
            t = G.mark(g_.tensor_tensor(zraw[:, 0:S], kk[:, :], kk[:, :], ALU.mult))
            nn = []
            for h in range(NHALF):
                cs = slice(h * HALF, (h + 1) * HALF)
                b = K.bank()
                mm = K.product(b.ap, [(headsum[:, :], zraw[:, cs], [t])], b)
                V.wait(mm)
                t3 = V.mark(v_.tensor_scalar(b.ap, b.ap, 1e-24, None, ALU.max))
                A.wait(t3)
                t3 = A.mark(s_.activation(b.ap, b.ap, ACT.Sqrt))
                V.wait(t3, mm)
                t3 = V.mark(v_.reciprocal(b.ap, b.ap))
                V.wait(t3, tkk)
                t3 = V.mark(v_.tensor_tensor(kk[:, cs], kk[:, cs], b.ap, ALU.mult))
                b.busy = [t3]
                nn.append(t3)
                gates.fill(1 + h * 1)
            V.wait(tp)
            V.mark(v_.tensor_tensor(gain[:, 0:NCH - 1], Pd[:, 0:NCH - 1, CH], pmid[:, 1:NCH], ALU.mult))
            V.wait(*nn, *sg)
            V.wait(V.mark(v_.tensor_scalar(tmp[:, :], a[:, :], 1.0, K.p_("k_a", blk), ALU.subtract, ALU.mult)))
            tk = V.mark(v_.scalar_tensor_tensor(k[:, :], tmp[:, :], 1.0, k[:, :], ALU.add, ALU.mult))
            V.wait(tk)
            V.wait(tr, t)
            t = V.mark(v_.scalar_tensor_tensor(ck(tmp), rT, K.p_("r_k", blk), ck(k), ALU.mult, ALU.mult))
            b = K.bank()
            PE.wait(t, *b.busy)
            for c in range(NCH):
                mm = nc.tensor.matmul(b.ap[:, 2 * c:2 * c + 2], tmp[:, c * CH:(c + 1) * CH], headsel[:, :],
                                      start=True, stop=True)
            mm = PE.mark(mm)
            V.wait(mm)
            b.busy = [V.mark(v_.tensor_copy(bonus[:, :], b.ap[:, 0:2 * NCH]))]
            gates.fill(1)
            G.wait(t, tp)
            G.mark(g_.tensor_tensor(rT, rT, Pd[:, :, 1:CH + 1], ALU.mult))
            V.wait(V.mark(v_.scalar_tensor_tensor(AR[:, :, 0, :], ck(kk), -1.0, Pd[:, :, 0:CH], ALU.mult, ALU.mult)))
            t = V.mark(v_.reciprocal(ck(tmp), Pd[:, :, 1:CH + 1]))
            G.wait(V.last())
            G.wait(G.mark(g_.tensor_tensor(a[:, :], a[:, :], kk[:, :], ALU.mult)))
            G.mark(g_.tensor_tensor(Bt[:, :, :], ck(a), ck(tmp), ALU.mult))
            V.wait(t)
            V.mark(v_.tensor_tensor(Kt[:, :, :], ck(k), ck(tmp), ALU.mult))
            elem = [V.last(), G.last()]
            gates.fill(gates.limit - gates.done)
            PE.wait(*elem, tv)
            for n, src in enumerate((AR[:, :, 0, :], Bt[:, :, :], Kt[:, :, :], ck(v))):
                for c0 in range(0, NCH, 4):
                    b = K.bank()
                    PE.wait(*b.busy)
                    for c in range(4):
                        mm = nc.tensor.transpose(b.ap[:, c * P:(c + 1) * P], src[:, c0 + c, :], K.ident[:, :])
                    mm = PE.mark(mm)
                    A.wait(mm)
                    tt = A.mark(s_.activation(tok[:, n, c0:c0 + 4, :], b.ap.rearrange("p (c t) -> p c t", c=4), ACT.Copy))
                    b.busy = [tt]
            gates.close()
            K.handover()
        with ExitStack() as c2:
            cb = ExitStack()
            bufs = [[K.sb(cb, f"m4_{i}", [P, 4, 4 * P])] + [K.sb(cb, f"{n}{i}", [P, 4, P]) for n in ("T", "TT", "Wm", "Al")]
                    for i in range(2)]
            V.mark(v_.memset(state[:, 0, :], 0.0))
            chain = {"state": [V.last()], "y": []}
            busy = [[], []]

            def batch(n, side):
                m4, T, TT, Wm, Al = bufs[side]
                tiles = [(q, 2 * n + q // 2, q % 2) for q in range(4)]
                flat = lambda x: x[:, :, :].rearrange("p q c -> p (q c)")
                ev = []
                for q, c, h in tiles:
                    b = K.bank()
                    PE.wait(*b.busy)
                    rhs = AR[hd(h), c, :, :]
                    nc.tensor.matmul(b.ap[:, 0:2 * P], Bt[hd(h), c, :], rhs, start=True, stop=True)
                    mm = PE.mark(nc.tensor.matmul(b.ap[:, 2 * P:4 * P], Kt[hd(h), c, :], rhs, start=True, stop=True))
                    V.wait(mm, *busy[side])
                    t = V.mark(v_.tensor_tensor(m4[:, q, :], b.ap, mask4[:, :], ALU.mult))
                    b.busy = [t]
                    ev.append(t)
                    yield
                G.wait(*ev, *busy[side])
                lv = lambda l: levels[:, l, :].unsqueeze(1).broadcast_to([P, 4, P])
                t = G.mark(g_.tensor_tensor(Al[:, :, :], m4[:, :, 0:P], lv(0), ALU.mult))
                V.wait(t)
                tTT = V.mark(v_.tensor_tensor(TT[:, :, :], Al[:, :, :], K.ident[:, :].unsqueeze(1).broadcast_to([P, 4, P]), ALU.add))
                b = K.bank()
                PE.wait(tTT, *b.busy)
                for q in range(4):
                    mm = nc.tensor.transpose(b.ap[:, q * P:(q + 1) * P], TT[:, q, :], K.ident[:, :])
                mm = PE.mark(mm)
                A.wait(mm, *busy[side])
                tT = A.mark(s_.activation(flat(T), b.ap, ACT.Copy))
                b.busy = [tT]
                read_Al = [tTT]
                yield
                for l in range(1, LEVELS):
                    G.wait(*read_Al)
                    tA = G.mark(g_.tensor_tensor(Al[:, :, :], m4[:, :, 0:P], lv(l), ALU.mult))
                    b = K.bank()
                    PE.wait(tA, tT, *b.busy)
                    for q in range(4):
                        mm = nc.tensor.matmul(b.ap[:, q * P:(q + 1) * P], Al[:, q, :], T[:, q, :], start=True, stop=True)
                    mm = PE.mark(mm)
                    read_Al = [mm]
                    A.wait(mm)
                    tW = A.mark(s_.activation(flat(Wm), b.ap, ACT.Copy))
                    b.busy = [tW]
                    yield
                    PE.wait(tW, tTT)
                    b2 = K.bank()
                    PE.wait(*b2.busy)
                    for q in range(4):
                        m2 = nc.tensor.matmul(b2.ap[:, q * P:(q + 1) * P], Wm[:, q, :], TT[:, q, :], start=True, stop=True)
                    m2 = PE.mark(m2)
                    if l < LEVELS - 1:
                        b1 = K.bank()
                        PE.wait(*b1.busy)
                        for q in range(4):
                            m1 = nc.tensor.matmul(b1.ap[:, q * P:(q + 1) * P], TT[:, q, :], Wm[:, q, :], start=True, stop=True)
                        m1 = PE.mark(m1)
                        V.wait(m1)
                        tT = V.mark(v_.tensor_tensor(flat(T), flat(T), b1.ap, ALU.add))
                        b1.busy = [tT]
                    V.wait(m2, m1)
                    tTT = V.mark(v_.tensor_tensor(flat(TT), flat(TT), b2.ap, ALU.add))
                    b2.busy = [tTT]
                    yield
                b = K.bank()
                PE.wait(*b.busy)
                for q, c, h in tiles:
                    mm = nc.tensor.matmul(b.ap[:, q * 64:(q + 1) * 64], m4[:, q, 2 * P:3 * P], tok[:, 3, c, hd(h)],
                                          start=True, stop=True)
                mm = PE.mark(mm)
                A.wait(mm, tT)
                A.mark(s_.activation(T[:, :, 64:128], b.ap[:, 0:256].rearrange("p (q c) -> p q c", q=4), ACT.Copy))
                A.mark(s_.activation(T[:, :, 0:64].rearrange("p (c h) k -> p c h k", c=2),
                                     tok[:, 0, 2 * n:2 * n + 2, :].rearrange("p c (h k) -> p c h k", h=2), ACT.Copy))
                tX = A.last()
                b.busy = [tX]
                yield
                b = K.bank()
                PE.wait(tX, tTT, *b.busy)
                for q in range(4):
                    mm = nc.tensor.matmul(b.ap[:, q * P:(q + 1) * P], TT[:, q, :], T[:, q, :], start=True, stop=True)
                mm = PE.mark(mm)
                A.wait(mm)
                tW = A.mark(s_.activation(flat(Wm), b.ap, ACT.Copy))
                b.busy = [tW]
                yield
                bR, bM = K.bank(), K.bank()
                PE.wait(tW, *bR.busy, *bM.busy)
                for q, c, h in tiles:
                    nc.tensor.matmul(bR.ap[hd(h), (q // 2) * P:(q // 2 + 1) * P], Wm[:, q, 0:64], m4[:, q, P:2 * P],
                                     start=True, stop=True)
                for q, c, h in tiles:
                    o = (q // 2) * P
                    nc.tensor.matmul(bM.ap[hd(h), o:o + 64], Wm[:, q, 0:64], tok[:, 1, c, hd(h)], start=True, stop=True)
                for q, c, h in tiles:
                    o = (q // 2) * P + 64
                    nc.tensor.matmul(bM.ap[hd(h), o:o + 64], tok[:, 1, c, hd(h)], Wm[:, q, 64:128], start=True, stop=False)
                    mm = nc.tensor.matmul(bM.ap[hd(h), o:o + 64], tok[:, 2, c, hd(h)], tok[:, 3, c, hd(h)],
                                          start=False, stop=True)
                mm = PE.mark(mm)
                V.wait(mm)
                rh = TT[:, 0:2, :]
                V.mark(v_.tensor_tensor(rh, bR.ap[:, 0:2 * P].rearrange("p (c t) -> p c t", c=2),
                                        AR[:, 2 * n:2 * n + 2, 1, :], ALU.add))
                bR.busy = [V.last()]
                MT = TT[:, 2, :].rearrange("p (c k) -> p c k", c=2)
                for h in range(2):
                    V.mark(v_.tensor_tensor(MT[hd(h), :, :], bM.ap[hd(h), 0:2 * P].rearrange("p (c k) -> p c k", c=2)[:, :, 0:64],
                                            K.ident[hd(h), hd(h)].unsqueeze(1).broadcast_to([64, 2, 64]), ALU.add))
                gN = TT[:, 3, :].rearrange("p (c k) -> p c k", c=2)
                for i in range(2):
                    c = 2 * n + i
                    if c < NCH - 1:
                        V.mark(v_.tensor_scalar(gN[:, i, :], bM.ap[:, i * P + 64:(i + 1) * P], gain[:, c:c + 1], None, ALU.mult))
                bM.busy = [V.last()]
                ready_M = V.last()
                yield
                for i in range(2):
                    c = 2 * n + i
                    PE.wait(ready_M, *chain["state"])
                    if c < NCH - 1:
                        b = K.bank()
                        PE.wait(*b.busy)
                        for h in range(2):
                            mm = nc.tensor.matmul(b.ap[hd(h), 0:64], MT[hd(h), i, :], state[hd(h), c, :], start=True, stop=True)
                        mm = PE.mark(mm)
                        V.wait(mm)
                        t = V.mark(v_.scalar_tensor_tensor(state[:, c + 1, :], b.ap[:, 0:64], gain[:, c:c + 1], gN[:, i, :],
                                                           ALU.mult, ALU.add))
                        b.busy = [t]
                        chain["state"] = [t]
                    done = []
                    for h in range(2):
                        q = 2 * i + h
                        b = K.bank()
                        PE.wait(*b.busy)
                        o = b.ap[:, 0:64]
                        nc.tensor.matmul(o, TT[hd(h), i, :], state[hd(h), c, :], start=True, stop=False)
                        nc.tensor.matmul(o, m4[:, q, 3 * P:4 * P], tok[:, 3, c, hd(h)], start=False, stop=False)
                        mm = PE.mark(nc.tensor.matmul(o, m4[:, q, P:2 * P], Wm[:, q, 64:128], start=False, stop=True))
                        A.wait(mm)
                        t = A.mark(s_.activation(Y[:, c, h, :], o, ACT.Copy))
                        b.busy = [t]
                    chain["y"].append(t)
                    busy[side] = [mm, t, *chain["state"]]

            for n0 in (0, 2):
                running = [batch(n0, 0), batch(n0 + 1, 1)]
                while running:
                    running = [g for g in running if next(g, "end") != "end"]
            K.handover()
            cb.close()
        last_y = chain["y"]
    with ExitStack() as c3:
        gates.open(c3)
        gates.limit += GATES_LAST
        for _ in finish(NR - 1, c3, last_y):
            gates.fill(1)
        gates.fill(GATES_LAST)
        gates.close()
        K.handover()
    ctx.close()


def compressed_stage(K, hT, ready, cT, kpe, between):
    nc, io, A, V, G, PE = K.nc, K.io, K.A, K.V, K.G, K.PE
    with ExitStack() as ctx:
        gl = Slot(None, K.semaphore("gqkv"))
        g = K.sb(ctx, "g", [P, QRANK + KVRANK])
        K.load(gl, g[:, 0:QRANK], io["g_q_a"][0].partition_broadcast(P))
        gt = K.load(gl, g[:, QRANK:], io["g_kv_a"][0].partition_broadcast(P))
        junk = K.sb(ctx, "junk", [P, QRANK])
        made = []
        for tiles, width, rank, c0, g0 in ((4, QRANK, QRANK, 0, 0), (3, KVRANK + ROPE, KVRANK, NQ, QRANK)):
            z = K.sb(ctx, "z", [P, NT, rank])
            stat = K.sb(ctx, "stat", [P, 5, NT])
            marks = []

            def evacuate(t, bank, mm):
                A.wait(mm, *marks[-1:])
                if rank == KVRANK:
                    A.mark(nc.scalar.activation(kpe[:, t, :], bank[:, rank:width], ACT.Copy))
                A.mark(nc.scalar.activation(z[:, t, :], bank[:, 0:rank], ACT.Copy))
                last = A.mark(nc.scalar.activation(junk[:, 0:rank], bank[:, 0:rank], ACT.Square, accum_out=stat[:, 0, t:t + 1]))
                marks.append(last)
                return [last]
            K.token_major(hT, ready, 0, ND, width, tiles, range(NT), evacuate)
            tr = K.rsqrt(stat[:, 1, :], stat[:, 0, :], 1.0 / rank, EPS, [stat[:, 2 + i, :] for i in range(3)], marks)
            V.wait(tr, gt)
            scaled = []
            for t in range(NT):
                scaled.append(V.mark(nc.vector.scalar_tensor_tensor(z[:, t, :], z[:, t, :], stat[:, 1, t:t + 1],
                                                                    g[:, g0:g0 + rank], ALU.mult, ALU.mult)))
            made.append((z, rank, c0, scaled))
            if len(made) == 1:
                between()
        for z, rank, c0, scaled in made:
            for t0 in range(0, NT, 4):
                for c in range(rank // P):
                    b = K.bank()
                    PE.wait(scaled[t0 + 3], *b.busy)
                    for t in range(4):
                        mm = nc.tensor.transpose(b.ap[:, t * P:(t + 1) * P], z[:, t0 + t, c * P:(c + 1) * P], K.ident[:, :])
                    mm = PE.mark(mm)
                    A.wait(mm)
                    tc = A.mark(nc.scalar.activation(cT[:, c0 + c, t0 * P:(t0 + 4) * P], b.ap, ACT.Copy))
                    b.busy = [tc]
        K.handover()
    return tc


def angles(K, cs, causal):
    nc, io, A, V = K.nc, K.io, K.A, K.V
    half = ROPE // 2
    ctx = ExitStack()
    ld = Slot(None, K.semaphore("pos_load"))
    pos = K.sb(ctx, "pos", [NT, P], I32)
    posr = K.sb(ctx, "posr", [NT, P])
    posf = K.sb(ctx, "posf", [P, NT])
    freq = K.sb(ctx, "freq", [P, half])
    ang = K.sb(ctx, "ang", [P, NT, half])
    n = K.sb(ctx, "n", [P, NT, half])
    ni = K.sb(ctx, "ni", [P, NT, half], I32)
    K.load(ld, causal[:, :], io["const"][:, CONST["causal"][0]:CONST["causal"][1]])
    K.load(ld, pos[:, :], io["positions"].rearrange("b (t p) -> (b t) p", p=P))
    t = K.load(ld, freq[:, :], io["const"][:, CONST["freq"][0]:CONST["freq"][1]])
    V.wait(t)
    t = V.mark(nc.vector.tensor_copy(posr[:, :], pos[:, :]))
    b = K.bank()
    K.PE.wait(t, *b.busy)
    t = K.PE.mark(nc.tensor.transpose(b.ap[:, 0:NT], posr[:, :], K.ident[0:NT, 0:NT]))
    V.wait(t)
    b.busy = [V.mark(nc.vector.tensor_copy(posf[:, :], b.ap[:, 0:NT]))]
    V.wait(*b.busy)
    V.wait(V.mark(nc.vector.tensor_tensor(ang[:, :, :], posf[:, :].unsqueeze(2).broadcast_to([P, NT, half]),
                                          freq[:, :].unsqueeze(1).broadcast_to([P, NT, half]), ALU.mult)))
    p1 = 6.28125
    p2 = round((2 * math.pi - p1) * 2 ** 22) / 2 ** 22
    p3 = float(np.float32(2 * math.pi - p1 - p2))
    for i, (shift, add) in enumerate(((0.25, math.pi / 2), (0.0, 0.0))):
        r = cs[:, i, :, :]
        V.wait(V.mark(nc.vector.tensor_scalar(n[:, :, :], ang[:, :, :], 1 / (2 * math.pi), shift, ALU.mult, ALU.add)))
        V.wait(V.mark(nc.vector.tensor_copy(ni[:, :, :], n[:, :, :])))
        V.wait(V.mark(nc.vector.tensor_copy(n[:, :, :], ni[:, :, :])))
        V.wait(V.mark(nc.vector.scalar_tensor_tensor(r, n[:, :, :], -p1, ang[:, :, :], ALU.mult, ALU.add)))
        V.wait(V.mark(nc.vector.scalar_tensor_tensor(r, n[:, :, :], -p2, r, ALU.mult, ALU.add)))
        V.wait(V.mark(nc.vector.scalar_tensor_tensor(r, n[:, :, :], -p3, r, ALU.mult, ALU.add)))
        V.wait(V.mark(nc.vector.tensor_scalar(r, r, add, 3.1415925, ALU.add, ALU.min)))
        t = V.mark(nc.vector.tensor_scalar(r, r, -3.1415925, None, ALU.max))
        A.wait(t)
        t = A.mark(nc.scalar.activation(r, r, ACT.Sin))
    for e in (V, K.G, K.SP):
        e.wait(t)
    ctx.close()



def rope(K, x, cs, tmp, heads, after):
    nc, V = K.nc, K.V
    half = ROPE // 2
    x1, x2 = x[:, :, :, 0:half], x[:, :, :, half:ROPE]
    c, s = (cs[:, i, :, :].unsqueeze(2).broadcast_to([P, NT, heads, half]) for i in range(2))
    t4 = [tmp[:, i, 0:NT * heads * half].rearrange("p (t h k) -> p t h k", t=NT, h=heads) for i in range(4)]
    V.wait(*after)
    V.mark(nc.vector.tensor_tensor(t4[0], x1, c, ALU.mult))
    V.mark(nc.vector.tensor_tensor(t4[1], x2, s, ALU.mult))
    V.mark(nc.vector.tensor_tensor(t4[2], x2, c, ALU.mult))
    V.wait(V.mark(nc.vector.tensor_tensor(t4[3], x1, s, ALU.mult)))
    V.mark(nc.vector.tensor_tensor(x1, t4[0], t4[1], ALU.subtract))
    t = V.mark(nc.vector.tensor_tensor(x2, t4[2], t4[3], ALU.add))
    V.wait(t)
    return t


QB_ORDER = (7, 0, 6, 1, 5, 2, 4, 3)
TURN_LAG, OUT_LAG = 2, 1


def attention_stage(K, cT, c_ready, kpe, cs, causal, weights, oT):
    nc, io, A, V, G, PE = K.nc, K.io, K.A, K.V, K.G, K.PE
    ctx = ExitStack()
    tmp = K.sb(ctx, "ropetmp", [P, 4, NT * 2 * 16])
    kp4 = kpe[:, :, :].unsqueeze(2)
    kpe_ready = rope(K, kp4, cs, tmp, 1, [c_ready, A.last()])
    scale = QK ** -0.5

    class Pair:
        pass
    sets = []
    for i in range(2):
        s = Pair()
        s.w = weights.slots[i]
        s.qT = K.sb(ctx, f"qT{i}", [P, 2, S])
        s.kT = K.sb(ctx, f"kT{i}", [P, 2, S])
        s.v = K.sb(ctx, f"v{i}", [P, NT, 2, VDIM])
        s.busy = []
        sets.append(s)
    qtok = K.sb(ctx, "qtok", [P, NT, 2, QK])
    ktok = K.sb(ctx, "ktok", [P, NT, 2, QK])
    otok = K.sb(ctx, "otok", [P, NT, P])
    Pm = Ring([Slot(K.sb(ctx, f"P{i}", [P, S])[:, :]) for i in range(4)])
    PT = Ring([Slot(K.sb(ctx, f"PT{i}", [P, NT, P])[:, :, :]) for i in range(3)])
    st = K.sb(ctx, "st", [P, 4, HEADS * NT])
    bank = [s for s in K.banks.slots]
    long, short = Slot(K.psum[:, 0:2, :].rearrange("p b c -> p (b c)")), bank[2]
    long.busy = [*bank[0].busy, *bank[1].busy]
    work = Ring(bank[3:7])
    tok_busy = {"q": [], "k": [], "o": []}

    def project(pair):
        s = sets[pair % 2]
        wq, wkv, t0 = weights.pop(pair)
        tq, tk = [], []
        for t in range(NT):
            tc = slice(t * P, (t + 1) * P)
            b = work.next()
            mm = K.product(b.ap[:, 0:2 * QK], [(cT[:, k, tc], wq[:, k, :], [t0, c_ready]) for k in range(NQ)], b)
            A.wait(mm, *tok_busy["q"])
            x = A.mark(nc.scalar.activation(qtok[:, t, :, :], b.ap[:, 0:2 * QK].rearrange("p (h k) -> p h k", h=2), ACT.Copy))
            b.busy = [x]
            tq.append(x)
            yield
        for t in range(NT):
            tc = slice(t * P, (t + 1) * P)
            b = work.next()
            mm = K.product(b.ap[:, 0:256], [(cT[:, NQ + k, tc], wkv[:, k, :], []) for k in range(NKV)], b)
            A.wait(mm, *tok_busy["k"], *s.busy)
            src = b.ap[:, 0:256].rearrange("p (h c) -> p h c", h=2)
            A.mark(nc.scalar.activation(ktok[:, t, :, 0:NOPE], src[:, :, 0:NOPE], ACT.Copy))
            x = A.mark(nc.scalar.activation(s.v[:, t, :, :], src[:, :, NOPE:], ACT.Copy))
            b.busy = [x]
            tk.append(x)
            yield
        s.w.busy = [mm]
        tr = rope(K, qtok[:, :, :, NOPE:QK], cs, tmp, 2, tq)
        V.wait(kpe_ready, *tok_busy["k"])
        x = V.mark(nc.vector.tensor_copy(ktok[:, :, :, NOPE:QK], kpe[:, :, :].unsqueeze(2).broadcast_to([P, NT, 2, ROPE])))
        yield
        done = [tk[-1]]
        for name, src, dst, after in (("q", qtok, s.qT, [tr, *tq]), ("k", ktok, s.kT, [x, *tk])):
            for h in range(2):
                for t1 in range(0, NT, 4):
                    b = work.next()
                    PE.wait(*after, *b.busy)
                    for t in range(4):
                        mm = nc.tensor.transpose(b.ap[0:QK, t * P:(t + 1) * P], src[:, t1 + t, h, :], K.ident[:, :])
                    mm = PE.mark(mm)
                    V.wait(mm, *s.busy)
                    y = V.mark(nc.vector.tensor_copy(dst[0:QK, h, t1 * P:(t1 + 4) * P], b.ap[0:QK, :]))
                    b.busy = [y]
                    done.append(y)
                    yield
            tok_busy[name] = [mm]
        s.ready = done

    units = [(pair, h, qb) for pair in range(HEADS // 2) for h in range(2) for qb in QB_ORDER]
    live = {}

    def score(u):
        pair, h, qb = units[u]
        s = sets[pair % 2]
        n = (qb + 1) * P
        sc = short if n <= HALF else long
        PE.wait(*s.ready, *sc.busy)
        for k0 in range(0, n, HALF):
            w = min(HALF, n - k0)
            mm = nc.tensor.matmul(sc.ap[:, k0:k0 + w], s.qT[0:QK, h, qb * P:(qb + 1) * P], s.kT[0:QK, h, k0:k0 + w],
                                  start=True, stop=True)
        mm = PE.mark(mm)
        V.wait(mm)
        V.wait(V.mark(nc.vector.tensor_tensor(sc.ap[:, qb * P:n], sc.ap[:, qb * P:n], causal[:, :], ALU.add)))
        V.wait(V.mark(nc.vector.reduce_max(st[:, 0, u:u + 1], sc.ap[:, 0:n], AX.X)))
        t = V.mark(nc.vector.tensor_scalar(st[:, 1, u:u + 1], st[:, 0, u:u + 1], -scale, None, ALU.mult))
        live[u] = [sc, t, n]

    def exponent(u):
        sc, t, n = live[u]
        p = Pm.next()
        A.wait(t, *p.busy)
        t = A.mark(nc.scalar.activation(p.ap[:, 0:n], sc.ap[:, 0:n], ACT.Exp, bias=st[:, 1, u:u + 1], scale=scale,
                                        accum_out=st[:, 2, u:u + 1]))
        sc.busy = [t]
        live[u] = [p, t]

    def turn(u):
        pair, h, qb = units[u]
        p, t = live[u][:2]
        x = PT.next()
        evs = []
        for j0 in range(0, qb + 1, 4):
            nj = min(4, qb + 1 - j0)
            b = work.next()
            PE.wait(t, *b.busy)
            for j in range(nj):
                mm = nc.tensor.transpose(b.ap[:, j * P:(j + 1) * P], p.ap[:, (j0 + j) * P:(j0 + j + 1) * P], K.ident[:, :])
            mm = PE.mark(mm)
            e, op = (V, nc.vector.tensor_copy) if j0 else (A, nc.scalar.copy)
            e.wait(mm, *x.busy)
            ev = e.mark(op(x.ap[:, j0:j0 + nj, :], b.ap[:, 0:nj * P].rearrange("p (j c) -> p j c", j=nj)))
            b.busy = [ev]
            evs.append(ev)
        p.busy = [mm]
        V.wait(t)
        r = V.mark(nc.vector.reciprocal(st[:, 3, u:u + 1], st[:, 2, u:u + 1]))
        live[u] = [r, x, evs]

    def output(u):
        pair, h, qb = units[u]
        s = sets[pair % 2]
        r, x, evs = live.pop(u)
        b = bank[7]
        mm = K.product(b.ap[:, 0:VDIM], [(x.ap[:, j, :], s.v[:, j, h, :], evs) for j in range(qb + 1)], b)
        x.busy = [mm]
        V.wait(mm, r, *tok_busy["o"])
        t = V.mark(nc.vector.tensor_scalar(otok[:, qb, h * VDIM:(h + 1) * VDIM], b.ap[:, 0:VDIM], st[:, 3, u:u + 1], None, ALU.mult))
        b.busy = [t]
        s.busy = [mm]
        if u % (2 * NT) == 2 * NT - 1:
            for t0 in range(0, NT, 4):
                b = work.next()
                PE.wait(t, *b.busy)
                for i in range(4):
                    m2 = nc.tensor.transpose(b.ap[:, i * P:(i + 1) * P], otok[:, t0 + i, :], K.ident[:, :])
                m2 = PE.mark(m2)
                hi, lo = (o[:, pair, t0 * P:(t0 + 4) * P] for o in oT)
                A.wait(m2)
                th = A.mark(nc.scalar.activation(hi, b.ap, ACT.Copy))
                V.wait(th)
                tl = V.mark(nc.vector.tensor_tensor(lo, b.ap, hi.bitcast(F32), ALU.subtract))
                b.busy = [tl]
            tok_busy["o"] = [m2]

    work, work_later = Ring(bank), work
    for _ in project(0):
        pass
    work = work_later
    long.busy = [*bank[0].busy, *bank[1].busy]
    feed = iter(())
    for i in range(len(units) + TURN_LAG + OUT_LAG):
        if i < len(units):
            pair = units[i][0]
            if i % (2 * NT) == 0:
                for _ in feed:
                    pass
                feed = project(pair + 1) if pair + 1 < HEADS // 2 else iter(())
                fed = -3
            score(i)
        fed += 1
        more = lambda: next(feed, None) if fed > 0 else None
        more()
        if 0 <= i - TURN_LAG < len(units):
            turn(i - TURN_LAG)
        more()
        if i - TURN_LAG - OUT_LAG >= 0:
            output(i - TURN_LAG - OUT_LAG)
        more()
        if i < len(units):
            exponent(i)
    bank[0].busy = bank[1].busy = long.busy
    K.handover()
    ctx.close()


def load_split_steps(K, name, dram, n, cols, pair, before, slots, out):
    for k in range(n):
        s = slots.next()
        t = K.load(s, s.ap, dram[k, :, cols], after=K.stored[name])
        hi, lo = (x[:, k, :] for x in pair)
        s.busy = K.split(s.ap, hi, lo, [t], before, (K.G, K.V)[k % 2])
        out.append(s.busy)
        yield


def residual_source(K, ctx, dram, name=None):
    slots = Ring([Slot(K.sb(ctx, f"res{i}", [P, HALF])[:, :], K.semaphore(f"res{K.names}")) for i in range(2)])
    rows = dram.rearrange("(t p) d -> t p d", p=P)

    def source(t, n):
        s = slots.next()
        return s, K.load(s, s.ap, rows[t][:, n * HALF:(n + 1) * HALF], after=K.stored.get(name, []))
    return source


GATE_SLOTS = 4


def merge_stage(K, branches, gates, gate_name, w_out, res_dram, res_name, x, parts, norm, make_hT):
    nc, io, A, V, G, PE = K.nc, K.io, K.A, K.V, K.G, K.PE
    span = S // parts
    halves = span // HALF
    branch_memory = ExitStack()
    K.low_engines = [G, V]
    with ExitStack() as ctx:
        res = residual_source(K, ctx, res_dram, res_name)
        gs = Ring([Slot(K.sb(ctx, f"g{i}", [P, HALF])[:, :], K.semaphore(f"{gate_name}_load{i}")) for i in range(GATE_SLOTS)])
        merged = K.pair(ctx, "merged", [P, ND, span])
        merged_busy = []
        ops = [src if not isinstance(src[0], str) else K.pair(branch_memory, f"br{bi}", [P, n, span])
               for bi, (w, n, src) in enumerate(branches)]

        def branch_loads(part, before):
            ready = [[] for _ in branches]

            def steps():
                for tokens, op, (w, n, src) in zip(ready, ops, branches):
                    if isinstance(src[0], str):
                        yield from load_split_steps(K, src[0], src[1], n, slice(part * span, (part + 1) * span), op, before,
                                                    gs, tokens)
                    else:
                        tokens.extend([done_before] * n)
            return ready, steps()
        done_before = [A.last(), V.last(), G.last()]
        waits, loads = branch_loads(0, [PE.last()])
        for _ in loads:
            pass
        for part in range(parts):
            merged_ready = [[] for _ in range(ND)]
            gate_order = [(j, h, bi) for j in range(ND) for h in range(halves) for bi in range(2)]
            gate_tiles = {}

            def fetch_gates(n):
                while gate_order and len(gate_tiles) < n:
                    j, h, bi = key = gate_order.pop(0)
                    g = gs.next()
                    gh = slice(part * span + h * HALF, part * span + (h + 1) * HALF)
                    gate_tiles[key] = (g, K.load(g, g.ap, gates[bi * ND + j, :, gh], after=K.stored[gate_name]))
            fetch_gates(GATE_SLOTS)
            for j in range(ND):
                taken = [[K.take() for _ in range(2 if n > 8 else 1)] for _, n, _ in branches]
                for h in range(halves):
                    hs = slice(h * HALF, (h + 1) * HALF)
                    gh = slice(part * span + h * HALF, part * span + (h + 1) * HALF)
                    prods = []
                    for bi, (op, tl) in enumerate(zip(ops, taken)):
                        g, gt = gate_tiles.pop((j, h, bi))
                        ks = [(hi[:, i, :], lo[:, i, :], d) for _, hi, lo, d in tl for i in range(hi.shape[1])]
                        terms = []
                        for k, (hi, lo, d) in enumerate(ks):
                            oc = hs if isinstance(branches[bi][2][0], str) else gh
                            terms += K.three((hi, lo), (op[0][:, k, oc], op[1][:, k, oc]), [*d, *waits[bi][k]])
                        b = K.bank()
                        mm = K.product(b.ap, terms, b)
                        prods.append((b, mm, g, gt))
                    (b0, mm0, g0, gt0), (b1, mm1, g1, gt1) = prods
                    V.wait(mm0, gt0)
                    ta = V.mark(nc.vector.tensor_tensor(g0.ap, b0.ap, g0.ap, ALU.mult))
                    V.wait(mm1, gt1)
                    tb = V.mark(nc.vector.tensor_tensor(g1.ap, b1.ap, g1.ap, ALU.mult))
                    b0.busy, b1.busy = [ta], [tb]
                    V.wait(ta, tb)
                    tm = V.mark(nc.vector.tensor_tensor(g1.ap, g1.ap, g0.ap, ALU.add))
                    done = K.split(g1.ap, merged[0][:, j, hs], merged[1][:, j, hs], [tm], merged_busy)
                    g0.busy, g1.busy = [tm], done
                    fetch_gates(GATE_SLOTS)
                    merged_ready[j] += done
                K.release([s[0] for tl in taken for s in tl], mm)
            if part == parts - 1:
                K.handover()
                branch_memory.close()
                norm.hT = make_hT()
            else:
                waits, loads = branch_loads(part + 1, [PE.last()])
            for n in range(2):
                pre = {}

                def evacuate(t, bank, mm, n=n):
                    tt = part * (span // P) + t
                    s, rt = pre.pop(t)
                    V.wait(mm, rt)
                    v = V.mark(nc.vector.tensor_tensor(x[:, tt, n * HALF:(n + 1) * HALF], bank, s.ap, ALU.add))
                    sq = K.square(x, tt, n, [v], bank)
                    s.busy = [v]
                    if t + 2 < span // P:
                        pre[t + 2] = res(tt + 2, n)
                    if part < parts - 1:
                        for _ in range(3):
                            next(loads, None)
                    elif 0 < n * (span // P) + t <= NORM_STEPS:
                        norm.advance(1)
                    return [sq]
                for t in range(2):
                    pre[t] = res(part * (span // P) + t, n)
                K.token_major(merged, [], 0, ND, HALF, 4, range(span // P), evacuate, merged_ready)
            for _ in loads:
                pass
            merged_busy = [PE.last()]
        K.low_engines = [G]
        K.handover()


RWKV_GATES = (4, 3, 4, 5)
GATES_LAST = 4
GATES_AHEAD = 4
POOL_GATES = (0, 0, 1, 1)
GRP = 2


FFN_AHEAD, FFN2_AHEAD = 3, 1


def ffn_plan(blocks):
    plan, nxt = [], 0
    for g in range(blocks // GRP):
        ahead = 2 if g == blocks // GRP - 2 else 1
        while nxt < min(blocks, GRP * (g + 1) + ahead):
            plan.append(("up", nxt))
            nxt += 1
        plan.append(("down", g))
    return plan


def weight_order(io):
    w1, w2 = io["w_in"][0], io["w_in_2"][0]
    rcol = MLA_COLS
    out = [weight_block(w1, rcol + c * P) for c in (NZ - 2, NZ - 1)]
    for b in range(NR):
        out += [weight_block(w1, rcol + c * P) for c in (b, NR + b, 2 * NR + b)]
        out += [weight_block(w1, rcol + RWKV_COLS + c * P) for c in range(sum(RWKV_GATES[:b]), sum(RWKV_GATES[:b + 1]))]
    out += [weight_block(w1, 0, QRANK, k, k + 2) for k in range(0, ND, 2)]
    out += [weight_block(w1, QRANK, KVRANK + ROPE, k, min(k + 3, ND)) for k in range(0, ND, 3)]

    def rows512(w, k0=0, k1=ND):
        return [weight_block(w, n * HALF, HALF, k, k + 2) for n in range(2) for k in range(k0, k1, 2)]

    def merge(branches, w_out):
        t = []
        for _ in range(2):
            for j in range(ND):
                for w, n in branches:
                    cuts = (0, n) if n <= ND else (0, n // 2, n)
                    t += [weight_block(w, j * P, P, a, b) for a, b in zip(cuts, cuts[1:])]
            t += rows512(w_out)
        return t

    def ffn(blocks, up, down):
        t = []
        for kind, i in ffn_plan(blocks):
            t += up(i) if kind == "up" else rows512(down, GRP * i, GRP * (i + 1))
        return t
    out += merge([(io["w_o_mla"][0], NR), (io["w_o_rwkv"][0], NR)], io["w_out"][0])
    out += ffn(DFF // P, lambda i: [weight_block(io["w_ffn_up"][0], i * P)], io["w_ffn_down"][0])
    out += rows512(io["w_ple_gate"][0]) * NHALF
    gate2 = [weight_block(w2, LW + PW + c * P) for c in range(2 * ND)]
    out += [gate2.pop(0) for _ in range(GATES_AHEAD)]
    for c in range(NL):
        out += [weight_block(w2, c * P), gate2.pop(0)]
    for g in range(len(WINDOWS)):
        out += [weight_block(w2, LW + c * P) for c in (2 * g, 2 * g + 1)] + [gate2.pop(0) for _ in range(POOL_GATES[g])]
    out += merge([(io["p_a_2"][0], NL), (io["p_b_2"][0], PW // P)], io["w_out_2"][0])
    out += ffn(NF2, lambda i: [weight_block(io["w_up_2"][0], i * P), weight_block(io["w_up_2"][0], (NF2 + i) * P)],
               io["w_down_2"][0])
    return out


def ffn_stage(K, x, hT, norm, blocks, make, ahead, on_last_group, on_block_done):
    nc, A, V, G, PE = K.nc, K.A, K.V, K.G, K.PE
    with ExitStack() as ctx:
        act = K.pair(ctx, "act", [P, 4, S])
        busy = [[] for _ in range(4)]
        done, x_done = {}, {}
        slot = lambda i: (act[0][:, i % 4, :], act[1][:, i % 4, :])
        first = []
        for i in range(ahead):
            blocks_i, done[i] = make(i, slot(i), busy[i])
            first += blocks_i
        K.staggered(first, norm)

        def evacuate(t, n, bank, mm, last=False):
            dst = x[:, t, n * HALF:(n + 1) * HALF]
            V.wait(mm, x_done.get((t, n)))
            v = V.mark(nc.vector.tensor_tensor(dst, dst, bank, ALU.add))
            x_done[(t, n)] = v
            return [K.square(x, t, n, [v], bank)] if last else [v]

        for kind, i in ffn_plan(blocks):
            if kind == "up":
                if i >= ahead:
                    steps, done[i] = make(i, slot(i), busy[i % 4])
                    for b in steps:
                        for _ in b:
                            pass
                continue
            k0 = (GRP * i) % 4
            after = done[GRP * i] + done[GRP * i + 1]
            if i < blocks // GRP - 1:
                for n in range(2):
                    K.token_major(act, after, k0, GRP, HALF, 1, range(NT), lambda t, bank, mm, n=n: evacuate(t, n, bank, mm))
                busy[k0] = busy[k0 + 1] = [PE.last()]
                continue
            on_last_group(PE.last())
            taken = [K.take() for _ in range(2)]
            for t in range(NT):
                tc = slice(t * P, (t + 1) * P)
                for n, (w_slot, hi, lo, w_done) in enumerate(taken):
                    b = K.bank()
                    terms = []
                    for k in range(GRP):
                        terms += K.three((act[0][:, k0 + k, tc], act[1][:, k0 + k, tc]), (hi[:, k, :], lo[:, k, :]),
                                         [*w_done, *after])
                    mm = K.product(b.ap, terms, b)
                    if t == NT - 1:
                        K.release([w_slot], mm)
                    b.busy = evacuate(t, n, b.ap, mm, True)
                on_block_done(t)
        K.handover()


def lru_stage(K, hT, ready, ya_dram, yb_dram, gates):
    nc, io, A, V, G, PE = K.nc, K.io, K.A, K.V, K.G, K.PE
    w = io["w_in_2"][0]
    with ExitStack() as ctx:
        nl2 = 2 * NL
        sp = K.sb(ctx, "sp", [P, 6, nl2])
        y, e, z, z2, acc, c_rate = (sp[:, i, :] for i in range(6))
        for i, n in enumerate(("lam_f_2", "lam_b_2")):
            V.mark(nc.vector.tensor_scalar(y[:, i * NL:(i + 1) * NL], K.param[:, K.col[n]:K.col[n] + NL], -1.0, None, ALU.mult))
        V.wait(V.last())
        V.wait(V.mark(nc.vector.tensor_scalar(e, y, -1.0, None, ALU.mult)))
        t = V.mark(nc.vector.tensor_tensor(e, e, y, ALU.min))
        A.wait(t)
        t = A.mark(nc.scalar.activation(e, e, ACT.Exp))
        V.wait(t)
        V.wait(V.mark(nc.vector.tensor_scalar(z, e, 2.0, None, ALU.add)))
        V.wait(V.mark(nc.vector.reciprocal(z, z)))
        V.wait(V.mark(nc.vector.tensor_tensor(z, z, e, ALU.mult)))
        V.wait(V.mark(nc.vector.tensor_tensor(z2, z, z, ALU.mult)))
        terms = 9
        V.wait(V.mark(nc.vector.memset(acc, 1.0 / (2 * terms - 1))))
        for n in range(terms - 2, -1, -1):
            V.wait(V.mark(nc.vector.tensor_tensor(acc, acc, z2, ALU.mult)))
            V.wait(V.mark(nc.vector.tensor_scalar(acc, acc, 1.0 / (2 * n + 1), None, ALU.add)))
        V.wait(V.mark(nc.vector.tensor_tensor(acc, acc, z, ALU.mult)))
        V.wait(V.mark(nc.vector.tensor_scalar(acc, acc, 2.0, None, ALU.mult)))
        V.wait(V.mark(nc.vector.scalar_tensor_tensor(acc, y, 0.0, acc, ALU.max, ALU.add)))
        neg = K.sb(ctx, "neg", [P, nl2])
        V.mark(nc.vector.tensor_scalar(c_rate, acc, -8.0, None, ALU.mult))
        t = V.mark(nc.vector.tensor_scalar(neg[:, :], acc, 8.0, None, ALU.mult))
        A.wait(t)

        gates.open(ctx)
        raw = K.sb(ctx, "raw", [P, 16 + S + 16])
        wts = Ring([Slot(K.sb(ctx, f"wbd{i}", [P, 4, P])[:, :, :], K.semaphore(f"wbd_load{i}")) for i in range(2)])
        xcs = Ring([Slot(K.sb(ctx, f"xc{i}", [P, S])) for i in range(2)])
        gt = [Slot(K.sb(ctx, f"gt{i}", [P, S])) for i in range(4)]
        dc = [Slot(K.sb(ctx, f"dc{i}", [P, S])) for i in range(2)]
        th = [Slot(K.sb(ctx, f"th{i}", [P, S])) for i in range(2)]
        hs = [Slot(K.sb(ctx, f"hs{i}", [P, S])) for i in range(2)]
        y_sem = Slot(None, K.semaphore("ya_store"))
        raw_busy = []
        V.mark(nc.vector.memset(raw[:, 0:16], 0.0))
        tz = V.mark(nc.vector.memset(raw[:, 16 + S:], 0.0))
        V.wait(tz)
        A.wait(tz)

        def front(j):
            nonlocal raw_busy
            w_slot, xs = wts.next(), xcs.next()
            for i, n in enumerate(("wa_f_2", "wx_f_2", "wa_b_2", "wx_b_2")):
                wl = K.load(w_slot, w_slot.ap[:, i, :], io[n][0, j])
            copies = []

            def evacuate(h, bank, mm):
                A.wait(mm, *raw_busy)
                t = A.mark(nc.scalar.activation(raw[:, 16 + h * HALF:16 + (h + 1) * HALF], bank, ACT.Copy))
                copies.append(t)
                return [t]
            K.channel_major(hT, ready, evacuate)
            xc = xs.ap
            tap = lambda k: raw[:, 16 + k - 2:16 + k - 2 + S]
            cw = lambda k: K.p_("conv_a_w_2", k * NL + j)
            A.wait(*copies, *xs.busy)
            t = A.mark(nc.scalar.activation(xc[:, :], tap(0), ACT.Identity, scale=cw(0), bias=K.p_("conv_a_b_2", j)))
            V.wait(t, *copies)
            for k in range(1, 4):
                t = V.mark(nc.vector.scalar_tensor_tensor(xc[:, :], tap(k), cw(k), xc[:, :], ALU.mult, ALU.add))
                V.wait(t)
            raw_busy = [t]
            return w_slot, wl, xs, t

        head = front(0)
        for j in range(NL):
            w_slot, wl, xs, tx = head
            xc = xs.ap
            marks = []
            for i, bn in enumerate(("ba_f_2", "bx_f_2", "ba_b_2", "bx_b_2")):
                for h in range(NHALF):
                    cs = slice(h * HALF, (h + 1) * HALF)
                    b = K.bank()
                    mm = K.product(b.ap, [(w_slot.ap[:, i, :], xc[:, cs], [wl, tx])], b)
                    A.wait(mm, *gt[i].busy)
                    t = A.mark(nc.scalar.activation(gt[i].ap[:, cs], b.ap, ACT.Sigmoid, bias=K.p_(bn, j)))
                    b.busy = [t]
                    marks.append(t)
            w_slot.busy = [mm]
            te, tv, ti = [], [], []
            for d in range(2):
                ci = d * NL + j
                A.wait(*marks[4 * d:4 * d + 2], *dc[d].busy, *th[d].busy)
                A.mark(nc.scalar.activation(dc[d].ap[:, :], gt[2 * d].ap[:, :], ACT.Exp, scale=c_rate[:, ci:ci + 1]))
                te.append(A.mark(nc.scalar.activation(th[d].ap[:, :], gt[2 * d].ap[:, :], ACT.Tanh, scale=neg[:, ci:ci + 1])))
            for d in range(2):
                r, i_, th_, dc_ = gt[2 * d].ap, gt[2 * d + 1].ap, th[d].ap, dc[d].ap
                G.wait(te[d])
                ta = G.mark(nc.gpsimd.tensor_tensor(r[:, :], dc_[:, :], dc_[:, :], ALU.mult))
                ti.append(G.mark(nc.gpsimd.tensor_tensor(i_[:, :], i_[:, :], xc[:, :], ALU.mult)))
                V.wait(te[d], ta)
                t = V.mark(nc.vector.scalar_tensor_tensor(th_[:, :], r[:, :], 1.0, th_[:, :], ALU.add, ALU.mult))
                gt[2 * d].busy = [t]
                V.wait(t)
                tv.append(V.mark(nc.vector.tensor_scalar(th_[:, :], th_[:, :], 1e-34, None, ALU.max)))
            xs.busy = [mm, ti[1]]
            gates.fill(1)
            for d in range(2):
                th_, dc_, h_ = th[d].ap, dc[d].ap, hs[d].ap
                A.wait(tv[d])
                t = A.mark(nc.scalar.activation(th_[:, :], th_[:, :], ACT.Sqrt))
                V.wait(t, ti[d])
                t = V.mark(nc.vector.tensor_tensor(th_[:, :], th_[:, :], gt[2 * d + 1].ap[:, :], ALU.mult))
                gt[2 * d + 1].busy = [t]
                V.wait(t, *hs[d].busy)
                if d == 0:
                    t = V.mark(nc.vector.tensor_tensor_scan(h_[:, :], dc_[:, :], th_[:, :], 0.0, ALU.mult, ALU.add))
                else:
                    t = V.mark(nc.vector.tensor_tensor_scan(h_[:, ::-1], dc_[:, ::-1], th_[:, ::-1], 0.0, ALU.mult, ALU.add))
                dc[d].busy = th[d].busy = [t]
            G.wait(t)
            tg = G.mark(nc.gpsimd.tensor_tensor(hs[0].ap[:, :], hs[0].ap[:, :], hs[1].ap[:, :], ALU.add))
            ts = K.store("ya", y_sem, ya_dram[j], hs[0].ap[:, :], G, [tg])
            hs[0].busy, hs[1].busy = [ts], [tg]
            if j + 1 < NL:
                head = front(j + 1)
            gates.fill(1)
        for e in (A, V, G, K.SP):
            e.wait(*hs[0].busy, *dc[1].busy, *gt[3].busy)
        gt, dc, th = ([s.ap for s in x] for x in (gt, dc, th))
        wp = Slot(K.sb(ctx, "wpool", [P, 2, GDIM])[:, :, :], K.semaphore("wpool_load"))
        rc = Slot(gt[0][:, :], K.semaphore("count_load"))
        sums = [K.sb(ctx, f"sums{i}", [P, 16 + S + 16]) for i in range(2)]
        raw2 = K.sb(ctx, "raw2", [P, 16 + S + 16])
        pooled = [dc[0], dc[1]]
        yb = Ring([Slot(th[0][:, :], K.semaphore("yb_store0")), Slot(th[1][:, :], K.semaphore("yb_store1"))])
        pooled_busy = []
        V.mark(nc.vector.memset(raw2[:, 0:16], 0.0))
        V.wait(V.mark(nc.vector.memset(raw2[:, 16 + S:], 0.0)))
        L = 16 + S + 16
        raws = Ring([Slot(raw), Slot(raw2)])
        for g, win in enumerate(WINDOWS):
            rl = K.load(rc, rc.ap, io["counts"][g].partition_broadcast(P))
            pl = K.load(wp, wp.ap, io["w_pool_2"][0, g].rearrange("(k p) n -> p k n", p=P))
            made = []
            for i in range(2):
                rs = raws.next()
                u = rs.ap
                copies = []

                def evacuate(h, bank, mm):
                    A.wait(mm, *rs.busy)
                    t = A.mark(nc.scalar.activation(u[:, 16 + h * HALF:16 + (h + 1) * HALF], bank, ACT.Copy))
                    copies.append(t)
                    return [t]
                K.channel_major(hT, ready, evacuate)
                V.wait(*copies)
                src, m, at = u, 1, 0
                while m < win:
                    dst = sums[at]
                    V.wait(V.mark(nc.vector.tensor_tensor(dst[:, 2 * m - 1:L], src[:, 2 * m - 1:L], src[:, m - 1:L - m], ALU.add)))
                    src, m, at = dst, 2 * m, 1 - at
                o = 16 + win // 2 - 1
                V.wait(rl, *pooled_busy)
                V.wait(V.mark(nc.vector.tensor_tensor(pooled[i][:, :], src[:, o:o + S], rc.ap, ALU.mult)))
                t = V.mark(nc.vector.tensor_tensor(pooled[i][:, :], pooled[i][:, :], u[:, 16:16 + S], ALU.subtract))
                rs.busy = [t]
                made.append(t)
            rc.busy = [t]
            gates.fill(2 * POOL_GATES[g])
            for jo in range(2):
                blk = 2 * g + jo
                out = yb.next()
                for h in range(NHALF):
                    cs = slice(h * HALF, (h + 1) * HALF)
                    b = K.bank()
                    mm = K.product(b.ap, [(wp.ap[:, k, jo * P:(jo + 1) * P], pooled[k][:, cs], [pl, *made]) for k in range(2)], b)
                    V.wait(mm, *out.busy)
                    t = V.mark(nc.vector.tensor_scalar(out.ap[:, cs], b.ap, K.p_("b_pool_2", blk), K.p_("pool_scale_2", blk), ALU.add, ALU.mult))
                    b.busy = [t]
                out.busy = [K.store("yb", out, yb_dram[blk], out.ap, A, [t])]
            wp.busy = [mm]
            pooled_busy = [mm]
        for e in (K.A, K.V, K.G, K.SP):
            for s in yb.slots:
                e.wait(*s.busy)
        gates.close()
        K.handover()


class NormRows:

    def __init__(self, K, memory, x, gain, dram, name, again):
        self.K, self.x, self.name, self.again = K, x, name, again
        self.gain = memory.gain
        self.gain_loaded = K.load(self.gain, self.gain.ap, gain.partition_broadcast(P), queue=K.G)
        self.rows = dram.rearrange("(t p) d -> t p d", p=P)
        self.store_sem = Slot(None, K.semaphore(f"{name}_store"))

    def make(self, ts):
        K, x = self.K, self.x
        K.V.wait(K.rstd_of(ts), self.gain_loaded)
        for t in ts:
            ty = K.V.mark(K.nc.vector.scalar_tensor_tensor(x[:, t, :], x[:, t, :], K.squares[:, 3, t:t + 1],
                                                           self.gain.ap, ALU.mult, ALU.mult))
            self.gain.busy = [ty]
            if self.again:
                b = K.bank()
                for n in range(2):
                    b.busy = [K.square(x, t, n, [ty, *b.busy], b.ap)]
            K.store(self.name, self.store_sem, self.rows[t], x[:, t, :], K.SP, [ty])


def program(nc, io, out):
    K = Kernel(nc, io)
    A, V, G, PE, SP = K.A, K.V, K.G, K.PE, K.SP
    K.setup()
    scratch = {}
    for name, shape in (("gates1", [2 * ND, P, S]), ("gates2", [2 * ND, P, S]), ("yT", [NR, P, S]),
                        ("ya", [NL, P, S]), ("yb", [PW // P, P, S]), ("x2", [S, D])):
        scratch[name] = nc.dram_tensor("scratch_" + name, shape, F32, kind="Internal").ap()

    right = ExitStack()
    hT = K.pair(right, "hT", [P, ND, S], side="right")
    with ExitStack() as ctx:
        memory = Norm.Memory(K, ctx)
        x = K.sb(ctx, "x_in", [P, NT, D])
        rows_in = io["x"][0].rearrange("(t p) d -> t p d", p=P)
        arrived = []
        for t in range(NT):
            xl = Slot(None, K.semaphore(f"x_in_load{t}"))
            arrived.append(K.load(xl, x[:, t, :], rows_in[t], queue=(A, SP)[t % 2]))
            if t == 1:
                norm = Norm(K, memory, x, hT, io["g_mix"][0], [[], []])
        for t in range(NT):
            for n in range(2):
                b = K.bank()
                b.busy = [K.square(x, t, n, [arrived[t], *b.busy], b.ap)]
            if t >= NT // NHALF - 1:
                norm.advance(1)
        params = K.load_parameters(ctx)
        norm.advance(3)
        K.queue_weights(weight_order(io))
        norm.finish()
        ready = norm.ready
        K.transpose_parameters(params)
        K.handover()
    rwkv_stage(K, hT, ready, scratch["yT"], Gates(K, hT, ready, None, scratch["gates1"], "gates1"))
    with ExitStack() as ctx:
        cT = K.sb(ctx, "cT", [P, NQ + NKV, S])
        kpe = K.sb(ctx, "kpe", [P, NT, ROPE])
        weights = HeadWeights(K, ctx)
        weights.load(0)
        cs = K.sb(ctx, "cs", [P, 2, NT, ROPE // 2])
        causal = K.sb(ctx, "causal", [P, P])
        c_ready = compressed_stage(K, hT, ready, cT, kpe, lambda: angles(K, cs, causal))
        right.close()
        right = ExitStack()
        oT = K.pair(right, "oT", [P, NR, S], side="right")
        attention_stage(K, cT, c_ready, kpe, cs, causal, weights, oT)
    left = ExitStack()
    x = K.sb(left, "x", [P, NT, D])
    memory = Norm.Memory(K, left, 0)
    norm = Norm(K, memory, x, None, io["g_ffn"][0], [[], []])

    def hT_where_branches_were():
        right.close()
        right_next = ExitStack()
        memory.add_blocks(K, right_next, 2, "right")
        hTs.append((right_next, K.pair(right_next, "hT", [P, ND, S], side="right")))
        return hTs[-1][1]
    hTs = []
    merge_stage(K, [(io["w_o_mla"][0], NR, oT), (io["w_o_rwkv"][0], NR, ("yT", scratch["yT"]))],
                scratch["gates1"], "gates1", io["w_out"][0], io["x"][0], None, x, 2, norm, hT_where_branches_were)
    right, hT = hTs.pop()

    with ExitStack() as ctx:
        rel = Ring([Slot(K.sb(ctx, f"rel{i}", [P, HALF])[:, :]) for i in range(3)])
        ready = norm.ready

        def squared_relu(j, dst, before):
            done = []

            def evacuate(h, bank, mm):
                cs = slice(h * HALF, (h + 1) * HALF)
                r = rel.next()
                A.wait(mm, *r.busy)
                t = A.mark(nc.scalar.activation(r.ap, bank, ACT.Relu))
                V.wait(t)
                tq = V.mark(nc.vector.tensor_tensor(r.ap, r.ap, bank, ALU.mult))
                d = K.split(r.ap, dst[0][:, cs], dst[1][:, cs], [tq], before)
                r.busy = d
                done.extend(d)
                return [tq]
            return [K.channel_major_steps(hT, ready, evacuate)], done

        def start_norm(last_read):
            nonlocal norm
            norm = Norm(K, memory, x, hT, io["g_ple"][0], [[last_read], [last_read]])

        def block_done(t):
            if t >= NT // NHALF - 1:
                norm.advance(1)
        ffn_stage(K, x, hT, norm, DFF // P, squared_relu, FFN_AHEAD, start_norm, block_done)

    with ExitStack() as ctx:
        pT = K.sb(ctx, "pT", [P, 2, S])
        prow = Slot(K.sb(ctx, "prow", [P, NT, PLE])[:, :, :], K.semaphore("prow_load"))
        wpp = Slot(K.sb(ctx, "wpp", [P, 2, D])[:, :, :], K.semaphore("wpp_load"))
        tp = K.load(prow, prow.ap, io["p"][0, 0].rearrange("(t p) c -> p t c", p=P))
        tw = K.load(wpp, wpp.ap, io["w_ple_proj"][0].rearrange("(k p) n -> p k n", p=P))
        final = NormRows(K, Norm.Memory(K, ctx, 0), x, io["g_final"], scratch["x2"], "x2", True)
        pT_ready = []

        def make_pT():
            for c in range(2):
                for t0 in range(0, NT, 4):
                    b = K.bank()
                    PE.wait(tp, *b.busy)
                    for t in range(4):
                        mm = nc.tensor.transpose(b.ap[:, t * P:(t + 1) * P], prow.ap[:, t0 + t, c * P:(c + 1) * P], K.ident[:, :])
                    mm = PE.mark(mm)
                    V.wait(mm)
                    b.busy = [V.mark(nc.vector.tensor_copy(pT[:, c, t0 * P:(t0 + 4) * P], b.ap))]
            pT_ready.extend(b.busy)
        sg = Ring([Slot(K.sb(ctx, f"sg{i}", [P, HALF])[:, :]) for i in range(3)])
        ready = norm.ready
        mix_norm = None
        K.low_engines = [G, V]
        for half in range(NHALF):
            for n in range(2):
                def evacuate(t, bank, mm, n=n):
                    if not pT_ready:
                        make_pT()
                    b = K.bank()
                    m2 = K.product(b.ap, [(pT[:, k, t * P:(t + 1) * P], wpp.ap[:, k, n * HALF:(n + 1) * HALF], [*pT_ready, tw])
                                          for k in range(2)], b)
                    s = sg.next()
                    A.wait(mm, *s.busy)
                    ta = A.mark(nc.scalar.activation(s.ap, bank, ACT.Sigmoid))
                    V.wait(ta, m2)
                    tb = V.mark(nc.vector.tensor_tensor(s.ap, s.ap, b.ap, ALU.mult))
                    b.busy = [tb]
                    dst = x[:, t, n * HALF:(n + 1) * HALF]
                    V.wait(tb)
                    tx = V.mark(nc.vector.tensor_tensor(dst, dst, s.ap, ALU.add))
                    s.busy = [tx]
                    square = K.square(x, t, n, [tx], bank)
                    if mix_norm is None:
                        norm.advance(1)
                    elif 2 <= n * (NT // 2) + t - NT // 2 < 2 + NORM_STEPS:
                        mix_norm.advance(1)
                    if n and t % (NT // 2) == 2:
                        final.make([t - 2, t - 1])
                    return [square]
                K.token_major(hT, ready, 0, ND, HALF, 4, range(half * NT // 2, (half + 1) * NT // 2), evacuate)
            if half == 0:
                half_read = PE.last()
                final.make([NT // 2 - 2, NT // 2 - 1])
                mix_norm = Norm(K, memory, x, hT, io["g_mix_2"][0], [[half_read], []])
        K.low_engines = [G]
        mix_norm.before[1] = [PE.last()]
        final.make([NT - 2, NT - 1])
        K.handover()

    norm, ready = mix_norm, mix_norm.ready
    gates2 = Gates(K, hT, ready, lambda c: K.p_("b_gate_2", c), scratch["gates2"], "gates2")
    with ExitStack() as ctx:
        gates2.open(ctx)
        K.staggered([gates2.blocks.pop(0) for _ in range(GATES_AHEAD)], norm, 3)
        gates2.close()
        K.handover()
    left.close()
    for e in (A, V, G, K.SP):
        e.wait(*K.stored["x2"][-1:])
    lru_stage(K, hT, ready, scratch["ya"], scratch["yb"], gates2)
    right.close()
    x = K.sb(left, "x", [P, NT, D])
    memory = Norm.Memory(K, left, 0)
    norm = Norm(K, memory, x, None, io["g_ffn_2"][0], [[], []])
    right = ExitStack()
    merge_stage(K, [(io["p_a_2"][0], NL, ("ya", scratch["ya"])), (io["p_b_2"][0], PW // P, ("yb", scratch["yb"]))],
                scratch["gates2"], "gates2", io["w_out_2"][0], scratch["x2"], "x2", x, 2, norm, hT_where_branches_were)
    right, hT = hTs.pop()

    with ExitStack() as ctx:
        ready = norm.ready
        raws = Ring([Slot(K.sb(ctx, f"up{i}", [P, S + 2])) for i in range(3)])
        conv = memory.xn.slots
        for s in raws.slots:
            V.mark(nc.vector.memset(s.ap[:, 0:1], 0.0))
            V.wait(V.mark(nc.vector.memset(s.ap[:, S + 1:S + 2], 0.0)))
        A.wait(V.last())

        def gelu_product(j, dst, before):
            done = []

            def one(part):
                c = part * NF2 + j
                raw, cv = raws.next(), conv[part]
                copies = []

                def evacuate(h, bank, mm):
                    A.wait(mm, *raw.busy)
                    t = A.mark(nc.scalar.activation(raw.ap[:, 1 + h * HALF:1 + (h + 1) * HALF], bank, ACT.Copy))
                    copies.append(t)
                    return [t]
                yield from K.channel_major_steps(hT, ready, evacuate)
                cw = lambda k: K.p_("conv_f_w_2", k * 2 * NF2 + c)
                A.wait(*copies, *cv.busy)
                t = A.mark(nc.scalar.activation(cv.ap, raw.ap[:, 0:S], ACT.Identity, scale=cw(0), bias=K.p_("conv_f_b_2", c)))
                V.wait(t)
                for k in (1, 2):
                    t = V.mark(nc.vector.scalar_tensor_tensor(cv.ap, raw.ap[:, k:k + S], cw(k), cv.ap, ALU.mult, ALU.add))
                    V.wait(t)
                raw.busy = [t]
                if part == 0:
                    A.wait(t)
                    gelu.append(A.mark(nc.scalar.activation(cv.ap, cv.ap, ACT.Gelu_apprx_tanh)))
                else:
                    V.wait(t, *gelu)
                    tm = V.mark(nc.vector.tensor_tensor(conv[0].ap, conv[0].ap, conv[1].ap, ALU.mult))
                    conv[1].busy = [tm]
                    done.extend(K.split(conv[0].ap, dst[0], dst[1], [tm], before))
                    conv[0].busy = list(done)
            gelu = []
            return [one(0), one(1)], done

        def block_done(t):
            if t >= 2 and t % 2 == 0:
                final.make(range(t - 2, t))
            if t == NT - 1:
                final.make(range(t - 1, t + 1))
        def start_final(_):
            nonlocal final
            final = NormRows(K, memory, x, io["g_final_2"], out[0], "out", False)
        ffn_stage(K, x, hT, norm, NF2, gelu_product, FFN2_AHEAD, start_final, block_done)
    right.close()
    left.close()
    for toks in K.stored.values():
        SP.wait(*toks)
    K.stack.close()


_INS = ["x", "p", "positions", "g_mix", "w_in", "g_q_a", "w_uq", "g_kv_a", "w_ukv", "w_o_mla", "mu_rwkv", "w0", "w2",
        "a0", "a2", "g2", "k_k", "k_a", "r_k", "ln_x_w", "ln_x_b", "w_o_rwkv", "w_out", "g_ffn", "w_ffn_up",
        "w_ffn_down", "g_ple", "w_ple_gate", "w_ple_proj", "g_final", "g_mix_2", "w_in_2", "b_gate_2", "conv_a_w_2",
        "conv_a_b_2", "wa_f_2", "ba_f_2", "wx_f_2", "bx_f_2", "lam_f_2", "wa_b_2", "ba_b_2", "wx_b_2", "bx_b_2",
        "lam_b_2", "w_pool_2", "b_pool_2", "pool_scale_2", "p_a_2", "p_b_2", "w_out_2", "g_ffn_2", "w_up_2",
        "conv_f_w_2", "conv_f_b_2", "w_down_2", "g_final_2"]


def kernel(**inputs):
    import concourse.bacc as bacc
    from concourse.bass_utils import run_bass_kernel_spmd

    nc = bacc.Bacc("TRN2", target_bir_lowering=False, num_devices=1)
    arrays = {name: np.ascontiguousarray(inputs[name]) for name in _INS}
    arrays["const"] = constants()
    arrays["counts"] = pool_counts()
    feed, io = {}, {}
    for name, a in arrays.items():
        feed[f"in_{name}"] = a
        io[name] = nc.dram_tensor(f"in_{name}", a.shape, mybir.dt.from_np(a.dtype), kind="ExternalInput").ap()
    out = nc.dram_tensor("out_x", (1, S, D), F32, kind="ExternalOutput").ap()
    program(nc, io, out)
    r = run_bass_kernel_spmd(nc, [feed], core_ids=[0])
    return r.results[0]["out_x"]
```
